# Optimizing a Trainium2 kernel written in Bass

```python
import jax, jax.numpy as jnp
from jax import lax
import numpy as np

D_MODEL = 1024
BATCH = 1
SEQ = 256
DEPTH = 2

CTX_LEN = 256
GRID_W = 64
Q_BLOCK = 128
ROPE_THETA = 10000.0
EPS = 1e-6

F_GROUPS = 4
F_GROUP_DIM = 128
F_WIDTH = F_GROUPS * F_GROUP_DIM
MLA_HEADS = 8
MLA_Q_RANK = 256
MLA_KV_RANK = 256
MLA_NOPE_DIM = 64
MLA_ROPE_DIM = 32
MLA_QK_DIM = MLA_NOPE_DIM + MLA_ROPE_DIM
MLA_V_DIM = 64
MLA_WIDTH = MLA_HEADS * MLA_V_DIM
GQA_HEADS = 8
GQA_KV_HEADS = 2
GQA_GROUP = GQA_HEADS // GQA_KV_HEADS
GQA_HEAD_DIM = 64
GQA_WIDTH = GQA_HEADS * GQA_HEAD_DIM
GQA_KV_WIDTH = GQA_KV_HEADS * GQA_HEAD_DIM

N_BRANCHES = 3
D_FF = 4 * D_MODEL
N_MOD = 6

KV_COLS = MLA_KV_RANK + MLA_ROPE_DIM + 2 * GQA_KV_WIDTH
KV_SPLITS = (MLA_KV_RANK, MLA_KV_RANK + MLA_ROPE_DIM, MLA_KV_RANK + MLA_ROPE_DIM + GQA_KV_WIDTH)
REST_SPLITS = (F_WIDTH, F_WIDTH + MLA_Q_RANK, F_WIDTH + MLA_Q_RANK + GQA_WIDTH)
IN_COLS = KV_COLS + F_WIDTH + MLA_Q_RANK + GQA_WIDTH + N_BRANCHES * D_MODEL


def layer_norm(x, g=None, b=None):
    xf = x.astype(jnp.float32)
    mu = xf.mean(-1, keepdims=True)
    var = jnp.square(xf - mu).mean(-1, keepdims=True)
    y = (xf - mu) * lax.rsqrt(var + EPS)
    if g is not None:
        y = y * g.astype(jnp.float32) + b.astype(jnp.float32)
    return y.astype(x.dtype)

def rms_norm(x, g):
    xf = x.astype(jnp.float32)
    y = xf * lax.rsqrt(jnp.square(xf).mean(-1, keepdims=True) + EPS)
    return (y * g.astype(jnp.float32)).astype(x.dtype)

def modulate(x, shift, scale):
    return layer_norm(x) * (1 + scale) + shift

def rope_angles(rows, cols, d_rot):
    n = d_rot // 4
    freqs = ROPE_THETA ** (-jnp.arange(n, dtype=jnp.float32) / n)
    ang = jnp.concatenate([rows[:, None] * freqs, cols[:, None] * freqs], axis=-1)
    return jnp.cos(ang), jnp.sin(ang)

def apply_rope(x, cos, sin):
    x1, x2 = jnp.split(x, 2, axis=-1)
    cos = cos[:, None, :].astype(x.dtype)
    sin = sin[:, None, :].astype(x.dtype)
    return jnp.concatenate([x1 * cos - x2 * sin, x1 * sin + x2 * cos], axis=-1)

def attend(q, k, v):
    B, S, Hk, G, dk = q.shape
    nb = S // Q_BLOCK
    qb = jnp.moveaxis(q.reshape(B, nb, Q_BLOCK, Hk, G, dk), 1, 0)

    def block(qi):
        s = jnp.einsum("bqkgd,btkd->bkgqt", qi, k).astype(jnp.float32)
        w = jax.nn.softmax(s, axis=-1).astype(v.dtype)
        return jnp.einsum("bkgqt,btkd->bqkgd", w, v)

    o = lax.map(block, qb)
    return jnp.moveaxis(o, 0, 1).reshape(B, S, Hk * G * v.shape[-1])

def fourier_mix(u):
    B, S, _ = u.shape
    ug = u.reshape(B, S, F_GROUPS, F_GROUP_DIM).astype(jnp.float32)
    f = jnp.fft.fft2(ug, axes=(1, 3), norm="ortho").real
    return f.reshape(B, S, F_WIDTH).astype(u.dtype)

def kv_parts(p, lw, rope):
    B, T, _ = p.shape
    c_kv, k_r, k_g, v_g = jnp.split(p[..., :KV_COLS], KV_SPLITS, axis=-1)
    c_kv = rms_norm(c_kv, lw["mla_kv_g"])
    k_nope = (c_kv @ lw["w_uk"]).reshape(B, T, MLA_HEADS, MLA_NOPE_DIM)
    v_m = (c_kv @ lw["w_uv"]).reshape(B, T, MLA_HEADS, MLA_V_DIM)
    k_r = k_r[:, :, None, :]
    k_g = rms_norm(k_g.reshape(B, T, GQA_KV_HEADS, GQA_HEAD_DIM), lw["gqa_k_g"])
    v_g = v_g.reshape(B, T, GQA_KV_HEADS, GQA_HEAD_DIM)
    if rope is not None:
        k_r = apply_rope(k_r, *rope[0])
        k_g = apply_rope(k_g, *rope[1])
    k_m = jnp.concatenate([k_nope, jnp.broadcast_to(k_r, (B, T, MLA_HEADS, MLA_ROPE_DIM))], axis=-1)
    return (k_m, v_m, k_g, v_g)

def mixer(p, kv, lw, rope):
    B, S, _ = p.shape
    k_m, v_m, k_g, v_g = kv
    f_in, c_q, q_g, gate_logits = jnp.split(p[..., KV_COLS:], REST_SPLITS, axis=-1)
    y_f = fourier_mix(f_in) @ lw["w_fo"]
    q_m = (rms_norm(c_q, lw["mla_q_g"]) @ lw["w_uq"]).reshape(B, S, MLA_HEADS, MLA_QK_DIM)
    q_nope, q_rope = jnp.split(q_m, [MLA_NOPE_DIM], axis=-1)
    q_g = rms_norm(q_g.reshape(B, S, GQA_HEADS, GQA_HEAD_DIM), lw["gqa_q_g"])
    if rope is not None:
        q_rope = apply_rope(q_rope, *rope[0])
        q_g = apply_rope(q_g, *rope[1])
    q_m = jnp.concatenate([q_nope, q_rope], axis=-1)[:, :, :, None, :] * (MLA_QK_DIM ** -0.5)
    y_m = attend(q_m, k_m, v_m) @ lw["w_mo"]
    q_g = q_g.reshape(B, S, GQA_KV_HEADS, GQA_GROUP, GQA_HEAD_DIM) * (GQA_HEAD_DIM ** -0.5)
    y_g = attend(q_g, k_g, v_g) @ lw["w_go"]
    g_f, g_m, g_g = jnp.split(jax.nn.sigmoid(gate_logits + lw["b_gate"]), N_BRANCHES, axis=-1)
    return (g_f * y_f + g_m * y_m + g_g * y_g) @ lw["w_o"]

def sq_relu_mlp(h, lw):
    return jnp.square(jax.nn.relu(h @ lw["w1"])) @ lw["w2"]

def first_inputs(seed: int = 0) -> dict:
    key = jax.random.key(seed)
    ks = iter(jax.random.split(key, 32))

    def nrm(shape, scale):
        return jax.random.normal(next(ks), shape, jnp.float32) * scale

    def gain(shape):
        return 1.0 + nrm(shape, 0.02)

    L, D = DEPTH, D_MODEL
    beta = (8.0 * DEPTH) ** -0.25
    return {
        "x": nrm((BATCH, SEQ, D), 1.0),
        "c": nrm((BATCH, D), 1.0),
        "ctx": nrm((BATCH, CTX_LEN, D), 1.0),
        "c_ctx": nrm((D,), 1.0),
        "w_ada": nrm((L, D, N_MOD * D), 0.5 * D ** -0.5),
        "b_ada": nrm((L, N_MOD * D), 0.01),
        "w_in": nrm((L, D, IN_COLS), D ** -0.5),
        "b_gate": nrm((L, N_BRANCHES * D), 0.01),
        "mla_q_g": gain((L, MLA_Q_RANK)),
        "mla_kv_g": gain((L, MLA_KV_RANK)),
        "w_uq": nrm((L, MLA_Q_RANK, MLA_HEADS * MLA_QK_DIM), MLA_Q_RANK ** -0.5),
        "w_uk": nrm((L, MLA_KV_RANK, MLA_HEADS * MLA_NOPE_DIM), MLA_KV_RANK ** -0.5),
        "w_uv": nrm((L, MLA_KV_RANK, MLA_HEADS * MLA_V_DIM), MLA_KV_RANK ** -0.5),
        "gqa_q_g": gain((L, GQA_HEAD_DIM)),
        "gqa_k_g": gain((L, GQA_HEAD_DIM)),
        "w_fo": nrm((L, F_WIDTH, D), F_WIDTH ** -0.5),
        "w_mo": nrm((L, MLA_WIDTH, D), MLA_WIDTH ** -0.5),
        "w_go": nrm((L, GQA_WIDTH, D), GQA_WIDTH ** -0.5),
        "w_o": nrm((L, D, D), beta * D ** -0.5),
        "ln1_g": gain((L, D)),
        "ln1_b": nrm((L, D), 0.02),
        "w1": nrm((L, D, D_FF), D ** -0.5),
        "w2": nrm((L, D_FF, D), beta * D_FF ** -0.5),
        "ln2_g": gain((L, D)),
        "ln2_b": nrm((L, D), 0.02),
    }

def first_block(x, c, ctx, c_ctx, w_ada, b_ada, w_in, b_gate, mla_q_g, mla_kv_g, w_uq, w_uk, w_uv,
              gqa_q_g, gqa_k_g, w_fo, w_mo, w_go, w_o, ln1_g, ln1_b, w1, w2, ln2_g, ln2_b):
    B, S, D = x.shape
    ROWS = S // GRID_W
    rows = jnp.repeat(jnp.arange(ROWS), GRID_W).astype(jnp.float32)
    cols = jnp.tile(jnp.arange(GRID_W), ROWS).astype(jnp.float32)
    rope = (rope_angles(rows, cols, MLA_ROPE_DIM), rope_angles(rows, cols, GQA_HEAD_DIM))
    alpha = (2.0 * DEPTH) ** 0.25
    xc = ctx
    for l in range(DEPTH):
        last = l == DEPTH - 1
        lw = {
            "w_in": w_in[l], "b_gate": b_gate[l], "mla_q_g": mla_q_g[l], "mla_kv_g": mla_kv_g[l],
            "w_uq": w_uq[l], "w_uk": w_uk[l], "w_uv": w_uv[l], "gqa_q_g": gqa_q_g[l],
            "gqa_k_g": gqa_k_g[l], "w_fo": w_fo[l], "w_mo": w_mo[l], "w_go": w_go[l], "w_o": w_o[l],
            "w1": w1[l], "w2": w2[l],
        }
        mod_x = (jax.nn.silu(c) @ w_ada[l] + b_ada[l])[:, None, :]
        mod_c = (jax.nn.silu(c_ctx) @ w_ada[l] + b_ada[l])[None, None, :]
        sh1, sc1, g1, sh2, sc2, g2 = jnp.split(mod_x, N_MOD, axis=-1)
        csh1, csc1, cg1, csh2, csc2, cg2 = jnp.split(mod_c, N_MOD, axis=-1)

        h_x = modulate(x, sh1, sc1)
        h_c = modulate(xc, csh1, csc1)
        p_x = h_x @ lw["w_in"]
        p_c = h_c @ (lw["w_in"][:, :KV_COLS] if last else lw["w_in"])
        kv_c = kv_parts(p_c, lw, None)
        kv_x = kv_parts(p_x, lw, rope)
        kv_all = (
            jnp.concatenate([kv_c[0], kv_x[0]], axis=1),
            jnp.concatenate([kv_c[1], kv_x[1]], axis=1),
            jnp.concatenate([kv_c[2], kv_x[2]], axis=1),
            jnp.concatenate([kv_c[3], kv_x[3]], axis=1),
        )
        mix_x = mixer(p_x, kv_all, lw, rope)
        x = layer_norm(alpha * x + g1 * mix_x, ln1_g[l], ln1_b[l])
        x = layer_norm(alpha * x + g2 * sq_relu_mlp(modulate(x, sh2, sc2), lw), ln2_g[l], ln2_b[l])

        if not last:
            mix_c = mixer(p_c, kv_c, lw, None)
            xc = layer_norm(alpha * xc + cg1 * mix_c, ln1_g[l], ln1_b[l])
            xc = layer_norm(alpha * xc + cg2 * sq_relu_mlp(modulate(xc, csh2, csc2), lw), ln2_g[l], ln2_b[l])
    return x


DEPTH_2 = 1

CHUNK = 64
D_MIX = D_MODEL
LRU_WIDTH = D_MIX // 4
LRU_HEADS = 4
LRU_HEAD_DIM = LRU_WIDTH // LRU_HEADS
CONV_WIDTH = 4
LRU_C = 8.0
FOX_WIDTH = D_MIX // 2
FOX_HEAD_DIM = 64
FOX_HEADS = FOX_WIDTH // FOX_HEAD_DIM
RWKV_WIDTH = D_MIX - LRU_WIDTH - FOX_WIDTH
RWKV_HEAD_DIM = 64
RWKV_HEADS = RWKV_WIDTH // RWKV_HEAD_DIM
DECAY_RANK = 32
AAA_RANK = 32
GATE_RANK = 64
N_GROUPS = 4
EXPERTS_PER_GROUP = 4
N_EXPERTS = N_GROUPS * EXPERTS_PER_GROUP
TOP_K = 2
D_EXPERT = 256
NORM_EPS = 1e-6
GN_EPS = 64e-5
LRU_COLS = 2 * LRU_WIDTH
FOX_COLS = 3 * FOX_WIDTH + FOX_HEADS
RWKV_COLS = 3 * RWKV_WIDTH + DECAY_RANK + AAA_RANK + GATE_RANK
D_IN = LRU_COLS + FOX_COLS + RWKV_COLS


def rms_norm_2(x, g, eps=NORM_EPS):
    xf = x.astype(jnp.float32)
    y = xf * lax.rsqrt(jnp.mean(xf * xf, axis=-1, keepdims=True) + eps)
    return (y * g.astype(jnp.float32)).astype(x.dtype)

def rglru_group(x_in, gate_in, conv_w, conv_b, wa, ba, wx, bx, lam, norm_g):
    f32 = jnp.float32
    B, S, W = x_in.shape
    xp = jnp.pad(x_in, ((0, 0), (CONV_WIDTH - 1, 0), (0, 0)))
    xc = conv_b + sum(xp[:, j:j + S] * conv_w[j] for j in range(CONV_WIDTH))
    xh = xc.reshape(B, S, LRU_HEADS, LRU_HEAD_DIM)
    r = jax.nn.sigmoid((jnp.einsum('bshi,hij->bshj', xh, wa).reshape(B, S, W) + ba).astype(f32))
    i = jax.nn.sigmoid((jnp.einsum('bshi,hij->bshj', xh, wx).reshape(B, S, W) + bx).astype(f32))
    log_a = -LRU_C * r * jax.nn.softplus(-lam.astype(f32))
    a = jnp.exp(log_a)
    b = jnp.sqrt(-jnp.expm1(2.0 * log_a)) * (i * xc.astype(f32))

    def combine(left, right):
        a1, b1 = left
        a2, b2 = right
        return a1 * a2, a2 * b1 + b2

    _, h = lax.associative_scan(combine, (a, b), axis=1)
    y = jax.nn.gelu(gate_in.astype(f32)) * h
    return rms_norm_2(y.astype(x_in.dtype), norm_g)

def fox_group(q, k, v, f_logit, fb, qn_g, kn_g, norm_g):
    f32 = jnp.float32
    B, S, _ = q.shape
    H, Dh = FOX_HEADS, FOX_HEAD_DIM
    qh = rms_norm_2(q.reshape(B, S, H, Dh), qn_g).transpose(0, 2, 1, 3)
    kh = rms_norm_2(k.reshape(B, S, H, Dh), kn_g).transpose(0, 2, 1, 3)
    vh = v.reshape(B, S, H, Dh).transpose(0, 2, 1, 3)
    log_f = jax.nn.log_sigmoid((f_logit + fb).astype(f32))
    c = jnp.cumsum(log_f, axis=1).transpose(0, 2, 1)
    nb = S // Q_BLOCK
    q_blocks = qh.reshape(B, H, nb, Q_BLOCK, Dh).transpose(2, 0, 1, 3, 4)
    c_blocks = c.reshape(B, H, nb, Q_BLOCK).transpose(2, 0, 1, 3)
    starts = jnp.arange(nb, dtype=jnp.int32) * Q_BLOCK
    k_pos = jnp.arange(S, dtype=jnp.int32)
    scale = FOX_HEAD_DIM ** -0.5

    def block(args):
        qb, cb, s0 = args
        s = jnp.einsum('bhqd,bhkd->bhqk', qb, kh).astype(f32) * scale
        s = s + cb[..., None] - c[:, :, None, :]
        q_pos = s0 + jnp.arange(Q_BLOCK, dtype=jnp.int32)
        mask = k_pos[None, :] <= q_pos[:, None]
        p = jax.nn.softmax(jnp.where(mask, s, -jnp.inf), axis=-1)
        return jnp.einsum('bhqk,bhkd->bhqd', p.astype(vh.dtype), vh)

    o = lax.map(block, (q_blocks, c_blocks, starts))
    o = o.transpose(1, 0, 3, 2, 4).reshape(B, S, FOX_WIDTH)
    return rms_norm_2(o.astype(q.dtype), norm_g)

def rwkv7_group(p, mu, w0, w2, a0, a2, g2, k_k, k_a, r_k, ln_g, ln_b):
    f32 = jnp.float32
    B, S, _ = p.shape
    H, N = RWKV_HEADS, RWKV_HEAD_DIM
    prev = jnp.pad(p, ((0, 0), (1, 0), (0, 0)))[:, :-1]
    p = p + (prev - p) * mu
    o1 = RWKV_WIDTH
    o2 = 2 * RWKV_WIDTH
    o3 = 3 * RWKV_WIDTH
    o4 = o3 + DECAY_RANK
    o5 = o4 + AAA_RANK
    r, k, v, wd, ad, gd = jnp.split(p, [o1, o2, o3, o4, o5], axis=-1)
    r = r.astype(f32)
    k = k.astype(f32)
    v = v.astype(f32)
    w = -jax.nn.softplus(-(w0 + jnp.tanh(wd) @ w2).astype(f32)) - 0.5
    decay = jnp.exp(-jnp.exp(w))
    a = jax.nn.sigmoid((a0 + ad @ a2).astype(f32))
    g = (jax.nn.sigmoid(gd) @ g2).astype(f32)

    def heads(t):
        return t.reshape(B, S, H, N)

    kk = heads(k * k_k)
    kk = kk / jnp.maximum(jnp.sqrt(jnp.sum(kk * kk, axis=-1, keepdims=True)), 1e-12)
    k = k * (1.0 + (a - 1.0) * k_a)
    rh, wh, kh, vh, ah = heads(r), heads(decay), heads(k), heads(v), heads(a)
    n_chunks = S // CHUNK

    def to_chunks(t):
        return t.transpose(1, 0, 2, 3).reshape(n_chunks, CHUNK, B, H, N)

    xs = (to_chunks(rh), to_chunks(wh), to_chunks(kh), to_chunks(vh), to_chunks(kk), to_chunks(kk * ah))

    def frame_step(state, inp):
        r_t, w_t, k_t, v_t, kk_t, b_t = inp
        sa = jnp.einsum('bhvk,bhk->bhv', state, -kk_t)
        state = (state * w_t[:, :, None, :] + sa[..., None] * b_t[:, :, None, :]
                 + v_t[..., None] * k_t[:, :, None, :])
        return state, jnp.einsum('bhvk,bhk->bhv', state, r_t)

    def chunk_step(state, chunk):
        return lax.scan(frame_step, state, chunk)

    state0 = jnp.zeros((B, H, N, N), f32)
    _, o = lax.scan(chunk_step, state0, xs)
    o = o.reshape(S, B, H, N).transpose(1, 0, 2, 3)
    mean = jnp.mean(o, axis=-1, keepdims=True)
    var = jnp.mean(jnp.square(o - mean), axis=-1, keepdims=True)
    o = ((o - mean) * lax.rsqrt(var + GN_EPS)).reshape(B, S, RWKV_WIDTH) * ln_g + ln_b
    bonus = jnp.sum(rh * kh * r_k, axis=-1, keepdims=True) * vh
    return (o + bonus.reshape(B, S, RWKV_WIDTH)) * g

def hier_moe(x, wg, bg, we, be, w_gate, w_up, w_down):
    f32 = jnp.float32
    B, S, D = x.shape
    t = x.reshape(B * S, D)
    g_probs = jax.nn.softmax((t @ wg).astype(f32) + bg, axis=-1)
    g_p, g_idx = lax.top_k(g_probs, 1)
    e_logits = ((t @ we).astype(f32) + be).reshape(-1, N_GROUPS, EXPERTS_PER_GROUP)
    sel = jax.nn.one_hot(g_idx[:, 0], N_GROUPS, dtype=f32)
    e_logits = jnp.einsum('tg,tge->te', sel, e_logits)
    e_p, e_idx = lax.top_k(jax.nn.softmax(e_logits, axis=-1), TOP_K)
    e_p = e_p / jnp.sum(e_p, axis=-1, keepdims=True)
    weights = g_p * e_p
    ids = g_idx * EXPERTS_PER_GROUP + e_idx
    combine = jnp.sum(jax.nn.one_hot(ids, N_EXPERTS, dtype=f32) * weights[..., None], axis=1)
    hid = jax.nn.silu(jnp.einsum('td,edf->tef', t, w_gate)) * jnp.einsum('td,edf->tef', t, w_up)
    hid = hid * combine[..., None].astype(hid.dtype)
    y = jnp.einsum('tef,efd->td', hid, w_down)
    return y.reshape(B, S, D).astype(x.dtype)

def second_inputs(seed: int = 0) -> dict:
    key = jax.random.key(seed)
    ks = iter(jax.random.split(key, 40))
    L = DEPTH_2

    def nrm(shape, scale):
        return jax.random.normal(next(ks), shape, jnp.float32) * scale

    def uni(shape, lo, hi):
        return jax.random.uniform(next(ks), shape, jnp.float32, lo, hi)

    x = nrm((BATCH, SEQ, D_MODEL), 1.0)
    norm1_g = 1.0 + nrm((L, D_MODEL), 0.02)
    w_in = nrm((L, D_MODEL, D_IN), D_MODEL ** -0.5)
    conv_w = nrm((L, CONV_WIDTH, LRU_WIDTH), CONV_WIDTH ** -0.5)
    conv_b = nrm((L, LRU_WIDTH), 0.01)
    lru_wa = nrm((L, LRU_HEADS, LRU_HEAD_DIM, LRU_HEAD_DIM), LRU_HEAD_DIM ** -0.5)
    lru_ba = nrm((L, LRU_WIDTH), 0.01)
    lru_wx = nrm((L, LRU_HEADS, LRU_HEAD_DIM, LRU_HEAD_DIM), LRU_HEAD_DIM ** -0.5)
    lru_bx = nrm((L, LRU_WIDTH), 0.01)
    a_pow = uni((L, LRU_WIDTH), 0.9, 0.999)
    s = a_pow ** (1.0 / LRU_C)
    lru_lambda = jnp.log(s) - jnp.log1p(-s)
    lru_norm_g = 1.0 + nrm((L, LRU_WIDTH), 0.02)
    fox_fb = uni((L, FOX_HEADS), 1.0, 5.0)
    fox_qnorm_g = 1.0 + nrm((L, FOX_HEAD_DIM), 0.02)
    fox_knorm_g = 1.0 + nrm((L, FOX_HEAD_DIM), 0.02)
    fox_norm_g = 1.0 + nrm((L, FOX_WIDTH), 0.02)
    rwkv_mu = uni((L, RWKV_COLS), 0.0, 1.0)
    rwkv_w0 = uni((L, RWKV_WIDTH), -4.0, 0.0)
    rwkv_w2 = nrm((L, DECAY_RANK, RWKV_WIDTH), 0.1 * DECAY_RANK ** -0.5)
    rwkv_a0 = nrm((L, RWKV_WIDTH), 0.1)
    rwkv_a2 = nrm((L, AAA_RANK, RWKV_WIDTH), 0.5 * AAA_RANK ** -0.5)
    rwkv_g2 = nrm((L, GATE_RANK, RWKV_WIDTH), GATE_RANK ** -0.5)
    rwkv_kk = 0.85 + nrm((L, RWKV_WIDTH), 0.05)
    rwkv_ka = 1.0 + nrm((L, RWKV_WIDTH), 0.05)
    rwkv_rk = nrm((L, RWKV_HEADS, RWKV_HEAD_DIM), 0.1)
    rwkv_ln_g = 1.0 + nrm((L, RWKV_WIDTH), 0.02)
    rwkv_ln_b = nrm((L, RWKV_WIDTH), 0.01)
    w_out = nrm((L, D_MIX, D_MODEL), D_MIX ** -0.5)
    norm2_g = 1.0 + nrm((L, D_MODEL), 0.02)
    router_gw = nrm((L, D_MODEL, N_GROUPS), D_MODEL ** -0.5)
    router_gb = nrm((L, N_GROUPS), 0.01)
    router_ew = nrm((L, D_MODEL, N_EXPERTS), D_MODEL ** -0.5)
    router_eb = nrm((L, N_EXPERTS), 0.01)
    exp_w_gate = nrm((L, N_EXPERTS, D_MODEL, D_EXPERT), D_MODEL ** -0.5)
    exp_w_up = nrm((L, N_EXPERTS, D_MODEL, D_EXPERT), D_MODEL ** -0.5)
    exp_w_down = nrm((L, N_EXPERTS, D_EXPERT, D_MODEL), D_EXPERT ** -0.5)
    return {'x': x, 'norm1_g': norm1_g, 'w_in': w_in, 'conv_w': conv_w, 'conv_b': conv_b,
            'lru_wa': lru_wa, 'lru_ba': lru_ba, 'lru_wx': lru_wx, 'lru_bx': lru_bx,
            'lru_lambda': lru_lambda, 'lru_norm_g': lru_norm_g, 'fox_fb': fox_fb,
            'fox_qnorm_g': fox_qnorm_g, 'fox_knorm_g': fox_knorm_g, 'fox_norm_g': fox_norm_g,
            'rwkv_mu': rwkv_mu, 'rwkv_w0': rwkv_w0, 'rwkv_w2': rwkv_w2, 'rwkv_a0': rwkv_a0,
            'rwkv_a2': rwkv_a2, 'rwkv_g2': rwkv_g2, 'rwkv_kk': rwkv_kk, 'rwkv_ka': rwkv_ka,
            'rwkv_rk': rwkv_rk, 'rwkv_ln_g': rwkv_ln_g, 'rwkv_ln_b': rwkv_ln_b, 'w_out': w_out,
            'norm2_g': norm2_g, 'router_gw': router_gw, 'router_gb': router_gb,
            'router_ew': router_ew, 'router_eb': router_eb, 'exp_w_gate': exp_w_gate,
            'exp_w_up': exp_w_up, 'exp_w_down': exp_w_down}

def second_block(x, norm1_g, w_in, conv_w, conv_b, lru_wa, lru_ba, lru_wx, lru_bx, lru_lambda,
              lru_norm_g, fox_fb, fox_qnorm_g, fox_knorm_g, fox_norm_g, rwkv_mu, rwkv_w0,
              rwkv_w2, rwkv_a0, rwkv_a2, rwkv_g2, rwkv_kk, rwkv_ka, rwkv_rk, rwkv_ln_g,
              rwkv_ln_b, w_out, norm2_g, router_gw, router_gb, router_ew, router_eb,
              exp_w_gate, exp_w_up, exp_w_down):
    splits = [LRU_WIDTH, LRU_COLS, LRU_COLS + FOX_WIDTH, LRU_COLS + 2 * FOX_WIDTH,
              LRU_COLS + 3 * FOX_WIDTH, LRU_COLS + FOX_COLS]
    for l in range(DEPTH_2):
        h = rms_norm_2(x, norm1_g[l])
        proj = h @ w_in[l]
        xa, ga, q, k, v, fl, pc = jnp.split(proj, splits, axis=-1)
        ya = rglru_group(xa, ga, conv_w[l], conv_b[l], lru_wa[l], lru_ba[l], lru_wx[l],
                         lru_bx[l], lru_lambda[l], lru_norm_g[l])
        yb = fox_group(q, k, v, fl, fox_fb[l], fox_qnorm_g[l], fox_knorm_g[l], fox_norm_g[l])
        yc = rwkv7_group(pc, rwkv_mu[l], rwkv_w0[l], rwkv_w2[l], rwkv_a0[l], rwkv_a2[l],
                         rwkv_g2[l], rwkv_kk[l], rwkv_ka[l], rwkv_rk[l], rwkv_ln_g[l], rwkv_ln_b[l])
        y = jnp.concatenate([ya, yb.astype(x.dtype), yc.astype(x.dtype)], axis=-1)
        x = x + (y @ w_out[l]).astype(x.dtype)
        x = x + hier_moe(rms_norm_2(x, norm2_g[l]), router_gw[l], router_gb[l], router_ew[l],
                         router_eb[l], exp_w_gate[l], exp_w_up[l], exp_w_down[l])
    return x


def setup_inputs(seed=0):
    out = dict(first_inputs(seed))
    for name, value in second_inputs(seed + 1).items():
        if name != "x":
            out[name + "_2"] = value
    return out


def reference(
    x, c, ctx, c_ctx, w_ada, b_ada, w_in, b_gate, mla_q_g, mla_kv_g, w_uq, w_uk, w_uv, gqa_q_g,
    gqa_k_g, w_fo, w_mo, w_go, w_o, ln1_g, ln1_b, w1, w2, ln2_g, ln2_b, norm1_g_2, w_in_2,
    conv_w_2, conv_b_2, lru_wa_2, lru_ba_2, lru_wx_2, lru_bx_2, lru_lambda_2, lru_norm_g_2,
    fox_fb_2, fox_qnorm_g_2, fox_knorm_g_2, fox_norm_g_2, rwkv_mu_2, rwkv_w0_2, rwkv_w2_2,
    rwkv_a0_2, rwkv_a2_2, rwkv_g2_2, rwkv_kk_2, rwkv_ka_2, rwkv_rk_2, rwkv_ln_g_2, rwkv_ln_b_2,
    w_out_2, norm2_g_2, router_gw_2, router_gb_2, router_ew_2, router_eb_2, exp_w_gate_2,
    exp_w_up_2, exp_w_down_2,
):
    x = first_block(
        x, c, ctx, c_ctx, w_ada, b_ada, w_in, b_gate, mla_q_g, mla_kv_g, w_uq, w_uk, w_uv,
        gqa_q_g, gqa_k_g, w_fo, w_mo, w_go, w_o, ln1_g, ln1_b, w1, w2, ln2_g, ln2_b,
    )
    return second_block(
        x, norm1_g_2, w_in_2, conv_w_2, conv_b_2, lru_wa_2, lru_ba_2, lru_wx_2, lru_bx_2,
        lru_lambda_2, lru_norm_g_2, fox_fb_2, fox_qnorm_g_2, fox_knorm_g_2, fox_norm_g_2,
        rwkv_mu_2, rwkv_w0_2, rwkv_w2_2, rwkv_a0_2, rwkv_a2_2, rwkv_g2_2, rwkv_kk_2, rwkv_ka_2,
        rwkv_rk_2, rwkv_ln_g_2, rwkv_ln_b_2, w_out_2, norm2_g_2, router_gw_2, router_gb_2,
        router_ew_2, router_eb_2, exp_w_gate_2, exp_w_up_2, exp_w_down_2,
    )


_drawn_inputs = setup_inputs


def setup_inputs(seed=0):
    import zlib

    import numpy as np

    out = dict(_drawn_inputs(seed))
    spreads = {}
    factors = {'ctx': 2.986,
     'b_ada': 2.872,
     'b_gate': 8.0,
     'mla_q_g': 8.0,
     'mla_kv_g': 8.0,
     'w_uq': 4.127,
     'w_uk': 5.531,
     'gqa_q_g': 8.0,
     'gqa_k_g': 8.0,
     'lru_ba_2': 8.0,
     'lru_bx_2': 8.0,
     'lru_norm_g_2': 4.645,
     'fox_qnorm_g_2': 3.783,
     'fox_knorm_g_2': 6.41,
     'fox_norm_g_2': 3.734,
     'rwkv_w2_2': 8.0,
     'rwkv_a0_2': 5.802,
     'rwkv_kk_2': 8.0,
     'rwkv_ka_2': 3.376,
     'rwkv_ln_g_2': 8.0,
     'rwkv_ln_b_2': 8.0,
     'norm2_g_2': 4.392,
     'router_gb_2': 8.0,
     'router_eb_2': 8.0}
    for name, (base, spread) in spreads.items():
        noise = np.random.default_rng([zlib.crc32(name.encode()), seed]).standard_normal(out[name].shape)
        drawn = base * np.exp(spread * noise) if base else spread * noise
        out[name] = __import__('jax').numpy.asarray(drawn.astype(out[name].dtype))
    for name, factor in factors.items():
        out[name] = (out[name] * factor).astype(out[name].dtype)
    return out
```

```python
from contextlib import ExitStack

import numpy as np
import concourse.bass as bass
from concourse import mybir

F32 = mybir.dt.float32
ALU = mybir.AluOpType
ACT = mybir.ActivationFunctionType
AX = mybir.AxisListType
EXP_LN = "natural_log_exp_and_others"
SIGMOID = "sigmoid_and_others"

P = 128
D = 1024
KT = D // P
S = 256
DEPTH = 2
N_MOD = 6
EPS = 1e-6
GN_EPS = 64e-5
ALPHA = (2.0 * DEPTH) ** 0.25
HEADS = 8
SCALE_M = 96 ** -0.5
SCALE_G = 64 ** -0.5
FF = 4096
NFF = FF // P
GATE_BLOCKS = 3 * KT
CHUNK = 64
N_EXPERTS = 16
RING = 4
TILE = 2048
BANKS = 8
NEG = -1.0e30

ADA_TILES = N_MOD * KT // 2
IN_TILES = 8
GATE_TILES = GATE_BLOCKS // 2
LAYER_TILES = ADA_TILES + IN_TILES + GATE_TILES + 2 + KT + 4 + 16 + 16
T_ADA = 0
T_IN = T_ADA + ADA_TILES
T_GATE = T_IN + IN_TILES
T_UP = T_GATE + GATE_TILES
T_BR = T_UP + 2
T_O = T_BR + KT
T_W1 = T_O + 4
T_W2 = T_W1 + 16
T_BLOCK2 = DEPTH * LAYER_TILES
T_IN2 = T_BLOCK2
T_V2 = T_IN2 + 10
T_OUT2 = T_V2 + 2
T_MOE = T_OUT2 + 4
N_TILES = T_MOE + 3 * N_EXPERTS
IN_NAMES = ["ckv0", "ckv1", "kr", "kg", "vg", "f0", "f1", "f2", "f3", "cq0", "cq1",
            "qg0", "qg1", "qg2", "qg3"]
IN2_NAMES = (["xa0", "xa1", "ga0", "ga1"] + [f"q{i}" for i in range(4)] + [f"k{i}" for i in range(4)]
             + [f"pc{i}" for i in range(7)] + ["fl"])

COLUMNS = [("c", 8), ("c_ctx", 8), ("b_ada0", 48), ("b_ada1", 48), ("b_gate0", 24), ("b_gate1", 24),
           ("mla_q_g0", 2), ("mla_q_g1", 2), ("mla_kv_g0", 2), ("mla_kv_g1", 2),
           ("gqa_q_g0", 1), ("gqa_q_g1", 1), ("gqa_k_g0", 1), ("gqa_k_g1", 1),
           ("norm1_g", 8), ("conv_w", 8), ("conv_b", 2), ("lru_ba", 2), ("lru_bx", 2),
           ("lru_lambda", 2), ("lru_norm_g", 2), ("fox_q_g", 1), ("fox_k_g", 1), ("fox_norm_g", 4),
           ("fox_fb", 1), ("mu", 7), ("w0", 2), ("a0", 2), ("k_k", 2), ("k_a", 2), ("r_k", 2),
           ("ln_g", 2), ("ln_b", 2), ("norm2_g", 8), ("eps", 1), ("gn_eps", 1), ("one", 1),
           ("zero", 1)]
COL = {}
for _name, _n in COLUMNS:
    COL[_name] = (sum(n for _, n in COLUMNS[:len(COL)]), _n)
N_COL = sum(n for _, n in COLUMNS)

CONST1 = [("ident", 128), ("ones", 128), ("bones", 128), ("dft_d", 256), ("dft_s", 512),
          ("ndft_s", 512), ("rot32", 128), ("rot64", 128), ("cos32", 256), ("sin32", 256),
          ("cos64", 256), ("sin64", 256)]
CONST2 = [("causal", 128), ("strict_incl", 256), ("levels", 6 * 128), ("reset", 256),
          ("lora", 256), ("wa", 256), ("wx", 256), ("w_route", 160), ("b_route", 20), ("rev", 4),
          ("pad", 8)]


def offsets(table):
    out, at = {}, 0
    for name, n in table:
        out[name] = (at, n)
        at += n
    return out, at


C1, N_C1 = offsets(CONST1)
C2, N_C2 = offsets(CONST2)


class Job:
    def __init__(self, bank, turn):
        self.bank, self.turn = bank, turn


class Plan:

    def __init__(self):
        self.turns, self.jobs, self.at = [0] * BANKS, {}, 0

    def add(self, *key, bank=None):
        if bank is None:
            bank, self.at = self.at, (self.at + 1) % BANKS
        self.jobs[key] = Job(bank, self.turns[bank])
        self.turns[bank] += 1

    def __getitem__(self, key):
        return self.jobs[key]


def tiles_of(l):
    return 4 if l < DEPTH - 1 else 2


def attention_items(l):
    out = []
    for branch in ("m", "g"):
        for q in range(tiles_of(l)):
            for h in range(HEADS):
                out.append((branch, q, h, 0, 512) if q < 2 else (branch, q, h, S, S))
    return out


FOX_ITEMS = [("x", q, h, 0, P * (q + 1)) for q in range(2) for h in range(HEADS)]


def plan_attention(plan, tag, items):
    n, tiles = len(items), 0
    for i in range(n + 4):
        if i < n:
            plan.add(tag, "S", i, bank=i % 3)
        if 1 <= i <= n:
            plan.add(tag, "T", i - 1, bank=3 + (i - 1) % 2)
        if 2 <= i < n + 2 and (i - 2) % HEADS == 0:
            plan.add(tag, "O", (i - 2) // HEADS, bank=5 + (i - 2) // HEADS % 2)
        if i >= HEADS + 3 and (i - HEADS - 3) % HEADS == 0:
            plan.add(tag, "OT", (i - HEADS - 3) // HEADS, bank=7)


def plan_jobs():
    p = Plan()
    for l in range(DEPTH):
        n = tiles_of(l)
        p.add(l, "ada")
        for k in range(KT):
            p.add(l, "h1", k)
        for name in IN_NAMES:
            p.add(l, name)
        for name in ["ckv", "cq", "kg"] + [f"qg{b}" for b in range(4)]:
            p.add(l, "ss", name)
        p.at = 0
        for g in range(GATE_BLOCKS):
            p.add(l, "gate", g)
        for name in ["kr", "kg"] + [f"qg{b}" for b in range(4)]:
            p.add(l, "rot", name)
        for b in range(4):
            p.add(l, "kn", b)
        for t in range(4):
            p.add(l, "vm", t)
        for b in range(4):
            p.add(l, "qn", b)
        for b in range(2):
            p.add(l, "qr", b)
        for s in range(n // 2):
            for g in range(4):
                p.add(l, "dft1", s, g)
            for g in range(4):
                p.add(l, "dft2", s, g)
        for b in range(2):
            p.add(l, "rot", f"qr{b}")
        plan_attention(p, (l, "att"), attention_items(l))
        for b in range(KT):
            for r in range(3):
                p.add(l, "branch", b, r)
        for w, out in ((2, "o"), (5, "mlp")):
            if out == "mlp":
                for k in range(KT):
                    p.add(l, "h2", k)
            for v in range(n // 2):
                for half in range(2):
                    p.add(l, "g", w, v, half)
            if out == "mlp":
                for f in range(NFF):
                    p.add(l, "ff", f)
            for half in range(2):
                for t in range(n):
                    p.add(l, out, half, t)
    for k in range(KT):
        p.add("h3", k)
    for name in IN2_NAMES:
        p.add("b2", name)
    for t in range(2):
        p.add("b2", "v", t)
    p.add("lru", "r")
    p.add("lru", "i")
    for name in ("w", "a", "g"):
        p.add("rwkv", name)
    for name in [f"q{b}" for b in range(4)] + [f"k{b}" for b in range(4)]:
        p.add("ss", name)
    p.add("rwkv", "kk")
    plan_attention(p, "fox", FOX_ITEMS)
    p.add("rwkv", "bonus")
    p.add("lru", "ss")
    for name in ("Btok", "Ktok", "Vtok"):
        p.add("rwkv", name)
    for x in ("BR", "KR"):
        for m in range(4):
            p.add("rwkv", x, m)
    p.add("rwkv", "MV")
    for j in range(6):
        for x in ("T1", "X", "XT"):
            if x == "X" and j == 5:
                continue
            for half in range(2):
                p.add("rwkv", x, j, half)
    p.at = 0
    for c in range(4):
        if c:
            p.add("rwkv", "U", c, 0, bank=0)
            p.add("rwkv", "U", c, 1, bank=7)
        p.add("rwkv", "SA", c, bank=1)
        if c < 3:
            p.add("rwkv", "ST", c, bank=2)
    for x in range(4):
        p.add("rwkv", "O", x, bank=3 + x)
    p.add("rwkv", "mean", bank=4)
    p.add("rwkv", "var", bank=5)
    p.at = 0
    for half in range(2):
        for t in range(2):
            p.add("out2", half, t)
    for k in range(KT):
        p.add("h4", k)
    p.add("route")
    p.add("combT")
    for e in range(8):
        p.add("comb", e)
    for half in range(2):
        for t in range(2):
            p.add("moe", half, t, bank=2 * half + t)
    for e in range(N_EXPERTS):
        p.add("gate2", e, bank=4 + 2 * (e % 2))
        p.add("up2", e, bank=5 + 2 * (e % 2))
    return p


def build(nc, stream, columns, const1, const2, x, ctx_in, ln_rows, out):
    plan = plan_jobs()
    with ExitStack() as ctx:
        def sb(name, n):
            return ctx.enter_context(nc.sbuf_tensor(name, [P, n], F32))

        def sem(name):
            return ctx.enter_context(nc.semaphore(name))

        def view(t, at, *dims):
            n = int(np.prod(dims))
            v = t[:, at:at + n]
            if len(dims) == 1:
                return v
            names = "abc"[:len(dims)]
            return v.rearrange(f"p ({' '.join(names)}) -> p {' '.join(names)}",
                               **dict(zip(names[1:], dims[1:])))

        ring_t = sb("ring", RING * TILE)
        resid_t = sb("resid", 4 * D)
        feat_t = sb("feat", KT * 512)
        big = sb("big", NFF * 512)
        c1 = sb("const1_sb", N_C1)
        col = sb("columns_sb", N_COL)
        rows_t = sb("ln_rows_sb", 2 * D)
        gb_t = sb("gain_rows", 2 * D)
        mod_t = sb("mod", 96)
        act_c = sb("silu_c", 16)
        stat = sb("stat", 256)
        work = sb("work", 23 * 512)

        def ring(slot):
            return ring_t[:, slot * TILE:(slot + 1) * TILE]

        resid = view(resid_t, 0, 4, D)
        feat = view(feat_t, 0, KT, 512)
        xn = view(big, 0, 4, D)
        gates = view(big, 0, GATE_BLOCKS, 512)
        hidden = view(big, 0, NFF, 512)
        mod = view(mod_t, 0, 48, 2)
        silu_c = view(act_c, 0, KT, 2)
        gain_rows = view(gb_t, 0, 2, D)
        lnr = view(rows_t, 0, 2, D)
        psum = ctx.enter_context(nc.psum_tensor("psum", [P, BANKS, 512], F32))

        def c(name, rows=slice(0, P)):
            at, n = C1[name]
            return c1[rows, at:at + n]

        def cols(name, i=0, n=1):
            at = COL[name][0] + i
            return col[:, at:at + n]

        ident, ones, bones = c("ident"), c("ones"), c("bones")

        def slots(at, n):
            if at < 23:
                return view(work, at * 512, n, 512)
            return view(big, (GATE_BLOCKS + at - 23) * 512, n, 512)

        ckv, cq = slots(0, 2), slots(2, 2)
        out_m = slots(0, 4)
        kr, kg, vg = slots(4, 1)[:, 0], slots(5, 1)[:, 0], view(work, 6 * 512, 4, P)
        f_in = slots(7, 4)
        qg = slots(11, 4)
        qr = slots(15, 2)
        vm = slots(17, 4)
        out_g = slots(17, 4)
        o_tok = slots(21, 2)
        probs = slots(23, 2)
        probs_t = slots(25, 2)
        dft_mid = slots(23, 4)
        tmp = slots(27, 4)
        qn = feat[:, 0:4]
        kn = feat[:, 4:8]

        c2 = work[:, 0:N_C2]
        at2 = [N_C2]

        def more(*dims):
            n = int(np.prod(dims))
            v = view(work, at2[0], *dims)
            at2[0] += n
            assert at2[0] <= 23 * 512
            return v

        def k2(name, rows=slice(0, P)):
            at, n = C2[name]
            return c2[rows, at:at + n]

        at3 = [0]

        def big2(*dims):
            n = int(np.prod(dims))
            v = view(big, at3[0], *dims)
            at3[0] += n
            assert at3[0] <= NFF * 512
            return v

        y_t = more(KT, S)
        v2 = more(2, 512)
        probs2 = more(2, S)
        probs_t2 = more(2, S)
        o_tok2 = more(2, 512)
        f2 = big2(20, S)
        pm = big2(7, S)
        lru = [big2(2, S) for _ in range(3)]
        rw = {n: big2(2, S) for n in ("ld", "cl", "W", "Wi", "a", "kk", "g", "t")}
        AR = big2(2, 2, S)
        Bm, Km = big2(2, S), big2(2, S)
        BR, KR = view(feat_t, 0, 8, 256), view(feat_t, 2048, 8, 256)
        inv_x, inv_xt = view(rows_t, 0, 8, P), view(rows_t, 1024, 8, P)
        inv_t1 = view(gb_t, 0, 8, P)
        Btok, Ktok, Vtok = (view(resid_t, 2 * D + 512 * i, 2, S) for i in range(3))
        MV = view(resid_t, 2 * D + 1536, 8, 64)
        U_sb, SA_sb = f2[:, 0:1], f2[:, 1:2]
        state = [f2[:, 2, 0:P].rearrange("p (b v) -> p b v", v=64),
                 f2[:, 3, 0:P].rearrange("p (b v) -> p b v", v=64)]
        comb_b = view(big, 0, N_EXPERTS, S)
        hid = view(big, N_EXPERTS * S, 2, 512)
        sig2 = view(big, N_EXPERTS * S + 1024, 2, 512)
        h_t1 = view(big, N_EXPERTS * S + 2048, 2, 512)
        out_sb = view(big, N_EXPERTS * S + 3072, 2, D)
        rt_t = big[:, N_EXPERTS * S + 5120:N_EXPERTS * S + 5632]
        comb16 = view(rt_t, 448, 2, N_EXPERTS)
        combT = view(big, N_EXPERTS * S + 5632, S)

        def probs_sq(s):
            return dft_mid[:, s] if s < 4 else o_tok[:, 0]

        def rw2(name):
            return rw[name].rearrange("p a b -> p (a b)")

        def flat(v):
            return v.rearrange("p a b -> p (a b)")

        def sq2(s):
            return view(feat_t, s * S, S)

        cum, ncum = big2(S), big2(S)
        diag = view(work, 17 * 512, 2, D)
        level_l = [view(gb_t, 1024, 8, P), more(8, P)]
        m8, gq8 = stat[:, 216:218], stat[:, 218:219]

        def rcol(at, *dims):
            return view(rt_t, at, *dims)

        tile_loaded = [sem(f"tile_loaded{i}") for i in range(RING)]
        tiles_started = sem("tiles_started")
        bank_full = [sem(f"bank_full{i}") for i in range(BANKS)]
        bank_free = [sem(f"bank_free{i}") for i in range(BANKS)]
        consts_in = sem("consts_in")
        x_in = sem("x_in")
        const2_in = sem("const2_in")
        rows_in = sem("rows_in")
        rows_used = sem("rows_used")
        out_stored = sem("out_stored")
        silu_exp = sem("silu_exp")
        silu_ready = sem("silu_ready")
        mod_ready = sem("mod_ready")
        stats_ready = sem("stats_ready")
        rstd_ready = sem("rstd_ready")
        xn_ready = sem("xn_ready")
        squares_ready = sem("squares_ready")
        rstd_rows_ready = sem("rstd_rows_ready")
        normed = sem("normed")
        roped = sem("roped")
        neg_max = sem("neg_max")
        mix_ready = sem("mix_ready")
        gated = sem("gated")
        relu_ready = sem("relu_ready")
        gain_diag = sem("gain_diag")
        resid_ready = sem("resid_ready")
        post_rstd = sem("post_rstd")
        post_stats = sem("post_stats")
        b2 = {n: sem("b2_" + n) for n in (
            "log_f_exp", "z", "spl_exp", "spl", "abs_z", "log_f", "cum", "xc", "mixed", "lora", "gelu_arg",
            "gelu", "log_a", "tanh_a", "decay_log", "cl", "expW", "kk_sq", "kk_clamped", "kk_rstd",
            "lnd", "lru_b", "y_sq", "y_rstd", "o_tok_sq", "fox_rstd", "onorm", "AR", "BK",
            "bonus_in", "lev", "U", "ST", "qk", "out", "o_sb", "o_d", "o_sq", "o_rstd", "y_done", "exp_a",
            "sq_in", "rsq", "route_shift", "route_exp", "route2_shift", "route2_exp", "comb",
            "hid", "sig", "kkn", "inv0", "sqrt_b")}

        def full(eng, job):
            eng.wait_ge(bank_full[job.bank], job.turn + 1)

        def freed(eng, job):
            eng.wait_ge(bank_free[job.bank], job.turn + 1)

        def claim(pe, job):
            if job.turn:
                pe.wait_ge(bank_free[job.bank], job.turn)

        block = ctx.enter_context(nc.Block())

        @block.sync
        def _(sp):
            sp.dma_start(c1[:, :], const1).then_inc(consts_in, 16)
            sp.dma_start(col[:, :], columns).then_inc(consts_in, 16)
            for n in range(RING):
                sp.dma_start(ring(n), stream[n]).then_inc(tile_loaded[n], 16)
                if n == 0:
                    sp.dma_start(resid[:, 0:2], x.rearrange("a (t p) d -> p (a t) d", p=P)).then_inc(x_in, 16)
                    sp.dma_start(resid[:, 2:4], ctx_in.rearrange("a (t p) d -> p (a t) d", p=P)).then_inc(x_in, 16)
            with sp.Fori(1, N_TILES // RING) as i:
                for j in range(RING):
                    sp.wait_ge(tiles_started, RING * i + (j - 2))
                    sp.dma_start(ring(j), stream[bass.ds(RING * i + j, 1)].rearrange("a p n -> (a p) n"))\
                        .then_inc(tile_loaded[j], 16)

        @block.tensor
        def _(pe):
            def tile(n):
                pe.wait_ge(tile_loaded[n % RING], 16 * (n // RING + 1))
                return ring(n % RING)

            def feature_blocks(n, names, tag, tokens):
                for b, name in enumerate(names):
                    if b % 2 == 0:
                        w = tile(n + b // 2)
                    job = plan[tag, name]
                    claim(pe, job)
                    T = tokens(name)
                    for k in range(KT):
                        at = (b % 2) * D + k * P
                        if name == "vg":
                            continue
                        mm = pe.matmul(psum[:, job.bank, 0:T], w[:, at:at + P], feat[:, k, 0:T],
                                       start=k == 0, stop=k == KT - 1)
                        if b % 2 == 0 and k == 0:
                            mm.then_inc(tiles_started, 1)
                    if name == "vg":
                        for t in range(4):
                            for k in range(KT):
                                at = (b % 2) * D + k * P
                                mm = pe.matmul(psum[:, job.bank, t * P:t * P + P],
                                               feat[:, k, t * P:t * P + P], w[:, at:at + P],
                                               start=k == 0, stop=k == KT - 1)
                                if t == 0 and k == 0:
                                    mm.then_inc(tiles_started, 1)
                    mm.then_inc(bank_full[job.bank], 1)

            def transposes(tag, tiles, ready, base):
                pe.wait_ge(ready, base)
                for k in range(KT):
                    job = plan[(*tag, k)]
                    claim(pe, job)
                    for t in range(tiles):
                        mm = pe.transpose(psum[:, job.bank, t * P:t * P + P],
                                          xn[:, t, k * P:k * P + P], ident)
                    mm.then_inc(bank_full[job.bank], 1)

            def token_major(n, tag, tiles, kt, lhs):
                per = kt // 4
                for half in range(2):
                    for t in range(tiles):
                        claim(pe, plan[(*tag, half, t)])
                    for g in range(per):
                        w = tile(n + half * per + g)
                        for t in range(tiles):
                            job = plan[(*tag, half, t)]
                            for k in range(4):
                                mm = pe.matmul(psum[:, job.bank, :], lhs(4 * g + k, t),
                                               w[:, k * 512:k * 512 + 512],
                                               start=g == 0 and k == 0, stop=g == per - 1 and k == 3)
                                if t == 0 and k == 0:
                                    mm.then_inc(tiles_started, 1)
                            if g == per - 1:
                                mm.then_inc(bank_full[job.bank], 1)

            def attention(tag, items, S_mm, v_of, probs, probs_t, o_tok):
                n = len(items)
                for i in range(n + 4):
                    if i < n:
                        job = plan[tag, "S", i]
                        claim(pe, job)
                        S_mm(items[i], psum[:, job.bank, 0:items[i][4]]).then_inc(bank_full[job.bank], 1)
                    if 1 <= i <= n:
                        job = plan[tag, "T", i - 1]
                        claim(pe, job)
                        freed(pe, plan[tag, "S", i - 1])
                        for k in range(items[i - 1][4] // P):
                            mm = pe.transpose(psum[:, job.bank, k * P:k * P + P],
                                              probs[:, (i - 1) % 2, k * P:k * P + P], ident)
                        mm.then_inc(bank_full[job.bank], 1)
                    if 2 <= i < n + 2:
                        branch, q, h, first, keys = items[i - 2]
                        job = plan[tag, "O", (i - 2) // HEADS]
                        if h == 0:
                            claim(pe, job)
                        freed(pe, plan[tag, "T", i - 2])
                        mm = None
                        for k in range(keys // P):
                            mm = pe.matmul(psum[:, job.bank, h * 64:h * 64 + 64],
                                           probs_t[:, i % 2, k * P:k * P + P],
                                           v_of(branch, first // P + k, h), start=k == 0,
                                           stop=k == keys // P - 1)
                        if h == HEADS - 1:
                            mm.then_inc(bank_full[job.bank], 1)
                    if i >= HEADS + 3 and (i - HEADS - 3) % HEADS == 0:
                        t = (i - HEADS - 3) // HEADS
                        job = plan[tag, "OT", t]
                        claim(pe, job)
                        if tag == "fox":
                            pe.wait_ge(b2["onorm"], t + 1)
                        else:
                            freed(pe, plan[tag, "O", t])
                        for b in range(4):
                            mm = pe.transpose(psum[:, job.bank, b * P:b * P + P],
                                              o_tok[:, t % 2, b * P:b * P + P], ident)
                        mm.then_inc(bank_full[job.bank], 1)

            def one(job, lhs, rhs, n, wait=None):
                claim(pe, job)
                m = len(lhs)
                for i in range(m):
                    mm = pe.matmul(psum[:, job.bank, 0:n], lhs[i], rhs[i], start=i == 0, stop=i == m - 1)
                mm.then_inc(bank_full[job.bank], 1)

            def gain_rows_mm(l, w, order):
                for v in range(tiles_of(l) // 2):
                    pe.wait_ge(gain_diag, order + v + 1)
                    for half in range(2):
                        one(plan[l, "g", w, v, half], [ones], [diag[:, v, half * 512:half * 512 + 512]], 512)

            pe.wait_ge(consts_in, 32)
            gdiag = 0
            for l in range(DEPTH):
                L, n = l * LAYER_TILES, tiles_of(l)
                T = n * P
                if l == 0:
                    pe.wait_ge(silu_ready, 1)
                job = plan[l, "ada"]
                claim(pe, job)
                with pe.Fori(0, ADA_TILES // RING) as i:
                    for j in range(RING):
                        m = L + T_ADA + j
                        pe.wait_ge(tile_loaded[m % RING], 16 * i + 16 * (m // RING + 1))
                        for b in range(2):
                            for k in range(KT):
                                mm = pe.matmul(psum[:, job.bank, bass.ds(16 * i + (4 * j + 2 * b), 2)],
                                               ring(m % RING)[:, b * D + k * P:b * D + k * P + P],
                                               silu_c[:, k], start=k == 0, stop=k == KT - 1)
                                if b == 0 and k == 0:
                                    mm.then_inc(tiles_started, 1)
                pe.transpose(psum[:, job.bank, 384:512], ident, ident).then_inc(bank_full[job.bank], 1)
                transposes((l, "h1"), 4, xn_ready, 4 + (0, 8)[l])
                for k in range(KT):
                    freed(pe, plan[l, "h1", k])
                feature_blocks(L + T_IN, IN_NAMES, l, lambda name: 512 if name[:2] in ("ck", "kr", "kg") else T)
                pe.wait_ge(squares_ready, 7 * l + 1)
                one(plan[l, "ss", "ckv"], [ones, ones], [tmp[:, 0], tmp[:, 1]], 512)
                pe.wait_ge(squares_ready, 7 * l + 2)
                one(plan[l, "ss", "cq"], [ones, ones], [tmp[:, 2, 0:T], tmp[:, 3, 0:T]], T)
                for s, name in enumerate(["kg"] + [f"qg{b}" for b in range(4)]):
                    pe.wait_ge(squares_ready, 7 * l + 3 + s)
                    one(plan[l, "ss", name], [bones], [probs_sq(s)[:, 0:512 if s == 0 else T]], 512 if s == 0 else T)
                with pe.Fori(0, GATE_BLOCKS // BANKS) as i:
                    for b in range(BANKS):
                        m = L + T_GATE + b // 2
                        job = plan[l, "gate", b]
                        if b % 2 == 0:
                            pe.wait_ge(tile_loaded[m % RING], 16 * i + 16 * (m // RING + 1))
                        pe.wait_ge(bank_free[job.bank], i + job.turn)
                        for k in range(KT):
                            at = (b % 2) * D + k * P
                            mm = pe.matmul(psum[:, job.bank, 0:T], ring(m % RING)[:, at:at + P],
                                           feat[:, k, 0:T], start=k == 0, stop=k == KT - 1)
                            if b % 2 == 0 and k == 0:
                                mm.then_inc(tiles_started, 1)
                        mm.then_inc(bank_full[job.bank], 1)
                base = 7 * l
                pe.wait_ge(normed, base + 7)
                one(plan[l, "rot", "kr"], [c("rot32")], [kr[:, 0:S]], S)
                one(plan[l, "rot", "kg"], [c("rot64")], [kg[:, 0:S]], S)
                for b in range(4):
                    one(plan[l, "rot", f"qg{b}"], [c("rot64")], [qg[:, b, 0:S]], S)
                w = tile(L + T_UP)
                for b in range(4):
                    job = plan[l, "kn", b]
                    claim(pe, job)
                    for k in range(2):
                        mm = pe.matmul(psum[:, job.bank, :], w[:, k * 512 + b * P:k * 512 + b * P + P],
                                       ckv[:, k], start=k == 0, stop=k == 1)
                        if b == 0 and k == 0:
                            mm.then_inc(tiles_started, 1)
                    mm.then_inc(bank_full[job.bank], 1)
                for t in range(4):
                    one(plan[l, "vm", t], [ckv[:, k, t * P:t * P + P] for k in range(2)],
                        [w[:, 1024 + k * 512:1536 + k * 512] for k in range(2)], 512)
                w = tile(L + T_UP + 1)
                for b in range(6):
                    job = plan[l, "qn", b] if b < 4 else plan[l, "qr", b - 4]
                    claim(pe, job)
                    for k in range(2):
                        mm = pe.matmul(psum[:, job.bank, 0:T], w[:, k * 768 + b * P:k * 768 + b * P + P],
                                       cq[:, k, 0:T], start=k == 0, stop=k == 1)
                        if b == 0 and k == 0:
                            mm.then_inc(tiles_started, 1)
                    mm.then_inc(bank_full[job.bank], 1)
                for s in range(n // 2):
                    for g in range(4):
                        job = plan[l, "dft1", s, g]
                        claim(pe, job)
                        for t in range(2):
                            mm = pe.matmul(psum[:, job.bank, t * S:t * S + S],
                                           f_in[:, g, (2 * s + t) * P:(2 * s + t + 1) * P], c("dft_d"),
                                           start=True, stop=True)
                        mm.then_inc(bank_full[job.bank], 1)
                    for g in range(4):
                        freed(pe, plan[l, "dft1", s, g])
                        one(plan[l, "dft2", s, g],
                            [dft_mid[:, g, t * S + h * P:t * S + h * P + P] for h in range(2) for t in range(2)],
                            [c("ndft_s" if h else "dft_s")[:, t * S:t * S + S] for h in range(2) for t in range(2)], S)
                for b in range(2):
                    freed(pe, plan[l, "qr", b])
                    one(plan[l, "rot", f"qr{b}"], [c("rot32")], [qr[:, b, 0:S]], S)

                def S_mm(item, o):
                    branch, q, h, first, keys = item
                    a = slice(first, first + keys)
                    t = slice(q * P, q * P + P)
                    if branch == "m":
                        r = slice(64 * (h % 2), 64 * (h % 2) + 64)
                        pe.matmul(o, qn[r, h // 2, t], kn[r, h // 2, a], start=True, stop=False)
                        r = slice(32 * (h % 4), 32 * (h % 4) + 32)
                        return pe.matmul(o, qr[r, h // 4, t], kr[r, a], start=False, stop=True,
                                         tile_position=(32 * (h % 4), 0))
                    r = slice(64 * (h // 4), 64 * (h // 4) + 64)
                    return pe.matmul(o, qg[r, h % 4, t], kg[r, a], start=True, stop=True)

                def v_of(branch, k, h):
                    if branch == "m":
                        return vm[:, k, h * 64:h * 64 + 64]
                    return vg[:, k, (h // 4) * 64:(h // 4) * 64 + 64]

                pe.wait_ge(roped, 8 * (l + 1))
                for b in range(4):
                    freed(pe, plan[l, "kn", b])
                    freed(pe, plan[l, "vm", b])
                    freed(pe, plan[l, "qn", b])
                attention((l, "att"), attention_items(l), S_mm, v_of, probs, probs_t, o_tok)
                for s in range(n // 2):
                    for g in range(4):
                        freed(pe, plan[l, "dft2", s, g])
                freed(pe, plan[(l, "att"), "OT", 2 * n - 1])
                freed(pe, plan[(l, "att"), "OT", 2 * n - 2])
                for b in range(KT):
                    w = tile(L + T_BR + b)
                    for r, src in enumerate((f_in, out_m, out_g)):
                        job = plan[l, "branch", b, r]
                        claim(pe, job)
                        for k in range(4):
                            mm = pe.matmul(psum[:, job.bank, 0:T], w[:, (4 * r + k) * P:(4 * r + k + 1) * P],
                                           src[:, k, 0:T], start=k == 0, stop=k == 3)
                            if r == 0 and k == 0:
                                mm.then_inc(tiles_started, 1)
                        mm.then_inc(bank_full[job.bank], 1)
                gain_rows_mm(l, 2, gdiag)
                gdiag += n // 2
                pe.wait_ge(mix_ready, KT * (l + 1))
                token_major(L + T_O, (l, "o"), n, KT, lambda k, t: feat[:, k, t * P:t * P + P])
                transposes((l, "h2"), n, xn_ready, (8, 14)[l])
                for k in range(KT):
                    freed(pe, plan[l, "h2", k])
                gain_rows_mm(l, 5, gdiag)
                gdiag += n // 2
                with pe.Fori(0, NFF // BANKS) as i:
                    for b in range(BANKS):
                        m = L + T_W1 + b // 2
                        job = plan[l, "ff", b]
                        if b % 2 == 0:
                            pe.wait_ge(tile_loaded[m % RING], 16 * i + 16 * (m // RING + 1))
                        pe.wait_ge(bank_free[job.bank], i + job.turn)
                        for k in range(KT):
                            at = (b % 2) * D + k * P
                            mm = pe.matmul(psum[:, job.bank, 0:T], ring(m % RING)[:, at:at + P],
                                           feat[:, k, 0:T], start=k == 0, stop=k == KT - 1)
                            if b % 2 == 0 and k == 0:
                                mm.then_inc(tiles_started, 1)
                        mm.then_inc(bank_full[job.bank], 1)
                for f in range(NFF - BANKS, NFF):
                    freed(pe, plan[l, "ff", f])
                token_major(L + T_W2, (l, "mlp"), n, NFF, lambda k, t: hidden[:, k, t * P:t * P + P])

            transposes(("h3",), 2, xn_ready, 16)
            for k in range(KT):
                freed(pe, plan["h3", k])
            feature_blocks(T_IN2, IN2_NAMES, "b2", lambda name: S)
            for t in range(2):
                claim(pe, plan["b2", "v", t])
            for g in range(2):
                w = tile(T_V2 + g)
                for t in range(2):
                    job = plan["b2", "v", t]
                    for k in range(4):
                        mm = pe.matmul(psum[:, job.bank, :], feat[:, 4 * g + k, t * P:t * P + P],
                                       w[:, k * 512:k * 512 + 512], start=g == 0 and k == 0,
                                       stop=g == 1 and k == 3)
                        if t == 0 and k == 0:
                            mm.then_inc(tiles_started, 1)
                    if g == 1:
                        mm.then_inc(bank_full[job.bank], 1)
            pe.wait_ge(const2_in, 16)
            pe.wait_ge(b2["xc"], 1)
            for name, w in (("r", "wa"), ("i", "wx")):
                job = plan["lru", name]
                claim(pe, job)
                for b in range(2):
                    mm = pe.matmul(psum[:, job.bank, b * S:b * S + S], k2(w)[:, b * P:b * P + P], lru[0][:, b],
                                   start=True, stop=True)
                mm.then_inc(bank_full[job.bank], 1)
            pe.wait_ge(b2["lora"], 2)
            for name, r in (("w", slice(0, 32)), ("a", slice(32, 64)), ("g", slice(64, 128))):
                job = plan["rwkv", name]
                claim(pe, job)
                for b in range(2):
                    mm = pe.matmul(psum[:, job.bank, b * S:b * S + S], k2("lora", r)[:, b * P:b * P + P],
                                   pm[r, 6], start=True, stop=True, tile_position=(r.start, 0))
                mm.then_inc(bank_full[job.bank], 1)
            for s in range(8):
                pe.wait_ge(b2["sq_in"], s + 1)
                one(plan["ss", ("q%d" % s) if s < 4 else "k%d" % (s - 4)], [bones], [sq2(s)], S)
            pe.wait_ge(b2["kk_sq"], 1)
            one(plan["rwkv", "kk"], [bones], [rw2("t")], 512)

            def S_fox(item, o):
                _, q, h, first, keys = item
                r = slice(64 * (h % 2), 64 * (h % 2) + 64)
                t = slice(q * P, q * P + P)
                sel = ident[0:HEADS, h:h + 1]
                pe.matmul(o, f2[r, 4 + h // 2, t], f2[r, 8 + h // 2, 0:keys], start=True, stop=False)
                pe.matmul(o, cum[0:HEADS, t], sel.to_broadcast([HEADS, keys]), start=False, stop=False)
                pe.matmul(o[:, keys - P:keys], ident, k2("causal"), start=False, stop=False,
                          skip_group_check=True)
                return pe.matmul(o, sel.to_broadcast([HEADS, P]), ncum[0:HEADS, 0:keys], start=False,
                                 stop=True)

            pe.wait_ge(b2["qk"], 8)
            pe.wait_ge(b2["cum"], 2)
            for t in range(2):
                freed(pe, plan["b2", "v", t])
            attention("fox", FOX_ITEMS, S_fox, lambda branch, k, h: v2[:, k, h * 64:h * 64 + 64],
                      probs2, probs_t2, o_tok2)
            pe.wait_ge(b2["bonus_in"], 1)
            one(plan["rwkv", "bonus"], [bones], [rw2("t")], 512)
            pe.wait_ge(b2["y_sq"], 1)
            one(plan["lru", "ss"], [ones, ones], [lru[2][:, 0], lru[2][:, 1]], S)
            pe.wait_ge(b2["BK"], 1)
            for name, src in (("Btok", Bm), ("Ktok", Km), ("Vtok", pm[:, 4:6])):
                job = plan["rwkv", name]
                claim(pe, job)
                for t in range(2):
                    for b in range(2):
                        mm = pe.transpose(psum[:, job.bank, t * S + b * P:t * S + b * P + P],
                                          src[:, b, t * P:t * P + P], ident)
                mm.then_inc(bank_full[job.bank], 1)
            for name, src in (("BR", Bm), ("KR", Km)):
                for m in range(4):
                    job = plan["rwkv", name, m]
                    claim(pe, job)
                    t, odd = m // 2, m % 2
                    r = slice(64 * odd, 64 * odd + 64)
                    for j in range(2):
                        h = odd + 2 * j
                        mm = pe.matmul(psum[:, job.bank, j * S:j * S + S], src[r, h // 2, t * P:t * P + P],
                                       AR[r, h // 2, :, t * P:t * P + P], start=True, stop=True)
                    mm.then_inc(bank_full[job.bank], 1)
            for m in range(4):
                freed(pe, plan["rwkv", "KR", m])
            for name in ("Btok", "Ktok", "Vtok"):
                freed(pe, plan["rwkv", name])
            job = plan["rwkv", "MV"]
            claim(pe, job)
            for m in range(8):
                mm = pe.matmul(psum[:, job.bank, m * 64:m * 64 + 64], KR[:, m, 0:P],
                               Vtok[:, m // 4, (m % 4) * 64:(m % 4) * 64 + 64], start=True, stop=True)
            mm.then_inc(bank_full[job.bank], 1)
            pe.wait_ge(b2["inv0"], 2)
            for j in range(6):
                pe.wait_ge(b2["lev"], j + 1)
                for half in range(2):
                    job = plan["rwkv", "T1", j, half]
                    claim(pe, job)
                    if j:
                        freed(pe, plan["rwkv", "X", j - 1, half])
                    for m in range(4 * half, 4 * half + 4):
                        mm = pe.matmul(psum[:, job.bank, (m % 4) * P:(m % 4) * P + P], level_l[j % 2][:, m],
                                       inv_x[:, m], start=True, stop=True)
                    mm.then_inc(bank_full[job.bank], 1)
                for what in ("X", "XT"):
                    if what == "X" and j == 5:
                        continue
                    for half in range(2):
                        freed(pe, plan["rwkv", "T1", j, half])
                        job = plan["rwkv", what, j, half]
                        claim(pe, job)
                        if j:
                            freed(pe, plan["rwkv", "XT", j - 1, half])
                        for m in range(4 * half, 4 * half + 4):
                            a, b = (inv_t1, inv_xt) if what == "XT" else (inv_xt, inv_t1)
                            mm = pe.matmul(psum[:, job.bank, (m % 4) * P:(m % 4) * P + P], a[:, m], b[:, m],
                                           start=True, stop=True)
                        mm.then_inc(bank_full[job.bank], 1)
            for half in range(2):
                freed(pe, plan["rwkv", "XT", 5, half])
            for x in range(4):
                claim(pe, plan["rwkv", "O", x])
            for cc in range(4):
                t, r = cc // 2, slice(64 * (cc % 2), 64 * (cc % 2) + 64)
                old = state[cc % 2]
                if cc:
                    pe.wait_ge(b2["ST"], cc)
                    for h in (0, 2, 1, 3):
                        job = plan["rwkv", "U", cc, h % 2]
                        if h < 2:
                            claim(pe, job)
                        rh = slice(64 * (h % 2), 64 * (h % 2) + 64)
                        mm = pe.matmul(psum[r, job.bank, h * 64:h * 64 + 64],
                                       AR[rh, h // 2, 0, cc * 64:cc * 64 + 64], old[rh, h // 2],
                                       start=True, stop=True, tile_position=(rh.start, r.start))
                        if h >= 2:
                            mm.then_inc(bank_full[job.bank], 1)
                pe.wait_ge(b2["U"], cc + 1)
                job = plan["rwkv", "SA", cc]
                claim(pe, job)
                for h in range(4):
                    mm = pe.matmul(psum[r, job.bank, h * 64:h * 64 + 64], inv_xt[r, 4 * t + h, r],
                                   U_sb[r, 0, h * 64:h * 64 + 64], start=True, stop=True,
                                   tile_position=(r.start, r.start))
                mm.then_inc(bank_full[job.bank], 1)
                freed(pe, job)
                if cc < 3:
                    job = plan["rwkv", "ST", cc]
                    claim(pe, job)
                    for h in range(4):
                        rh = slice(64 * (h % 2), 64 * (h % 2) + 64)
                        o = psum[rh, job.bank, (h // 2) * 64:(h // 2) * 64 + 64]
                        hc = slice(h * 64, h * 64 + 64)
                        pe.matmul(o, Btok[r, t, hc], SA_sb[r, 0, hc], start=True, stop=False,
                                  tile_position=(r.start, rh.start))
                        mm = pe.matmul(o, Ktok[r, t, hc], Vtok[r, t, hc], start=False, stop=True,
                                       tile_position=(r.start, rh.start))
                    mm.then_inc(bank_full[job.bank], 1)
                for h in range(4):
                    rh = slice(64 * (h % 2), 64 * (h % 2) + 64)
                    hc, m = slice(h * 64, h * 64 + 64), 4 * t + h
                    at = (h // 2) * S + cc * 64
                    inner, outer = plan["rwkv", "O", cc % 2], plan["rwkv", "O", 2 + h % 2]
                    o = psum[rh, inner.bank, at:at + 64]
                    tr = slice(P + r.start, P + r.stop)
                    pe.matmul(o, Vtok[r, t, hc], KR[r, m, tr], start=True, stop=False,
                              tile_position=(r.start, rh.start))
                    mm = pe.matmul(o, SA_sb[r, 0, hc], BR[r, m, tr], start=False, stop=True,
                                   tile_position=(r.start, rh.start))
                    if cc >= 2 and h == 3:
                        mm.then_inc(bank_full[inner.bank], 1)
                    if cc:
                        mm = pe.matmul(psum[rh, outer.bank, at:at + 64], old[rh, h // 2],
                                       AR[rh, h // 2, 1, cc * 64:cc * 64 + 64],
                                       start=True, stop=True, tile_position=(rh.start, rh.start))
                        if cc == 3 and h >= 2:
                            mm.then_inc(bank_full[outer.bank], 1)
            pe.wait_ge(b2["o_sb"], 1)
            one(plan["rwkv", "mean"], [bones], [rw2("cl")], 512)
            pe.wait_ge(b2["o_sq"], 1)
            one(plan["rwkv", "var"], [bones], [rw2("t")], 512)
            pe.wait_ge(b2["y_done"], 1)
            for t in range(2):
                freed(pe, plan["fox", "OT", t])
            token_major(T_OUT2, ("out2",), 2, KT, lambda k, t: y_t[:, k, t * P:t * P + P])
            transposes(("h4",), 2, xn_ready, 18)
            for k in range(KT):
                freed(pe, plan["h4", k])
            job = plan["route",]
            claim(pe, job)
            for t in range(2):
                for k in range(KT):
                    mm = pe.matmul(psum[:, job.bank, t * 32:t * 32 + 20], feat[:, k, t * P:t * P + P],
                                   k2("w_route")[:, k * 20:k * 20 + 20], start=k == 0, stop=k == KT - 1)
            mm.then_inc(bank_full[job.bank], 1)
            job = plan["combT",]
            claim(pe, job)
            pe.wait_ge(b2["comb"], 1)
            for t in range(2):
                mm = pe.transpose(psum[0:N_EXPERTS, job.bank, t * P:t * P + P],
                                  comb16[:, t], ident)
            mm.then_inc(bank_full[job.bank], 1)
            freed(pe, job)
            for e in range(8):
                job = plan["comb", e]
                claim(pe, job)
                for j in range(2):
                    mm = pe.matmul(psum[:, job.bank, j * S:j * S + S],
                                   ident[0:N_EXPERTS, 2 * e + j:2 * e + j + 1].to_broadcast([N_EXPERTS, P]),
                                   combT[0:N_EXPERTS, :], start=True, stop=True)
                mm.then_inc(bank_full[job.bank], 1)
            for half in range(2):
                for t in range(2):
                    job = plan["moe", half, t]
                    claim(pe, job)
                    pe.matmul(psum[:, job.bank, :], ident, resid[:, t, half * 512:half * 512 + 512],
                              start=True, stop=False)

            def gate_up(n, loaded, e, turn):
                for x, name in enumerate(("gate2", "up2")):
                    job = plan[name, e]
                    pe.wait_ge(tile_loaded[(n + x) % RING], loaded(n + x))
                    turn(job)
                    for b in range(2):
                        for k in range(KT):
                            mm = pe.matmul(psum[:, job.bank, b * S:b * S + S],
                                           ring((n + x) % RING)[:, k * S + b * P:k * S + b * P + P],
                                           feat[:, k, 0:S], start=k == 0, stop=k == KT - 1)
                            if b == 0 and k == 0:
                                mm.then_inc(tiles_started, 1)
                    mm.then_inc(bank_full[job.bank], 1)

            def down(n, loaded, e, ready, last=False):
                pe.wait_ge(tile_loaded[n % RING], loaded(n))
                pe.wait_ge(b2["hid"], ready)
                for half in range(2):
                    for t in range(2):
                        for b in range(2):
                            mm = pe.matmul(psum[:, plan["moe", half, t].bank, :],
                                           hid[:, e % 2, b * S + t * P:b * S + t * P + P],
                                           ring(n % RING)[:, b * D + half * 512:b * D + half * 512 + 512],
                                           start=False, stop=last and b == 1, skip_group_check=not last)
                            if half == 0 and t == 0 and b == 0:
                                mm.then_inc(tiles_started, 1)
                return mm

            static = lambda n: 16 * (n // RING + 1)
            gate_up(T_MOE, static, 0, lambda job: claim(pe, job))
            with pe.Fori(0, 3) as i:
                for j in range(4):
                    n = T_MOE + 2 + 3 * j
                    loaded = lambda n: 48 * i + 16 * (n // RING + 1)
                    gate_up(n, loaded, j + 1, lambda job: pe.wait_ge(bank_free[job.bank], 2 * i + job.turn))
                    down(n + 2, loaded, j, 4 * i + (j + 1))
            for e in range(12, 16):
                n = T_MOE + 2 + 3 * e
                if e < 15:
                    gate_up(n, static, e + 1, lambda job: claim(pe, job))
                    n += 2
                mm = down(n, static, e, e + 1, e == N_EXPERTS - 1)
            mm.then_inc(bank_full[plan["moe", 1, 1].bank], 1)

        @block.vector
        def _(dve):
            count = {"post": 0, "pre": 0, "rows": 0, "rms": 0, "items": 0, "fox": 0}

            def stats(t, at):
                for half in range(2):
                    dve.bn_stats(stat[:, t * 12 + half * 6:t * 12 + half * 6 + 6],
                                 resid[:, t, half * 512:half * 512 + 512])
                dve.drain()
                return dve.bn_aggr(stat[:, 48 + 2 * t:50 + 2 * t], stat[:, t * 12:t * 12 + 12])

            def layer_norm_rows(tiles):
                base = count["post"]
                for t in range(tiles):
                    stats(t, base).then_inc(post_stats, 1)
                dve.wait_ge(rows_in, 16 * (count["rows"] + 1))
                for t in range(tiles):
                    dve.wait_ge(post_rstd, base + t + 1)
                    dve.scalar_tensor_tensor(resid[:, t], resid[:, t], stat[:, 48 + 2 * t:49 + 2 * t],
                                             lnr[:, 0], ALU.subtract, ALU.mult)
                    dve.drain()
                    ins = dve.scalar_tensor_tensor(resid[:, t], resid[:, t], stat[:, 56 + t:57 + t],
                                                   lnr[:, 1], ALU.mult, ALU.add)
                    if t == tiles - 1:
                        ins.then_inc(rows_used, 1)
                    dve.drain()
                count["post"] += tiles
                count["rows"] += 1

            def norm_tokens(tiles):
                base = count["pre"]
                for t in range(tiles):
                    stats(t, base).then_inc(stats_ready, 1)
                for t in range(tiles):
                    dve.wait_ge(rstd_ready, base + t + 1)
                    dve.tensor_scalar(xn[:, t], resid[:, t], stat[:, 48 + 2 * t:49 + 2 * t],
                                      stat[:, 56 + t:57 + t], ALU.subtract, ALU.mult).then_inc(xn_ready, 1)
                count["pre"] += tiles

            def rms_tokens():
                base = count["pre"]
                for t in range(2):
                    dve.wait_ge(rstd_ready, base + t + 1)
                    dve.tensor_scalar(xn[:, t], resid[:, t], stat[:, 56 + t:57 + t], None,
                                      ALU.mult).then_inc(xn_ready, 1)
                count["pre"] += 2

            def modulated(tag, tiles, shift, scale):
                for k in range(0, KT, 2):
                    job = plan[(*tag, k)]
                    full(dve, job)
                    for v in range(tiles // 2):
                        ins = dve.tensor_scalar(feat[:, k, v * S:v * S + S], psum[:, job.bank, v * S:v * S + S],
                                                mod[:, scale * KT + k, v:v + 1], mod[:, shift * KT + k, v:v + 1],
                                                ALU.mult, ALU.add)
                    ins.then_inc(bank_free[job.bank], 1)

            def rope(job, x, cos, sin, s):
                t = tmp[:, s % 4, 0:S]
                full(dve, job)
                dve.tensor_tensor(t, psum[:, job.bank, 0:S], c(sin), ALU.mult).then_inc(bank_free[job.bank], 1)
                dve.tensor_tensor(x[:, 0:S], x[:, 0:S], c(cos), ALU.mult)
                dve.drain()
                dve.tensor_tensor(x[:, 0:S], x[:, 0:S], t, ALU.add).then_inc(roped, 1)

            def residual(tag, tiles):
                s = 0
                for half in range(2):
                    for t in range(tiles):
                        job = plan[(*tag, half, t)]
                        hs = slice(half * 512, half * 512 + 512)
                        full(dve, job)
                        dve.tensor_tensor(o_tok[:, s % 2], psum[:, job.bank, :], gain_rows[:, t // 2, hs],
                                          ALU.mult).then_inc(bank_free[job.bank], 1)
                        dve.drain()
                        dve.scalar_tensor_tensor(resid[:, t, hs], resid[:, t, hs], ALPHA, o_tok[:, s % 2],
                                                 ALU.mult, ALU.add)
                        s += 1
                dve.drain()

            def gain_diagonals(l, w):
                for v in range(tiles_of(l) // 2):
                    dve.tensor_tensor(diag[:, v].rearrange("p (k f) -> p k f", f=P),
                                      ident.unsqueeze(1).to_broadcast([P, KT, P]),
                                      mod[:, w * KT:(w + 1) * KT, v:v + 1].to_broadcast([P, KT, P]),
                                      ALU.mult).then_inc(gain_diag, 1)

            def attention(tag, items, scale, probs_t, o_tok):
                n, base = len(items), count["items"]
                for i in range(n + 4):
                    if i < n:
                        job, m = plan[tag, "S", i], 64 + i
                        full(dve, job)
                        dve.reduce_max(stat[:, 208 + i % 2:209 + i % 2], psum[:, job.bank, 0:items[i][4]], AX.X)
                        dve.drain()
                        dve.tensor_scalar(stat[:, m:m + 1], stat[:, 208 + i % 2:209 + i % 2],
                                          -scale(items[i]), None, ALU.mult).then_inc(neg_max, 1)
                    if 1 <= i <= n and i % 2:
                        job = plan[tag, "T", i - 1]
                        full(dve, job)
                        keys = items[i - 1][4]
                        dve.tensor_copy(probs_t[:, (i - 1) % 2, 0:keys], psum[:, job.bank, 0:keys])\
                            .then_inc(bank_free[job.bank], 1)
                    if tag == "fox" and i >= HEADS + 2 and (i - HEADS - 2) % HEADS == 0:
                        t = (i - HEADS - 2) // HEADS
                        dve.wait_ge(b2["fox_rstd"], t + 1)
                        dve.tensor_scalar(o_tok[:, t % 2], o_tok[:, t % 2], stat[:, 212 + t:213 + t], None,
                                          ALU.mult).then_inc(b2["onorm"], 1)
                    if i >= HEADS + 1 and (i - HEADS - 1) % HEADS == 0:
                        t = (i - HEADS - 1) // HEADS
                        job, r = plan[tag, "O", t], 192 + 8 * (t % 2)
                        freed(dve, plan[tag, "S", HEADS * t + HEADS - 1])
                        dve.reciprocal(stat[:, r:r + HEADS], stat[:, 128 + HEADS * t:128 + HEADS * t + HEADS])
                        full(dve, job)
                        dve.drain()
                        if tag == "fox" and t >= 1:
                            pass
                        dve.tensor_tensor(o_tok[:, t % 2].rearrange("p (h v) -> p h v", v=64),
                                          psum[:, job.bank, :].rearrange("p (h v) -> p h v", v=64),
                                          stat[:, r:r + HEADS].unsqueeze(2).to_broadcast([P, HEADS, 64]),
                                          ALU.mult).then_inc(bank_free[job.bank], 1)
                count["items"] += n

            dve.wait_ge(consts_in, 32)
            dve.wait_ge(silu_exp, 1)
            cc16 = col[:, COL["c"][0]:COL["c"][0] + 16]
            dve.tensor_scalar(stat[:, 16:32], stat[:, 0:16], 1.0, None, ALU.add)
            dve.drain()
            dve.reciprocal(stat[:, 32:48], stat[:, 16:32])
            dve.drain()
            dve.tensor_tensor(silu_c.rearrange("p k v -> p v k"), cc16.rearrange("p (v k) -> p v k", v=2),
                              stat[:, 32:48].rearrange("p (v k) -> p v k", v=2), ALU.mult).then_inc(silu_ready, 1)
            dve.wait_ge(x_in, 32)
            for l in range(DEPTH):
                n = tiles_of(l)
                T = n * P
                norm_tokens(4)
                job = plan[l, "ada"]
                full(dve, job)
                dve.tensor_tensor(mod, psum[:, job.bank, 0:96].rearrange("p (j v) -> p j v", v=2),
                                  cols(f"b_ada{l}", 0, 48).unsqueeze(2).to_broadcast([P, 48, 2]),
                                  ALU.add).then_inc(bank_free[job.bank], 1)
                dve.drain()
                for j in (1, 4):
                    ins = dve.tensor_scalar(mod[:, j * KT:(j + 1) * KT], mod[:, j * KT:(j + 1) * KT], 1.0,
                                            None, ALU.add)
                ins.then_inc(mod_ready, 1)
                dve.drain()
                modulated((l, "h1"), 4, 0, 1)
                for name, to in (("ckv0", ckv[:, 0]), ("ckv1", ckv[:, 1]), ("kr", kr), ("kg", kg),
                                 ("cq0", cq[:, 0]), ("cq1", cq[:, 1]), ("qg0", qg[:, 0]),
                                 ("qg1", qg[:, 1]), ("qg2", qg[:, 2]), ("qg3", qg[:, 3])):
                    job, w = plan[l, name], T if "q" in name else 512
                    full(dve, job)
                    dve.tensor_copy(to[:, 0:w], psum[:, job.bank, 0:w]).then_inc(bank_free[job.bank], 1)
                dve.drain()
                r = 7 * l
                for s, (rows, group) in enumerate([
                        (tmp[:, 0], [(ckv[:, i], f"mla_kv_g{l}", i, 512) for i in range(2)]),
                        (tmp[:, 2], [(cq[:, i], f"mla_q_g{l}", i, T) for i in range(2)]),
                        (probs_sq(0), [(kg, f"gqa_k_g{l}", 0, 512)])]
                        + [(probs_sq(1 + b), [(qg[:, b], f"gqa_q_g{l}", 0, T)]) for b in range(4)]):
                    dve.wait_ge(rstd_rows_ready, r + s + 1)
                    for a, gain, i, w in group:
                        ins = dve.scalar_tensor_tensor(a[:, 0:w], a[:, 0:w], cols(gain, i), rows[:, 0:w],
                                                       ALU.mult, ALU.mult)
                    ins.then_inc(normed, 1)
                dve.drain()
                rope(plan[l, "rot", "kr"], kr, "cos32", "sin32", 0)
                rope(plan[l, "rot", "kg"], kg, "cos64", "sin64", 1)
                for b in range(4):
                    rope(plan[l, "rot", f"qg{b}"], qg[:, b], "cos64", "sin64", 2 + b)
                for t in range(4):
                    job = plan[l, "vm", t]
                    full(dve, job)
                    dve.tensor_copy(vm[:, t], psum[:, job.bank, :]).then_inc(bank_free[job.bank], 1)
                for s in range(n // 2):
                    for g in range(4):
                        job = plan[l, "dft2", s, g]
                        full(dve, job)
                        dve.tensor_copy(f_in[:, g, s * S:s * S + S], psum[:, job.bank, 0:S])\
                            .then_inc(bank_free[job.bank], 1)
                dve.drain()
                for b in range(2):
                    freed(dve, plan[l, "qr", b])
                    rope(plan[l, "rot", f"qr{b}"], qr[:, b], "cos32", "sin32", b)
                attention((l, "att"), attention_items(l), lambda it: SCALE_M if it[0] == "m" else SCALE_G,
                          probs_t, o_tok)
                for b in range(KT):
                    for r in range(3):
                        job, g = plan[l, "branch", b, r], gates[:, r * KT + b, 0:T]
                        full(dve, job)
                        freed(dve, plan[l, "gate", r * KT + b])
                        dve.tensor_tensor(g, psum[:, job.bank, 0:T], g, ALU.mult)\
                            .then_inc(bank_free[job.bank], 1)
                gain_diagonals(l, 2)
                for v in range(n // 2):
                    for half in range(2):
                        freed(dve, plan[l, "g", 2, v, half])
                residual((l, "o"), n)
                layer_norm_rows(n)
                norm_tokens(n)
                modulated((l, "h2"), n, 3, 4)
                gain_diagonals(l, 5)
                with dve.Fori(0, NFF // BANKS) as i:
                    for b in range(BANKS):
                        job = plan[l, "ff", b]
                        dve.wait_ge(relu_ready, 8 * i + (NFF * l + b + 1))
                        f = big[:, bass.ds(4096 * i + 512 * b, T)]
                        dve.scalar_tensor_tensor(f, psum[:, job.bank, 0:T], 0.0, f,
                                                 ALU.max, ALU.mult).then_inc(bank_free[job.bank], 1)
                for v in range(n // 2):
                    for half in range(2):
                        freed(dve, plan[l, "g", 5, v, half])
                residual((l, "mlp"), n)
                layer_norm_rows(n)
                if l == DEPTH - 1:
                    dve.nop().then_inc(resid_ready, 1)

            rms_tokens()

            def gained(tag, name):
                for k in range(0, KT, 2):
                    job = plan[tag, k]
                    full(dve, job)
                    dve.tensor_scalar(feat[:, k, 0:S], psum[:, job.bank, 0:S], cols(name, k), None,
                                      ALU.mult).then_inc(bank_free[job.bank], 1)

            gained("h3", "norm1_g")
            for b in range(0, 20, 2):
                job = plan["b2", IN2_NAMES[b]]
                full(dve, job)
                dve.tensor_copy(f2[:, b], psum[:, job.bank, 0:S]).then_inc(bank_free[job.bank], 1)
            for t in range(2):
                job = plan["b2", "v", t]
                full(dve, job)
                dve.tensor_copy(v2[:, t], psum[:, job.bank, :]).then_inc(bank_free[job.bank], 1)
            for b in range(1, 20, 2):
                freed(dve, plan["b2", IN2_NAMES[b]])
            dve.wait_ge(const2_in, 16)
            dve.drain()
            for b in range(2):
                dve.tensor_scalar(lru[0][:, b], f2[:, b], cols("conv_w", 4 * b + 3), cols("conv_b", b),
                                  ALU.mult, ALU.add)
            for j in (2, 1, 0):
                dve.drain()
                d = 3 - j
                for b in range(2):
                    ins = dve.scalar_tensor_tensor(lru[0][:, b, d:], f2[:, b, 0:S - d],
                                                   cols("conv_w", 4 * b + j), lru[0][:, b, d:],
                                                   ALU.mult, ALU.add)
            ins.then_inc(b2["xc"], 1)
            pc = f2[:, 12:19]
            dve.tensor_tensor(pm[:, :, 1:], pc[:, :, 0:S - 1], pc[:, :, 1:], ALU.subtract)
            dve.tensor_scalar(pm[:, :, 0:1], pc[:, :, 0:1], -1.0, None, ALU.mult)
            dve.drain()
            for b in range(7):
                ins = dve.scalar_tensor_tensor(pm[:, b], pm[:, b], cols("mu", b), pc[:, b], ALU.mult, ALU.add)
            ins.then_inc(b2["mixed"], 1)
            ga, gx = f2[:, 2:4], rw["Wi"]
            dve.tensor_tensor(gx, ga, ga, ALU.mult)
            dve.drain()
            dve.tensor_scalar(gx, gx, 0.044715, 1.0, ALU.mult, ALU.add)
            dve.drain()
            dve.tensor_tensor(gx, gx, ga, ALU.mult).then_inc(b2["gelu_arg"], 1)
            H = slice(0, HEADS)
            dve.tensor_scalar(gq8, cols("fox_q_g"), SCALE_G, None, ALU.mult)
            dve.tensor_scalar(cum[H], f2[H, 19], cols("fox_fb")[H], 0.0, ALU.add, ALU.min).then_inc(b2["z"], 1)
            dve.memset(rw["W"][H, 0], 1.0)
            dve.wait_ge(b2["log_f"], 1)
            dve.drain()
            dve.tensor_tensor(ncum[H], cum[H], f2[H, 19], ALU.subtract)
            dve.drain()
            dve.tensor_tensor_scan(cum[H], rw["W"][H, 0], ncum[H], 0.0, ALU.mult, ALU.add).then_inc(b2["cum"], 1)
            dve.drain()
            dve.tensor_scalar(ncum[H], cum[H], -1.0, None, ALU.mult).then_inc(b2["cum"], 1)
            for b in range(2):
                dve.tensor_scalar(rw["kk"][:, b], pm[:, 2 + b], cols("k_k", b), None, ALU.mult)
            dve.drain()
            dve.tensor_tensor(rw["t"], rw["kk"], rw["kk"], ALU.mult).then_inc(b2["kk_sq"], 1)
            dve.wait_ge(b2["spl"], 1)
            dve.tensor_scalar(m8, stat[:, 220:222], -8.0, None, ALU.mult)
            dve.drain()
            freed(dve, plan["lru", "r"])
            for b in range(2):
                ins = dve.tensor_scalar(lru[1][:, b], lru[1][:, b], m8[:, b:b + 1], None, ALU.mult)
            ins.then_inc(b2["log_a"], 1)
            freed(dve, plan["lru", "i"])
            dve.tensor_tensor(lru[2], lru[2], lru[0], ALU.mult).then_inc(b2["lru_b"], 1)
            freed(dve, plan["rwkv", "w"])
            dve.tensor_scalar(rw["ld"], rw["ld"], -float(np.exp(-0.5)), None, ALU.mult)
            dve.drain()
            for b in range(2):
                dve.tensor_tensor_scan(rw["cl"][:, b], k2("reset"), rw["ld"][:, b], 0.0, ALU.mult, ALU.add)
            dve.drain()
            dve.tensor_tensor(rw["ld"], rw["cl"], rw["ld"], ALU.subtract).then_inc(b2["cl"], 1)
            freed(dve, plan["rwkv", "a"])
            A, R = AR[:, :, 0], AR[:, :, 1]
            for b in range(2):
                dve.tensor_scalar(A[:, b], rw["a"][:, b], -1.0, cols("k_a", b), ALU.add, ALU.mult)
            dve.drain()
            dve.scalar_tensor_tensor(Km, A, 1.0, pm[:, 2:4], ALU.add, ALU.mult)
            dve.wait_ge(b2["gelu"], 1)
            dve.scalar_tensor_tensor(ga, gx, 1.0, ga, ALU.add, ALU.mult)
            dve.wait_ge(b2["tanh_a"], 1)
            u = f2[:, 0:2]
            dve.tensor_scalar(u, u, 2.0 ** -62, None, ALU.max).then_inc(b2["sqrt_b"], 1)
            for s in range(8):
                a = f2[:, 4 + s]
                dve.wait_ge(b2["rsq"], s + 1)
                dve.scalar_tensor_tensor(a, a, gq8 if s < 4 else cols("fox_k_g"), sq2(s), ALU.mult,
                                         ALU.mult).then_inc(b2["qk"], 1)
            job = plan["rwkv", "kk"]
            full(dve, job)
            dve.tensor_scalar(rw2("t"), psum[:, job.bank, :], 1e-24, None, ALU.max)\
                .then_inc(bank_free[job.bank], 1)
            dve.wait_ge(b2["lnd"], 1)
            dve.tensor_tensor(lru[0], lru[0], u, ALU.subtract).then_inc(b2["sqrt_b"], 1)
            dve.wait_ge(b2["exp_a"], 1)
            dve.tensor_tensor(lru[2], lru[2], lru[0], ALU.mult)
            dve.drain()
            for b in range(2):
                dve.tensor_tensor_scan(lru[0][:, b], u[:, b], lru[2][:, b], 0.0, ALU.mult, ALU.add)
            dve.drain()
            dve.scalar_tensor_tensor(lru[1], ga, 0.5, lru[0], ALU.mult, ALU.mult)
            dve.drain()
            dve.tensor_tensor(lru[2], lru[1], lru[1], ALU.mult).then_inc(b2["y_sq"], 1)
            dve.wait_ge(b2["kk_rstd"], 1)
            dve.tensor_tensor(rw["kk"], rw["kk"], rw["t"], ALU.mult)
            for b in range(2):
                dve.scalar_tensor_tensor(R[:, b], pm[:, b], cols("r_k", b), Km[:, b], ALU.mult, ALU.mult)
            dve.drain()
            dve.tensor_copy(rw["t"], R).then_inc(b2["bonus_in"], 1)
            dve.wait_ge(b2["expW"], 3)
            dve.tensor_tensor(Bm, rw["kk"], rw["a"], ALU.mult)
            dve.tensor_tensor(A, rw["kk"], rw["ld"], ALU.mult)
            dve.tensor_tensor(Km, Km, rw["Wi"], ALU.mult)
            dve.drain()
            dve.tensor_tensor(Bm, Bm, rw["Wi"], ALU.mult)
            dve.tensor_tensor(R, pm[:, 0:2], rw["W"], ALU.mult).then_inc(b2["BK"], 1)
            for m in (inv_x, inv_xt):
                dve.tensor_copy(m, ident.unsqueeze(1).to_broadcast([P, 8, P])).then_inc(b2["inv0"], 1)
            attention("fox", FOX_ITEMS, lambda it: 1.0, probs_t2, o_tok2)
            job = plan["rwkv", "bonus"]
            full(dve, job)
            dve.tensor_tensor(flat(pm[:, 2:4]), psum[:, job.bank, :], flat(pm[:, 4:6]), ALU.mult)\
                .then_inc(bank_free[job.bank], 1)
            dve.wait_ge(b2["y_rstd"], 1)
            for b in range(2):
                dve.scalar_tensor_tensor(y_t[:, b], lru[1][:, b], cols("lru_norm_g", b), lru[0][:, 0],
                                         ALU.mult, ALU.mult)
            for name, to in (("Btok", Btok), ("Ktok", Ktok), ("Vtok", Vtok)):
                job = plan["rwkv", name]
                full(dve, job)
                dve.tensor_copy(flat(to), psum[:, job.bank, :]).then_inc(bank_free[job.bank], 1)
            for name, to in (("BR", BR), ("KR", KR)):
                for m in range(4):
                    job = plan["rwkv", name, m]
                    full(dve, job)
                    at = 4 * (m // 2) + m % 2
                    dve.tensor_tensor(to[:, at:at + 3:2], psum[:, job.bank, :].rearrange("p (a b) -> p a b", b=S),
                                      k2("strict_incl").unsqueeze(1).to_broadcast([P, 2, S]),
                                      ALU.mult).then_inc(bank_free[job.bank], 1)
            job = plan["rwkv", "MV"]
            full(dve, job)
            dve.tensor_copy(flat(MV), psum[:, job.bank, :]).then_inc(bank_free[job.bank], 1)
            for j in range(6):
                for what, to in (("X", inv_x), ("XT", inv_xt)):
                    if what == "X" and j == 5:
                        continue
                    for half in range(2):
                        job, v = plan["rwkv", what, j, half], flat(to[:, 4 * half:4 * half + 4])
                        full(dve, job)
                        dve.drain()
                        dve.tensor_tensor(v, v, psum[:, job.bank, :], ALU.subtract)\
                            .then_inc(bank_free[job.bank], 1)
            for cc in range(4):
                t, r = cc // 2, slice(64 * (cc % 2), 64 * (cc % 2) + 64)
                mv = flat(MV[r, 4 * t:4 * t + 4])
                if cc:
                    for odd in range(2):
                        job = plan["rwkv", "U", cc, odd]
                        full(dve, job)
                        of_heads = lambda v: v.rearrange("p (b o v) -> p b o v", o=2, v=64)[:, :, odd]
                        dve.tensor_tensor(of_heads(U_sb[r, 0]), of_heads(psum[r, job.bank, 0:S]),
                                          of_heads(mv), ALU.add).then_inc(bank_free[job.bank], 1)
                    dve.drain()
                    dve.nop().then_inc(b2["U"], 1)
                else:
                    dve.tensor_copy(U_sb[r, 0], mv).then_inc(b2["U"], 1)
                job = plan["rwkv", "SA", cc]
                full(dve, job)
                dve.tensor_scalar(SA_sb[r, 0], psum[r, job.bank, 0:S], -1.0, None, ALU.mult)\
                    .then_inc(bank_free[job.bank], 1)
                if cc < 3:
                    job, new, old = plan["rwkv", "ST", cc], state[(cc + 1) % 2], state[cc % 2]
                    ps = psum[:, job.bank, 0:P].rearrange("p (b v) -> p b v", v=64)
                    full(dve, job)
                    end = rw["W"][:, :, cc * 64 + 63:cc * 64 + 64].to_broadcast([P, 2, 64])
                    if cc:
                        dve.tensor_tensor(new, ps, old, ALU.add).then_inc(bank_free[job.bank], 1)
                    else:
                        dve.tensor_copy(new, ps).then_inc(bank_free[job.bank], 1)
                    dve.drain()
                    dve.tensor_tensor(new, new, end, ALU.mult).then_inc(b2["ST"], 1)
            o, t = rw2("cl"), rw2("t")
            of_chunks = lambda v, odd: v.rearrange("p (a o t) -> p a o t", o=2, t=64)[:, :, odd]
            for odd in range(2):
                job = plan["rwkv", "O", odd]
                full(dve, job)
                dve.tensor_copy(of_chunks(o, odd), of_chunks(psum[:, job.bank, :], odd))\
                    .then_inc(bank_free[job.bank], 1)
            dve.drain()
            for odd in range(2):
                job, r = plan["rwkv", "O", 2 + odd], slice(64 * odd, 64 * odd + 64)
                full(dve, job)
                later = rw["cl"][r, :, CHUNK:]
                dve.tensor_tensor(later, later, psum[r, job.bank, :].rearrange("p (b t) -> p b t", t=S)[:, :, CHUNK:],
                                  ALU.add).then_inc(bank_free[job.bank], 1)
            dve.drain()
            dve.nop().then_inc(b2["o_sb"], 1)
            job = plan["rwkv", "mean"]
            full(dve, job)
            dve.scalar_tensor_tensor(o, psum[:, job.bank, :], -1.0 / 64, o, ALU.mult, ALU.add)\
                .then_inc(bank_free[job.bank], 1)
            dve.drain()
            dve.tensor_tensor(t, o, o, ALU.mult).then_inc(b2["o_sq"], 1)
            dve.wait_ge(b2["o_rstd"], 1)
            dve.tensor_tensor(o, o, rw2("ld"), ALU.mult)
            dve.drain()
            for b in range(2):
                dve.tensor_scalar(rw["cl"][:, b], rw["cl"][:, b], cols("ln_g", b), cols("ln_b", b),
                                  ALU.mult, ALU.add)
            dve.drain()
            dve.tensor_tensor(rw["cl"], rw["cl"], pm[:, 2:4], ALU.add)
            dve.drain()
            dve.tensor_tensor(y_t[:, 6:8], rw["cl"], rw["g"], ALU.mult).then_inc(b2["y_done"], 1)
            for half in range(2):
                for t in range(2):
                    job, hs = plan["out2", half, t], slice(half * 512, half * 512 + 512)
                    full(dve, job)
                    dve.tensor_tensor(resid[:, t, hs], resid[:, t, hs], psum[:, job.bank, :], ALU.add)\
                        .then_inc(bank_free[job.bank], 1)
            dve.drain()
            dve.nop().then_inc(resid_ready, 1)
            rms_tokens()
            gained("h4", "norm2_g")
            job = plan["route",]
            full(dve, job)
            lg = rcol(0, 2, 20)
            dve.tensor_tensor(lg, psum[:, job.bank, 0:64].rearrange("p (t e) -> p t e", e=32)[:, :, 0:20],
                              k2("b_route").unsqueeze(1).to_broadcast([P, 2, 20]), ALU.add)\
                .then_inc(bank_free[job.bank], 1)
            dve.drain()
            rev = k2("rev").unsqueeze(1).to_broadcast([P, 2, 4])
            at = [48]

            def new(*dims):
                v = rcol(at[0], *dims)
                at[0] += int(np.prod(dims))
                return v

            def bc(v, n=4):
                return v.unsqueeze(2).to_broadcast([P, 2, n])

            def first_max(v, top):
                eq, best, hot = new(2, 4), new(2), new(2, 4)
                dve.reduce_max(top, v, AX.X)
                dve.drain()
                dve.tensor_tensor(eq, v, bc(top), ALU.is_equal)
                dve.drain()
                dve.tensor_tensor(eq, eq, rev, ALU.mult)
                dve.drain()
                dve.reduce_max(best, eq, AX.X)
                dve.drain()
                dve.tensor_tensor(hot, rev, bc(best), ALU.is_equal)
                dve.drain()
                return hot

            g_top, g_sh, g_exp, g_sum, g_p = new(2), new(2, 4), new(2, 4), new(2), new(2)
            e_top, e_top2, e_diff, e_exp, e_den = new(2), new(2), new(2), new(2), new(2)
            group = first_max(lg[:, :, 0:4], g_top)
            dve.tensor_tensor(g_sh, lg[:, :, 0:4], bc(g_top), ALU.subtract).then_inc(b2["route_shift"], 1)
            prod, el = new(2, 16), new(2, 4)
            sel16 = [group[:, t].unsqueeze(2).to_broadcast([P, 4, 4]) for t in range(2)]
            for t in range(2):
                dve.tensor_tensor(prod[:, t].rearrange("p (g e) -> p g e", e=4),
                                  lg[:, t, 4:20].rearrange("p (g e) -> p g e", e=4), sel16[t], ALU.mult)
            dve.drain()
            dve.tensor_reduce(el, prod.rearrange("p t (g e) -> p t e g", e=4), AX.X, ALU.add)
            dve.drain()
            hot1 = first_max(el, e_top)
            rest = new(2, 4)
            dve.scalar_tensor_tensor(rest, hot1, -3.0e38, el, ALU.mult, ALU.add)
            dve.drain()
            hot2 = first_max(rest, e_top2)
            dve.tensor_tensor(e_diff, e_top2, e_top, ALU.subtract).then_inc(b2["route2_shift"], 1)
            dve.wait_ge(b2["route_exp"], 1)
            dve.tensor_reduce(g_sum, g_exp, AX.X, ALU.add)
            dve.wait_ge(b2["route2_exp"], 1)
            dve.tensor_scalar(e_den, e_exp, 1.0, None, ALU.add)
            dve.drain()
            dve.tensor_tensor(e_den, e_den, g_sum, ALU.mult)
            dve.drain()
            dve.reciprocal(g_p, e_den)
            dve.drain()
            dve.tensor_tensor(e_exp, e_exp, g_p, ALU.mult)
            dve.tensor_tensor(hot1, hot1, bc(g_p), ALU.mult)
            dve.drain()
            dve.tensor_tensor(hot2, hot2, bc(e_exp), ALU.mult)
            dve.drain()
            dve.tensor_tensor(hot1, hot1, hot2, ALU.add)
            dve.drain()
            for t in range(2):
                ins = dve.tensor_tensor(comb16[:, t].rearrange("p (g e) -> p g e", e=4), sel16[t],
                                        hot1[:, t].unsqueeze(1).to_broadcast([P, 4, 4]), ALU.mult)
            ins.then_inc(b2["comb"], 1)
            assert at[0] <= 448
            job = plan["combT",]
            full(dve, job)
            dve.tensor_copy(combT[0:N_EXPERTS, :], psum[0:N_EXPERTS, job.bank, 0:S])\
                .then_inc(bank_free[job.bank], 1)
            for e in range(8):
                freed(dve, plan["comb", e])
            with dve.Fori(0, N_EXPERTS // 4) as i:
                for j in range(4):
                    g, up, p = plan["gate2", j], plan["up2", j], j % 2
                    dve.wait_ge(b2["sig"], 4 * i + (j + 1))
                    dve.tensor_tensor(h_t1[:, p], sig2[:, p], psum[:, g.bank, :], ALU.mult)\
                        .then_inc(bank_free[g.bank], 1)
                    dve.drain()
                    dve.wait_ge(bank_full[up.bank], 2 * i + (up.turn + 1))
                    dve.tensor_tensor(h_t1[:, p], h_t1[:, p], psum[:, up.bank, :], ALU.mult)\
                        .then_inc(bank_free[up.bank], 1)
                    dve.drain()
                    dve.tensor_tensor(hid[:, p].rearrange("p (b t) -> p b t", t=S),
                                      h_t1[:, p].rearrange("p (b t) -> p b t", t=S),
                                      big[:, bass.ds(4 * S * i + S * j, S)].unsqueeze(1).to_broadcast([P, 2, S]),
                                      ALU.mult).then_inc(b2["hid"], 1)
            full(dve, plan["moe", 1, 1])
            for t in range(2):
                dve.tensor_copy(out_sb[:, t, 0:512], psum[:, plan["moe", 0, t].bank, :])\
                    .then_inc(b2["out"], 1)

        @block.scalar
        def _(act):
            count = {"post": 0, "pre": 0, "items": 0}
            act.preload_act_table_set(EXP_LN)
            act.dma_start(rows_t[:, :], ln_rows[0].partition_broadcast(P)).then_inc(rows_in, 16)
            act.wait_ge(consts_in, 32)
            act.activation(stat[:, 0:16], col[:, COL["c"][0]:COL["c"][0] + 16], ACT.Exp, bias=cols("zero"),
                           scale=-1.0).then_inc(silu_exp, 1)

            def rstd(to, of, eps, scale=1.0):
                act.activation(to, of, ACT.Ln, bias=eps, scale=scale)
                act.drain()
                return act.activation(to, to, ACT.Exp, bias=cols("zero"), scale=-0.5)

            def token_rstd(tiles, ready, done, which):
                for t in range(tiles):
                    act.wait_ge(ready, count[which] + t + 1)
                    rstd(stat[:, 56 + t:57 + t], stat[:, 49 + 2 * t:50 + 2 * t], cols("eps")).then_inc(done, 1)
                count[which] += tiles

            def modulated(tag, tiles, shift, scale):
                for k in range(1, KT, 2):
                    job = plan[(*tag, k)]
                    full(act, job)
                    for v in range(tiles // 2):
                        ins = act.activation(feat[:, k, v * S:v * S + S], psum[:, job.bank, v * S:v * S + S],
                                             ACT.Identity, bias=mod[:, shift * KT + k, v:v + 1],
                                             scale=mod[:, scale * KT + k, v:v + 1])
                    ins.then_inc(bank_free[job.bank], 1)

            def evacuate(job, to, n):
                full(act, job)
                act.activation(to, psum[:, job.bank, 0:n], ACT.Copy).then_inc(bank_free[job.bank], 1)

            def attention(tag, items, scale, probs, probs_t, o_tok, to):
                n, base = len(items), count["items"]
                for i in range(n + 4):
                    if i < n:
                        job, keys = plan[tag, "S", i], items[i][4]
                        act.wait_ge(neg_max, base + i + 1)
                        act.activation(probs[:, i % 2, 0:keys], psum[:, job.bank, 0:keys], ACT.Exp,
                                       bias=stat[:, 64 + i:65 + i], scale=scale(items[i]),
                                       accum_out=stat[:, 128 + i:129 + i]).then_inc(bank_free[job.bank], 1)
                    if 1 <= i <= n and i % 2 == 0:
                        job = plan[tag, "T", i - 1]
                        evacuate(job, probs_t[:, (i - 1) % 2, 0:items[i - 1][4]], items[i - 1][4])
                    if tag == "fox" and i >= HEADS + 1 and (i - HEADS - 1) % HEADS == 0:
                        t = (i - HEADS - 1) // HEADS
                        freed(act, plan[tag, "O", t])
                        act.activation(f2[:, 0:2], o_tok[:, t % 2].rearrange("p (a b) -> p a b", b=S), ACT.Square,
                                       accum_out=stat[:, 212 + t:213 + t])
                        act.drain()
                        rstd(stat[:, 212 + t:213 + t], stat[:, 212 + t:213 + t], cols("eps"), 1.0 / 512)\
                            .then_inc(b2["fox_rstd"], 1)
                    if i >= HEADS + 3 and (i - HEADS - 3) % HEADS == 0:
                        t = (i - HEADS - 3) // HEADS
                        job = plan[tag, "OT", t]
                        full(act, job)
                        to(t, items[HEADS * t], job)
                count["items"] += n

            next_rows = 1
            for l in range(DEPTH):
                n = tiles_of(l)
                T = n * P
                token_rstd(4, stats_ready, rstd_ready, "pre")
                act.wait_ge(mod_ready, l + 1)
                modulated((l, "h1"), 4, 0, 1)
                if l:
                    act.wait_ge(rows_used, next_rows)
                    act.dma_start(rows_t[:, :], ln_rows[next_rows].partition_broadcast(P)).then_inc(rows_in, 16)
                    next_rows += 1

                def squares(name, to, of, signal=True):
                    freed(act, plan[l, name])
                    ins = act.activation(to, of, ACT.Square)
                    if signal:
                        ins.then_inc(squares_ready, 1)

                squares("ckv0", tmp[:, 0], ckv[:, 0], False)
                squares("ckv1", tmp[:, 1], ckv[:, 1])
                evacuate(plan[l, "vg"], vg.rearrange("p a b -> p (a b)"), 512)
                for g in range(4):
                    evacuate(plan[l, f"f{g}"], f_in[:, g, 0:T], T)
                squares("cq0", tmp[:, 2, 0:T], cq[:, 0, 0:T], False)
                squares("cq1", tmp[:, 3, 0:T], cq[:, 1, 0:T])
                squares("kg", probs_sq(0), kg)
                for b in range(4):
                    squares(f"qg{b}", probs_sq(1 + b)[:, 0:T], qg[:, b, 0:T])
                for name, rows, w, k in ([("ckv", tmp[:, 0], 512, 256), ("cq", tmp[:, 2], T, 256),
                                          ("kg", probs_sq(0), 512, 64)]
                                         + [(f"qg{b}", probs_sq(1 + b), T, 64) for b in range(4)]):
                    job = plan[l, "ss", name]
                    full(act, job)
                    act.activation(rows[:, 0:w], psum[:, job.bank, 0:w], ACT.Ln, bias=cols("eps"),
                                   scale=1.0 / k).then_inc(bank_free[job.bank], 1)
                    act.drain()
                    act.activation(rows[:, 0:w], rows[:, 0:w], ACT.Exp, bias=cols("zero"), scale=-0.5)\
                        .then_inc(rstd_rows_ready, 1)
                at = COL[f"b_gate{l}"][0]
                act.preload_act_table_set(SIGMOID)
                with act.Fori(0, GATE_BLOCKS // BANKS) as i:
                    for b in range(BANKS):
                        job = plan[l, "gate", b]
                        act.wait_ge(bank_full[job.bank], i + (job.turn + 1))
                        act.activation(big[:, bass.ds(4096 * i + 512 * b, T)], psum[:, job.bank, 0:T], ACT.Sigmoid,
                                       bias=col[:, bass.ds(8 * i + (at + b), 1)])\
                            .then_inc(bank_free[job.bank], 1)
                act.preload_act_table_set(EXP_LN)
                for b in range(4):
                    evacuate(plan[l, "kn", b], kn[:, b], 512)
                for b in range(4):
                    evacuate(plan[l, "qn", b], qn[:, b, 0:T], T)
                for b in range(2):
                    evacuate(plan[l, "qr", b], qr[:, b, 0:T], T)
                for s in range(n // 2):
                    for g in range(4):
                        evacuate(plan[l, "dft1", s, g], dft_mid[:, g], 512)

                def to_features(t, item, job):
                    to = out_m if item[0] == "m" else out_g
                    q = item[1]
                    act.activation(to[:, 0:4, q * P:q * P + P],
                                   psum[:, job.bank, :].rearrange("p (b t) -> p b t", t=P), ACT.Copy)\
                        .then_inc(bank_free[job.bank], 1)

                attention((l, "att"), attention_items(l), lambda it: SCALE_M if it[0] == "m" else SCALE_G,
                          probs, probs_t, o_tok, to_features)
                for v in range(n // 2):
                    for half in range(2):
                        evacuate(plan[l, "g", 2, v, half], gain_rows[:, v, half * 512:half * 512 + 512], 512)
                if l == DEPTH - 1:
                    act.dma_start(c2, const2).then_inc(const2_in, 16)
                token_rstd(n, post_stats, post_rstd, "post")
                token_rstd(n, stats_ready, rstd_ready, "pre")
                modulated((l, "h2"), n, 3, 4)
                act.wait_ge(rows_used, next_rows)
                act.dma_start(rows_t[:, :], ln_rows[next_rows].partition_broadcast(P)).then_inc(rows_in, 16)
                next_rows += 1
                for v in range(n // 2):
                    for half in range(2):
                        evacuate(plan[l, "g", 5, v, half], gain_rows[:, v, half * 512:half * 512 + 512], 512)
                with act.Fori(0, NFF // BANKS) as i:
                    for b in range(BANKS):
                        job = plan[l, "ff", b]
                        act.wait_ge(bank_full[job.bank], i + (job.turn + 1))
                        act.activation(big[:, bass.ds(4096 * i + 512 * b, T)], psum[:, job.bank, 0:T], ACT.Relu)\
                            .then_inc(relu_ready, 1)
                token_rstd(n, post_stats, post_rstd, "post")

            def rms(wait, scratch):
                act.wait_ge(resid_ready, wait)
                for t in range(2):
                    act.drain()
                    act.activation(scratch, resid[:, t], ACT.Square, accum_out=stat[:, 60 + t:61 + t])
                    act.drain()
                    rstd(stat[:, 56 + t:57 + t], stat[:, 60 + t:61 + t], cols("eps"), 1.0 / D)\
                        .then_inc(rstd_ready, 1)

            def gained(tag, name):
                for k in range(1, KT, 2):
                    job = plan[tag, k]
                    full(act, job)
                    act.activation(feat[:, k, 0:S], psum[:, job.bank, 0:S], ACT.Copy, scale=cols(name, k))\
                        .then_inc(bank_free[job.bank], 1)

            scratch = view(work, 21 * 512, D)
            rms(1, scratch)
            gained("h3", "norm1_g")
            for b in range(1, 20, 2):
                evacuate(plan["b2", IN2_NAMES[b]], f2[:, b], S)
            for b in range(0, 20, 2):
                freed(act, plan["b2", IN2_NAMES[b]])
            for t in range(2):
                freed(act, plan["b2", "v", t])
            act.drain()
            for s in range(8):
                act.activation(sq2(s), f2[:, 4 + s], ACT.Square).then_inc(b2["sq_in"], 1)
            H = slice(0, HEADS)
            act.activation(stat[:, 220:222], cols("lru_lambda", 0, 2), ACT.Exp, bias=cols("zero"), scale=-1.0)
            act.activation(probs2[H, 0], f2[H, 19], ACT.Abs, bias=cols("fox_fb")[H])
            act.drain()
            act.activation(stat[:, 220:222], stat[:, 220:222], ACT.Ln, bias=cols("one")).then_inc(b2["spl"], 1)
            act.activation(probs2[H, 1], probs2[H, 0], ACT.Exp, bias=cols("zero")[H], scale=-1.0)
            act.wait_ge(b2["gelu_arg"], 1)
            act.wait_ge(b2["z"], 1)
            act.drain()
            act.activation(f2[H, 19], probs2[H, 1], ACT.Ln, bias=cols("one")[H]).then_inc(b2["log_f"], 1)
            act.wait_ge(b2["mixed"], 1)
            act.preload_act_table_set(SIGMOID)
            act.activation(pm[0:32, 6], pm[0:32, 6], ACT.Tanh).then_inc(b2["lora"], 1)
            act.activation(pm[64:128, 6], pm[64:128, 6], ACT.Sigmoid).then_inc(b2["lora"], 1)

            def blocks(job, to, func, bias):
                full(act, job)
                for b in range(2):
                    ins = act.activation(to[:, b], psum[:, job.bank, b * S:b * S + S], func, bias=cols(bias, b))
                ins.then_inc(bank_free[job.bank], 1)

            blocks(plan["lru", "r"], lru[1], ACT.Sigmoid, "lru_ba")
            blocks(plan["lru", "i"], lru[2], ACT.Sigmoid, "lru_bx")
            blocks(plan["rwkv", "w"], rw["ld"], ACT.Sigmoid, "w0")
            blocks(plan["rwkv", "a"], rw["a"], ACT.Sigmoid, "a0")
            evacuate(plan["rwkv", "g"], rw2("g"), 512)
            act.activation(rw["Wi"], rw["Wi"], ACT.Tanh, scale=float(np.sqrt(2 / np.pi))).then_inc(b2["gelu"], 1)
            act.wait_ge(b2["log_a"], 1)
            u = f2[:, 0:2]
            act.activation(u, lru[1], ACT.Tanh, scale=-1.0).then_inc(b2["tanh_a"], 1)
            act.preload_act_table_set(EXP_LN)
            for s in range(8):
                job = plan["ss", ("q%d" % s) if s < 4 else "k%d" % (s - 4)]
                full(act, job)
                act.activation(sq2(s), psum[:, job.bank, 0:S], ACT.Ln, bias=cols("eps"), scale=1.0 / 64)\
                    .then_inc(bank_free[job.bank], 1)
                act.drain()
                act.activation(sq2(s), sq2(s), ACT.Exp, bias=cols("zero"), scale=-0.5).then_inc(b2["rsq"], 1)
            act.wait_ge(b2["sqrt_b"], 1)
            act.wait_ge(b2["lru_b"], 1)
            act.activation(lru[0], u, ACT.Ln, bias=cols("zero"), scale=2.0)
            act.activation(u, u, ACT.Ln, bias=cols("one")).then_inc(b2["lnd"], 1)
            act.wait_ge(b2["sqrt_b"], 2)
            act.drain()
            act.activation(lru[0], lru[0], ACT.Exp, bias=cols("zero"), scale=0.5)
            act.activation(u, lru[1], ACT.Exp, bias=cols("zero")).then_inc(b2["exp_a"], 1)
            freed(act, plan["rwkv", "kk"])
            act.activation(rw["t"], rw["t"], ACT.Ln, bias=cols("zero"))
            act.drain()
            act.activation(rw["t"], rw["t"], ACT.Exp, bias=cols("zero"), scale=-0.5).then_inc(b2["kk_rstd"], 1)
            act.wait_ge(b2["cl"], 1)
            act.activation(rw["W"], rw["cl"], ACT.Exp, bias=cols("zero")).then_inc(b2["expW"], 1)
            act.activation(rw["Wi"], rw["cl"], ACT.Exp, bias=cols("zero"), scale=-1.0).then_inc(b2["expW"], 1)
            act.activation(rw["ld"], rw["ld"], ACT.Exp, bias=cols("zero")).then_inc(b2["expW"], 1)

            def fox_features(t, item, job):
                for b in range(4):
                    ins = act.activation(y_t[:, 2 + b, t * P:t * P + P], psum[:, job.bank, b * P:b * P + P],
                                         ACT.Copy, scale=cols("fox_norm_g", b))
                ins.then_inc(bank_free[job.bank], 1)

            attention("fox", FOX_ITEMS, lambda it: 1.0, probs2, probs_t2, o_tok2, fox_features)
            job = plan["lru", "ss"]
            full(act, job)
            act.activation(lru[0][:, 0], psum[:, job.bank, 0:S], ACT.Ln, bias=cols("eps"), scale=1.0 / S)\
                .then_inc(bank_free[job.bank], 1)
            act.drain()
            act.activation(lru[0][:, 0], lru[0][:, 0], ACT.Exp, bias=cols("zero"), scale=-0.5)\
                .then_inc(b2["y_rstd"], 1)
            for j in range(6):
                for half in range(2):
                    evacuate(plan["rwkv", "T1", j, half], flat(inv_t1[:, 4 * half:4 * half + 4]), 512)
            job = plan["rwkv", "var"]
            full(act, job)
            act.activation(rw2("ld"), psum[:, job.bank, :], ACT.Ln, bias=cols("gn_eps"), scale=1.0 / 64)\
                .then_inc(bank_free[job.bank], 1)
            act.drain()
            act.activation(rw2("ld"), rw2("ld"), ACT.Exp, bias=cols("zero"), scale=-0.5).then_inc(b2["o_rstd"], 1)
            rms(2, scratch)
            gained("h4", "norm2_g")
            r = lambda at, *dims: rcol(at, *dims)
            act.wait_ge(b2["route_shift"], 1)
            act.activation(r(58, 8), r(50, 8), ACT.Exp, bias=cols("zero")).then_inc(b2["route_exp"], 1)
            act.wait_ge(b2["route2_shift"], 1)
            act.activation(r(76, 2), r(74, 2), ACT.Exp, bias=cols("zero")).then_inc(b2["route2_exp"], 1)
            for e in range(8):
                evacuate(plan["comb", e], flat(comb_b[:, 2 * e:2 * e + 2]), 512)
            act.preload_act_table_set(SIGMOID)
            with act.Fori(0, N_EXPERTS // 4) as i:
                for j in range(4):
                    job = plan["gate2", j]
                    act.wait_ge(bank_full[job.bank], 2 * i + (job.turn + 1))
                    act.activation(sig2[:, j % 2], psum[:, job.bank, :], ACT.Sigmoid).then_inc(b2["sig"], 1)
            full(act, plan["moe", 1, 1])
            for t in range(2):
                act.activation(out_sb[:, t, 512:1024], psum[:, plan["moe", 1, t].bank, :], ACT.Copy)\
                    .then_inc(b2["out"], 1)
            act.wait_ge(b2["out"], 4)
            act.dma_start(out.rearrange("a (t p) d -> p (a t) d", p=P), out_sb).then_inc(out_stored, 16)
            act.wait_ge(out_stored, 16)

        @block.gpsimd
        def _(pool):
            for l in range(DEPTH):
                T = tiles_of(l) * P
                for b in range(KT):
                    for r in range(3):
                        freed(pool, plan[l, "branch", b, r])
                    g = [gates[:, r * KT + b, 0:T] for r in range(3)]
                    pool.tensor_tensor(g[0], g[0], g[1], ALU.add).then_inc(gated, 1)
                    pool.wait_ge(gated, KT * l + b + 1)
                    pool.tensor_tensor(feat[:, b, 0:T], g[0], g[2], ALU.add).then_inc(mix_ready, 1)
            pool.wait_ge(const2_in, 16)
            for m in range(4):
                freed(pool, plan["rwkv", "BR", m])
            for j in range(6):
                if j >= 2:
                    full(pool, plan["rwkv", "T1", j - 2, 1])
                pool.tensor_tensor(level_l[j % 2], BR[:, :, 0:P],
                                   k2("levels")[:, j * P:j * P + P].unsqueeze(1).to_broadcast([P, 8, P]),
                                   ALU.mult).then_inc(b2["lev"], 1)


def blocks_of(w, names_cols):
    out = np.zeros((len(names_cols), P, w.shape[0] // P, P), w.dtype)
    for i, idx in enumerate(names_cols):
        if len(idx):
            out[i, :, :, :len(idx)] = w[:, idx].reshape(-1, P, len(idx)).transpose(1, 0, 2)
    return out


def pairs(blocks):
    n = blocks.shape[0]
    if n % 2:
        blocks = np.concatenate([blocks, np.zeros_like(blocks[:1])])
    return blocks.reshape(-1, 2, P, D).transpose(0, 2, 1, 3).reshape(-1, P, TILE)


def halves(w):
    k = w.shape[0] // P
    return w.reshape(k // 4, 4, P, 2, 512).transpose(3, 0, 2, 1, 4).reshape(-1, P, TILE)


def padded(a):
    a = a.reshape(P, -1)
    return np.concatenate([a, np.zeros((P, TILE - a.shape[1]), a.dtype)], 1)[None]


def rows_first(w):
    return w.reshape(-1, P, w.shape[1]).transpose(1, 0, 2).reshape(P, -1)


def pack_stream(i):
    r = np.arange
    tiles = []
    for l in range(DEPTH):
        w = i["w_in"][l]
        tiles.append(pairs(blocks_of(i["w_ada"][l], [r(b * P, b * P + P) for b in range(48)])))
        q0 = 544 + 512 + 256
        qg = [np.concatenate([q0 + r(b * 64, b * 64 + 64), q0 + r((b + 4) * 64, (b + 4) * 64 + 64)])
              for b in range(4)]
        tiles.append(pairs(blocks_of(w, [r(0, 128), r(128, 256), np.tile(r(256, 288), 4), r(288, 416),
                                         r(416, 544)] + [544 + r(b * P, b * P + P) for b in range(4)]
                                     + [1056 + r(b * P, b * P + P) for b in range(2)] + qg)))
        tiles.append(pairs(blocks_of(w, [1824 + r(b * P, b * P + P) for b in range(GATE_BLOCKS)])))
        tiles.append(np.concatenate([rows_first(i["w_uk"][l]), rows_first(i["w_uv"][l])], 1)[None])
        heads = i["w_uq"][l].reshape(256, HEADS, 96)
        uq = np.concatenate([heads[:, :, :64].reshape(256, 512), heads[:, :, 64:].reshape(256, 256)], 1)
        tiles.append(padded(rows_first(uq)))
        for b in range(KT):
            tiles.append(padded(np.concatenate([rows_first(i[n][l][:, b * P:b * P + P])
                                                for n in ("w_fo", "w_mo", "w_go")], 1)))
        tiles.append(halves(i["w_o"][l]))
        tiles.append(pairs(blocks_of(i["w1"][l], [r(b * P, b * P + P) for b in range(NFF)])))
        tiles.append(halves(i["w2"][l]))
    w = i["w_in_2"][0]
    starts = [0, 128, 256, 384] + [512 + b * P for b in range(8)] + [2056 + b * P for b in range(7)]
    tiles.append(pairs(blocks_of(w, [r(s, s + P) for s in starts] + [r(2048, 2056)])))
    v = w[:, 1536:2048]
    tiles.append(v.reshape(2, 4, P, 512).transpose(0, 2, 1, 3).reshape(2, P, TILE))
    tiles.append(halves(i["w_out_2"][0]))
    gate = i["exp_w_gate_2"][0].reshape(N_EXPERTS, KT, P, 256).transpose(0, 2, 1, 3).reshape(N_EXPERTS, P, TILE)
    up = i["exp_w_up_2"][0].reshape(N_EXPERTS, KT, P, 256).transpose(0, 2, 1, 3).reshape(N_EXPERTS, P, TILE)
    down = i["exp_w_down_2"][0].reshape(N_EXPERTS, 2, P, D).transpose(0, 2, 1, 3).reshape(N_EXPERTS, P, TILE)
    tiles += [gate[0:1], up[0:1]]
    for e in range(N_EXPERTS):
        if e + 1 < N_EXPERTS:
            tiles += [gate[e + 1:e + 2], up[e + 1:e + 2]]
        tiles.append(down[e:e + 1])
    out = np.concatenate(tiles)
    assert out.shape == (N_TILES, P, TILE), out.shape
    return out


def pack_columns(i):
    out = np.zeros((P, N_COL), np.float32)

    def put(name, a):
        at, n = COL[name]
        a = np.asarray(a)
        out[:a.size // n if a.size < P * n else P, at:at + n] = a.reshape(n, -1).T

    put("c", i["c"][0])
    put("c_ctx", i["c_ctx"])
    for l in range(DEPTH):
        put(f"b_ada{l}", i["b_ada"][l])
        put(f"b_gate{l}", i["b_gate"][l])
        put(f"mla_q_g{l}", i["mla_q_g"][l])
        put(f"mla_kv_g{l}", i["mla_kv_g"][l])
        put(f"gqa_q_g{l}", np.tile(i["gqa_q_g"][l], 2))
        put(f"gqa_k_g{l}", np.tile(i["gqa_k_g"][l], 2))
    put("norm1_g", i["norm1_g_2"][0])
    put("conv_w", i["conv_w_2"][0].reshape(4, 2, P).transpose(1, 0, 2).reshape(-1))
    for name, of in (("conv_b", "conv_b_2"), ("lru_ba", "lru_ba_2"), ("lru_bx", "lru_bx_2"),
                     ("lru_lambda", "lru_lambda_2"), ("lru_norm_g", "lru_norm_g_2"),
                     ("fox_norm_g", "fox_norm_g_2"), ("fox_fb", "fox_fb_2"), ("mu", "rwkv_mu_2"),
                     ("w0", "rwkv_w0_2"), ("a0", "rwkv_a0_2"), ("k_k", "rwkv_kk_2"), ("k_a", "rwkv_ka_2"),
                     ("r_k", "rwkv_rk_2"), ("ln_g", "rwkv_ln_g_2"), ("ln_b", "rwkv_ln_b_2"),
                     ("norm2_g", "norm2_g_2")):
        put(name, i[of][0])
    put("fox_q_g", np.tile(i["fox_qnorm_g_2"][0], 2))
    put("fox_k_g", np.tile(i["fox_knorm_g_2"][0], 2))
    put("eps", np.full(P, EPS, np.float32))
    put("gn_eps", np.full(P, GN_EPS, np.float32))
    put("one", np.ones(P, np.float32))
    return out


def rope_tables(d):
    n = d // 4
    freqs = 10000.0 ** (-np.arange(n, dtype=np.float32) / n)
    t = np.arange(S)
    rows, cols = (t // 64).astype(np.float32), (t % 64).astype(np.float32)
    ang = np.concatenate([rows[:, None] * freqs, cols[:, None] * freqs], 1).astype(np.float32).T
    ang = np.tile(ang, (P // (d // 2), 1))
    return np.cos(ang), np.sin(ang)


def rotation(d):
    m = np.zeros((P, P), np.float32)
    for p in range(P):
        if p % d < d // 2:
            m[p + d // 2, p] = -1.0
        else:
            m[p - d // 2, p] = 1.0
    return m


def constants_1():
    i = np.arange(P)
    bones = (i[:, None] // 64 == i[None] // 64)
    t = np.arange(S)
    norm = (S * P) ** -0.5
    d = 2 * np.pi * np.outer(i, i) / P
    s = 2 * np.pi * np.outer(t, t) / S
    by_tile = lambda a: a.reshape(2, P, S).transpose(1, 0, 2).reshape(P, 512)
    c32, s32 = rope_tables(32)
    c64, s64 = rope_tables(64)
    parts = [np.eye(P), np.ones((P, P)), bones, np.concatenate([np.cos(d), np.sin(d)], 1) * norm,
             by_tile(np.cos(s)), -by_tile(np.sin(s)), rotation(32), rotation(64), c32, s32, c64, s64]
    out = np.concatenate([np.asarray(p, np.float32) for p in parts], 1)
    assert out.shape == (P, N_C1)
    return out


def constants_2(i):
    p = np.arange(P)
    s, t = p[:, None], p[None]
    causal = np.where(t <= s, 0.0, NEG)
    same = s // CHUNK == t // CHUNK
    levels = [(s >> (j + 1) == t >> (j + 1)) & ((s >> j) % 2 == 0) & ((t >> j) % 2 == 1) for j in range(6)]
    reset = np.tile((np.arange(S) % CHUNK != 0).astype(np.float32), (P, 1))

    def diagonal(w):
        out = np.zeros((P, 2, P), np.float32)
        for h in range(4):
            a = slice(64 * (h % 2), 64 * (h % 2) + 64)
            out[a, h // 2, a] = w[0, h]
        return out.reshape(P, 256)

    lora = np.concatenate([i["rwkv_w2_2"][0], i["rwkv_a2_2"][0], i["rwkv_g2_2"][0]], 0)
    route = np.concatenate([i["router_gw_2"][0], i["router_ew_2"][0]], 1)
    bias = np.tile(np.concatenate([i["router_gb_2"][0], i["router_eb_2"][0]]), (P, 1))
    parts = [causal, np.concatenate([same & (s < t), same & (s <= t)], 1), *levels, reset, lora,
             diagonal(i["lru_wa_2"]), diagonal(i["lru_wx_2"]), rows_first(route), bias,
             np.tile([4.0, 3.0, 2.0, 1.0], (P, 1)), np.zeros((P, 8))]
    out = np.concatenate([np.asarray(a, np.float32) for a in parts], 1)
    assert out.shape == (P, N_C2)
    return out


def kernel(**inputs):
    import concourse.bacc as bacc
    from concourse.bass_utils import run_bass_kernel_spmd as run

    i = {k: np.asarray(v) for k, v in inputs.items()}
    arrays = {
        "stream": pack_stream(i), "columns": pack_columns(i), "const1": constants_1(),
        "const2": constants_2(i), "x": np.ascontiguousarray(i["x"]), "ctx": np.ascontiguousarray(i["ctx"]),
        "ln_rows": np.stack([np.concatenate([i[f"ln{n}_g"][l], i[f"ln{n}_b"][l]])
                             for l in range(DEPTH) for n in (1, 2)]),
    }
    nc = bacc.Bacc("TRN2", target_bir_lowering=False, num_devices=1)
    aps = [nc.dram_tensor(name, a.shape, F32, kind="ExternalInput").ap() for name, a in arrays.items()]
    out = nc.dram_tensor("out", (1, S, D), F32, kind="ExternalOutput").ap()
    build(nc, *aps, out)
    r = run(nc, [arrays], core_ids=[0])
    return r.results[0]["out"]
```

```python
from contextlib import ExitStack

import numpy as np
import concourse.bass as bass
from concourse import mybir

F32 = mybir.dt.float32
F32R = mybir.dt.float32r
ALU = mybir.AluOpType
ACT = mybir.ActivationFunctionType
AX = mybir.AxisListType
EXP_LN = "natural_log_exp_and_others"
SIGMOID = "sigmoid_and_others"

P = 128
D = 1024
KT = D // P
S = 256
DEPTH = 2
N_MOD = 6
EPS = 1e-6
GN_EPS = 64e-5
ALPHA = (2.0 * DEPTH) ** 0.25
HEADS = 8
SCALE_M = 96 ** -0.5
SCALE_G = 64 ** -0.5
FF = 4096
NFF = FF // P
GATE_BLOCKS = 3 * KT
CHUNK = 64
N_EXPERTS = 16
RING = 4
TILE = 2048
BANKS = 8
NEG = -1.0e30

ADA_CHUNKS = N_MOD * D // 512
ADA_FIRST = 2 * D // 512
ADA_LATER = ADA_CHUNKS - ADA_FIRST
ADA_TILES = 2 * ADA_FIRST
IN_TILES = 8
GATE_TILES = GATE_BLOCKS // 2
LAYER_TILES = ADA_TILES + IN_TILES + GATE_TILES + 2 + 2 * ADA_LATER + KT + 4 + 16 + 16
T_ADA = 0
T_IN = T_ADA + ADA_TILES
T_GATE = T_IN + IN_TILES
T_UP = T_GATE + GATE_TILES
T_ADA_LATER = T_UP + 2
T_BR = T_ADA_LATER + 2 * ADA_LATER
T_O = T_BR + KT
T_W1 = T_O + 4
T_W2 = T_W1 + 16
T_BLOCK2 = DEPTH * LAYER_TILES
T_IN2 = T_BLOCK2
T_V2 = T_IN2 + 10
T_OUT2 = T_V2 + 2
T_MOE = T_OUT2 + 4
N_TILES = T_MOE + 3 * N_EXPERTS
IN_NAMES = ["ckv0", "ckv1", "kr", "kg", "vg", "f0", "f1", "f2", "f3", "cq0", "cq1",
            "qg0", "qg1", "qg2", "qg3"]
IN2_NAMES = (["xa0", "xa1", "ga0", "ga1"] + [f"q{i}" for i in range(4)] + [f"k{i}" for i in range(4)]
             + [f"pc{i}" for i in range(7)] + ["fl"])

FF_PART = NFF // 2
FF_TILES = FF_PART // 2
SPLIT_RUNS = [(T_IN, T_UP), (T_W1, LAYER_TILES), (LAYER_TILES + T_IN, LAYER_TILES + T_UP),
              (LAYER_TILES + T_W1, T_OUT2), (T_MOE, N_TILES)]
SPLIT_BUFFERS = 4
AHEAD = SPLIT_BUFFERS - 1


def step_of(tile):
    before = 0
    for a, z in SPLIT_RUNS:
        if a <= tile < z:
            return 4 * (before + tile - a)
        before += z - a
    raise ValueError(tile)


def tile_of(step):
    for a, z in SPLIT_RUNS:
        if step < 4 * (z - a):
            return a + step // 4, step % 4
        step -= 4 * (z - a)
    raise ValueError(step)


def run_end(step):
    end = 0
    for a, z in SPLIT_RUNS:
        end += 4 * (z - a)
        if step < end:
            return end
    raise ValueError(step)


class Split:

    def __init__(self, issue):
        self.issue, self.next = issue, 0

    def until(self, n, of):
        while self.next < min(n, run_end(of)):
            self.issue(self.next)
            self.next += 1


COLUMNS = [("c", 8), ("c_ctx", 8), ("b_ada0", 48), ("b_ada1", 48), ("b_gate0", 24), ("b_gate1", 24),
           ("mla_q_g0", 2), ("mla_q_g1", 2), ("mla_kv_g0", 2), ("mla_kv_g1", 2),
           ("gqa_q_g0", 1), ("gqa_q_g1", 1), ("gqa_k_g0", 1), ("gqa_k_g1", 1),
           ("norm1_g", 8), ("conv_w", 8), ("conv_b", 2), ("lru_ba", 2), ("lru_bx", 2),
           ("lru_lambda", 2), ("lru_norm_g", 2), ("fox_q_g", 1), ("fox_k_g", 1), ("fox_norm_g", 4),
           ("fox_fb", 1), ("mu", 7), ("w0", 2), ("a0", 2), ("k_k", 2), ("k_a", 2), ("r_k", 2),
           ("ln_g", 2), ("ln_b", 2), ("norm2_g", 8), ("eps", 1), ("gn_eps", 1), ("one", 1),
           ("zero", 1)]
COL = {}
for _name, _n in COLUMNS:
    COL[_name] = (sum(n for _, n in COLUMNS[:len(COL)]), _n)
N_COL = sum(n for _, n in COLUMNS)

CONST1 = [("ident", 128), ("ones", 128), ("bones", 128), ("dft_d", 256), ("dft_s", 512),
          ("ndft_s", 512), ("rot32", 128), ("rot64", 128), ("cos32", 256), ("sin32", 256),
          ("cos64", 256), ("sin64", 256)]
CONST2 = [("causal", 128), ("strict_incl", 256), ("levels", 6 * 128), ("reset", 256),
          ("lora", 256), ("wa", 256), ("wx", 256), ("w_route", 160), ("b_route", 20), ("rev", 4),
          ("pad", 8)]


def offsets(table):
    out, at = {}, 0
    for name, n in table:
        out[name] = (at, n)
        at += n
    return out, at


C1, N_C1 = offsets(CONST1)
C2, N_C2 = offsets(CONST2)


class Job:
    def __init__(self, bank, turn):
        self.bank, self.turn = bank, turn


class Plan:
    def __init__(self):
        self.turns, self.jobs, self.at = [0] * BANKS, {}, 0
    def add(self, *key, bank=None):
        if bank is None:
            bank, self.at = self.at, (self.at + 1) % BANKS
        self.jobs[key] = Job(bank, self.turns[bank])
        self.turns[bank] += 1
    def __getitem__(self, key):
        return self.jobs[key]


def tiles_of(l):
    return 4 if l < DEPTH - 1 else 2


def attention_items(l):
    out = []
    for branch in ("m", "g"):
        for q in range(tiles_of(l)):
            for h in range(HEADS):
                out.append((branch, q, h, 0, 512) if q < 2 else (branch, q, h, S, S))
    return out


FOX_ITEMS = [("x", q, h, 0, P * (q + 1)) for q in range(2) for h in range(HEADS)]


def ada_parts(l):
    n = len(attention_items(l))
    per = KT * ADA_LATER // n
    return [(per * i, per * (i + 1)) for i in range(n)]


def ada_sums_at(l, i):
    for c in range(ADA_LATER):
        if [first < KT * (c + 1) <= last for first, last in ada_parts(l)].index(True) + 2 == i:
            return c
    return None


def copied_by_dve(tag, item):
    return tag == "fox" and item % 2 == 0


def plan_attention(plan, tag, items):
    n, tiles = len(items), 0
    for i in range(n + 5):
        if i < n:
            plan.add(tag, "S", i, bank=i % 3)
        if 2 <= i < n + 2:
            plan.add(tag, "T", i - 2, bank=3 + i % 2)
        if 3 <= i < n + 3 and (i - 3) % HEADS == 0:
            plan.add(tag, "O", (i - 3) // HEADS, bank=5 + (i - 3) // HEADS % 2)
        if tag != "fox" and ada_sums_at(tag[0], i) is not None:
            plan.add(tag, "ada", ada_sums_at(tag[0], i), bank=7)
        if tag == "fox" and i >= HEADS + 4 and (i - HEADS - 4) % HEADS == 0:
            plan.add(tag, "OT", (i - HEADS - 4) // HEADS, bank=7)


def plan_jobs():
    p = Plan()
    for l in range(DEPTH):
        n = tiles_of(l)
        p.add(l, "ada rows", 0, bank=0)
        p.add(l, "ada rows", 1, bank=1)
        for _ in range(ADA_FIRST // 2 - 1):
            p.add(l, "ada rows, later", 0, bank=0)
            p.add(l, "ada rows, later", 1, bank=1)
        p.add(l, "ada", bank=2)
        for k in range(KT):
            p.add(l, "h1", k)
        for name in IN_NAMES:
            p.add(l, name)
        for name in ["ckv", "cq", "kg"] + [f"qg{b}" for b in range(4)]:
            p.add(l, "ss", name)
        p.at = 0
        for g in range(GATE_BLOCKS):
            p.add(l, "gate", g)
        for name in ["kr", "kg"] + [f"qg{b}" for b in range(4)]:
            p.add(l, "rot", name)
        for b in range(4):
            p.add(l, "kn", b)
        for t in range(4):
            p.add(l, "vm", t)
        for b in range(4):
            p.add(l, "qn", b)
        for b in range(2):
            p.add(l, "qr", b)
        for s in range(n // 2):
            for g in range(4):
                p.add(l, "dft1", s, g)
            for g in range(4):
                p.add(l, "dft2", s, g)
        for b in range(2):
            p.add(l, "rot", f"qr{b}")
        plan_attention(p, (l, "att"), attention_items(l))
        for b in range(KT):
            for r in range(3):
                p.add(l, "branch", b, r)
        for w, out in ((2, "o"), (5, "mlp")):
            if out == "mlp":
                for k in range(KT):
                    p.add(l, "h2", k)
            for v in range(n // 2):
                for half in range(2):
                    p.add(l, "g", w, v, half)
            for part in range(2 if out == "mlp" else 1):
                if out == "mlp":
                    for f in range(FF_PART):
                        p.add(l, "ff", part * FF_PART + f)
                for half in range(2):
                    for t in range(n):
                        p.add(l, out, part, half, t)
    for k in range(KT):
        p.add("h3", k)
    for name in IN2_NAMES:
        p.add("b2", name)
    for t in range(2):
        p.add("b2", "v", t)
    p.add("lru", "r")
    p.add("lru", "i")
    for name in ("w", "a", "g"):
        p.add("rwkv", name)
    for name in [f"q{b}" for b in range(4)] + [f"k{b}" for b in range(4)]:
        p.add("ss", name)
    p.add("rwkv", "kk")
    plan_attention(p, "fox", FOX_ITEMS)
    p.add("rwkv", "bonus")
    p.add("lru", "ss")
    for name in ("Btok", "Ktok", "Vtok"):
        p.add("rwkv", name)
    for x in ("BR", "KR"):
        for m in range(4):
            p.add("rwkv", x, m)
    p.add("rwkv", "MV")
    for j in range(6):
        for x in ("T1", "X", "XT"):
            if x == "X" and j == 5:
                continue
            for half in range(2):
                p.add("rwkv", x, j, half)
    p.at = 0
    for c in range(4):
        if c:
            p.add("rwkv", "U", c, 0, bank=0)
            p.add("rwkv", "U", c, 1, bank=7)
        p.add("rwkv", "SA", c, bank=1)
        if c < 3:
            p.add("rwkv", "ST", c, bank=2)
    for x in range(4):
        p.add("rwkv", "O", x, bank=3 + x)
    p.add("rwkv", "mean", bank=4)
    p.add("rwkv", "var", bank=5)
    p.at = 0
    for half in range(2):
        for t in range(2):
            p.add("out2", half, t)
    for k in range(KT):
        p.add("h4", k)
    p.add("route", bank=0)
    p.add("combT", bank=1)
    for e in range(8):
        p.add("comb", e, bank=e % 4)
    for half in range(2):
        for t in range(2):
            p.add("moe", half, t, bank=2 * half + t)
    for e in range(N_EXPERTS):
        p.add("gate2", e, bank=4 + 2 * (e % 2))
        p.add("up2", e, bank=5 + 2 * (e % 2))
    return p


def build(nc, stream, columns, const1, const2, x, ctx_in, ln_rows, out):
    plan = plan_jobs()
    with ExitStack() as ctx:
        def sb(name, n):
            return ctx.enter_context(nc.sbuf_tensor(name, [P, n], F32))
        def sem(name):
            return ctx.enter_context(nc.semaphore(name))
        def view(t, at, *dims):
            n = int(np.prod(dims))
            v = t[:, at:at + n]
            if len(dims) == 1:
                return v
            names = "abc"[:len(dims)]
            return v.rearrange(f"p ({' '.join(names)}) -> p {' '.join(names)}",
                               **dict(zip(names[1:], dims[1:])))
        ring_t = sb("ring", RING * TILE)
        resid_t = sb("resid", 4 * D)
        def over(name, n):
            with nc.sbuf_tensor(name, [P, n], F32R) as t:
                return t
        feat_r = over("feat_high", KT * 512)
        feat_t = sb("feat", KT * 512)
        big_r = over("hidden_parts", NFF * 512)
        big = sb("big", NFF * 512)
        c1 = sb("const1_sb", N_C1)
        col = sb("columns_sb", N_COL)
        feat_low_r = over("feat_low", KT * 512)
        rows_t = sb("ln_rows_sb", 2 * D)
        gb_t = sb("gain_rows", 2 * D)
        mod_t = sb("mod", 96)
        act_c = sb("silu_c", 16)
        stat = sb("stat", 224)
        with nc.sbuf_tensor("below_mlp_low", [P, 8 * 512], F32):
            mlp_low_r = over("mlp_low", KT * 512)
        with nc.sbuf_tensor("below_split", [P, 17 * 512], F32):
            split_r = over("split_weights", 2 * SPLIT_BUFFERS * 512)
        work = sb("work", 25 * 512)
        def ring(slot):
            return ring_t[:, slot * TILE:(slot + 1) * TILE]
        resid = view(resid_t, 0, 4, D)
        feat = view(feat_t, 0, KT, 512)
        xn = view(big, 0, 4, D)
        ada_rows = view(big, 4 * D, 2, 512)
        gates = view(big, 0, GATE_BLOCKS, 512)
        w_hi, w_lo = (view(split_r, i * SPLIT_BUFFERS * 512, SPLIT_BUFFERS, 512) for i in range(2))
        feat_hi, feat_lo, mlp_lo = (view(t, 0, KT, 512) for t in (feat_r, feat_low_r, mlp_low_r))
        ff_hi, ff_lo = (view(big_r, i * FF_PART * 512, FF_PART, 512) for i in range(2))
        mod = view(mod_t, 0, 48, 2)
        silu_c = view(act_c, 0, KT, 2)
        gain_rows = view(gb_t, 0, 2, D)
        lnr = view(rows_t, 0, 2, D)
        psum = ctx.enter_context(nc.psum_tensor("psum", [P, BANKS, 512], F32))
        def c(name, rows=slice(0, P)):
            at, n = C1[name]
            return c1[rows, at:at + n]
        def cols(name, i=0, n=1):
            at = COL[name][0] + i
            return col[:, at:at + n]
        ident, ones, bones = c("ident"), c("ones"), c("bones")
        def slots(at, n):
            if at < 23:
                return view(work, at * 512, n, 512)
            return view(big, (GATE_BLOCKS + at - 23) * 512, n, 512)
        ckv, cq = slots(0, 2), slots(2, 2)
        out_m = slots(0, 4)
        kr, kg, vg = slots(4, 1)[:, 0], slots(5, 1)[:, 0], view(work, 6 * 512, 4, P)
        f_in = slots(7, 4)
        qg = slots(11, 4)
        qr = slots(15, 2)
        vm = slots(17, 4)
        out_g = slots(17, 4)
        o_tok = slots(21, 2)
        probs = slots(23, 3)
        probs_t = view(work, 23 * 512, 2, 512)
        dft_mid = slots(23, 4)
        tmp = slots(27, 4)
        ada_sum = [tmp[:, 0:2], tmp[:, 2:4]]
        qn = feat[:, 0:4]
        kn = feat[:, 4:8]
        c2 = work[:, 0:N_C2]
        at2 = [N_C2]
        def more(*dims):
            n = int(np.prod(dims))
            v = view(work, at2[0], *dims)
            at2[0] += n
            assert at2[0] <= 23 * 512
            return v
        def k2(name, rows=slice(0, P)):
            at, n = C2[name]
            return c2[rows, at:at + n]
        at3 = [0]
        def big2(*dims):
            n = int(np.prod(dims))
            v = view(big, at3[0], *dims)
            at3[0] += n
            assert at3[0] <= NFF * 512
            return v
        y_t = more(KT, S)
        v2 = more(2, 512)
        probs2 = more(3, S)
        probs_t2 = more(2, S)
        o_tok2 = more(2, 512)
        f2 = big2(20, S)
        pm = big2(7, S)
        lru = [big2(2, S) for _ in range(3)]
        rw = {n: big2(2, S) for n in ("ld", "cl", "W", "Wi", "a", "kk", "g", "t")}
        AR = big2(2, 2, S)
        Bm, Km = big2(2, S), big2(2, S)
        BR, KR = view(feat_t, 0, 8, 256), view(feat_t, 2048, 8, 256)
        inv_x, inv_xt = view(rows_t, 0, 8, P), view(rows_t, 1024, 8, P)
        inv_t1 = view(gb_t, 0, 8, P)
        Btok, Ktok, Vtok = (view(resid_t, 2 * D + 512 * i, 2, S) for i in range(3))
        MV = view(resid_t, 2 * D + 1536, 8, 64)
        U_sb, SA_sb = f2[:, 0:1], f2[:, 1:2]
        state = [f2[:, 2, 0:P].rearrange("p (b v) -> p b v", v=64),
                 f2[:, 3, 0:P].rearrange("p (b v) -> p b v", v=64)]
        comb_b = view(big, 0, N_EXPERTS, S)
        hid = view(big, N_EXPERTS * S, 2, 512)
        hid_hi, hid_lo = (view(big_r, 10240 + 1024 * i, 2, 512) for i in range(2))
        sig2 = view(big, N_EXPERTS * S + 1024, 2, 512)
        h_t1 = view(big, N_EXPERTS * S + 2048, 2, 512)
        out_sb = view(big, N_EXPERTS * S + 3072, 2, D)
        rt_t = big[:, N_EXPERTS * S + 5120:N_EXPERTS * S + 5632]
        comb16 = view(rt_t, 448, 2, N_EXPERTS)
        combT = view(big, N_EXPERTS * S + 5632, S)
        def probs_sq(s):
            return dft_mid[:, s] if s < 4 else qr[:, 0]
        def rw2(name):
            return rw[name].rearrange("p a b -> p (a b)")
        def flat(v):
            return v.rearrange("p a b -> p (a b)")
        def sq2(s):
            return view(feat_t, s * S, S)
        cum, ncum = big2(S), big2(S)
        diag = {2: view(work, 11 * 512, 2, D), 5: view(big, 4 * D, 2, D)}
        relu = [slots(5, 1)[:, 0], slots(6, 1)[:, 0]]
        exact = [slots(7, 1)[:, 0], slots(16, 1)[:, 0]]
        level_l = [view(gb_t, 1024, 8, P), more(8, P)]
        m8, gq8 = stat[:, 216:218], stat[:, 218:219]
        def rcol(at, *dims):
            return view(rt_t, at, *dims)
        tile_loaded = [sem(f"tile_loaded{i}") for i in range(RING)]
        tiles_started = sem("tiles_started")
        bank_full = [sem(f"bank_full{i}") for i in range(BANKS)]
        bank_free = [sem(f"bank_free{i}") for i in range(BANKS)]
        consts_in = sem("consts_in")
        x_in = sem("x_in")
        const2_in = sem("const2_in")
        rows_in = sem("rows_in")
        rows_used = sem("rows_used")
        out_stored = sem("out_stored")
        split_started = sem("split_started")
        ada_partial = sem("ada_partial")
        split_high = sem("split_high")
        split_low = sem("split_low")
        feat_exact = sem("feat_exact")
        feat_high = sem("feat_high_ready")
        hidden_high = sem("hidden_high")
        relu_free = sem("relu_free")
        silu_exp = sem("silu_exp")
        silu_ready = sem("silu_ready")
        stats_ready = sem("stats_ready")
        rstd_ready = sem("rstd_ready")
        xn_ready = sem("xn_ready")
        squares_ready = sem("squares_ready")
        rstd_rows_ready = sem("rstd_rows_ready")
        normed = sem("normed")
        roped = sem("roped")
        neg_max = sem("neg_max")
        sum_inverse = sem("sum_inverse")
        probs_ready = sem("probs_ready")
        mix_ready = sem("mix_ready")
        gated = sem("gated")
        gain_diag = sem("gain_diag")
        resid_ready = sem("resid_ready")
        post_rstd = sem("post_rstd")
        post_stats = sem("post_stats")
        b2 = {n: sem("b2_" + n) for n in (
            "log_f_exp", "z", "spl_exp", "spl", "abs_z", "log_f", "cum", "xc", "mixed", "lora", "gelu_arg",
            "gelu", "log_a", "tanh_a", "decay_log", "cl", "expW", "kk_sq", "kk_clamped", "kk_rstd",
            "lnd", "lru_b", "y_sq", "y_rstd", "o_tok_sq", "fox_rstd", "onorm", "AR", "BK",
            "bonus_in", "lev", "U", "ST", "qk", "out", "o_sb", "o_d", "o_sq", "o_rstd", "y_done", "exp_a",
            "sq_in", "rsq", "route_shift", "route_exp", "route2_shift", "route2_exp", "comb",
            "hid", "sig", "hid_exact", "hid_high", "kkn", "inv0", "sqrt_b")}
        def full(eng, job):
            eng.wait_ge(bank_full[job.bank], job.turn + 1)
        def freed(eng, job):
            eng.wait_ge(bank_free[job.bank], job.turn + 1)
        def claim(pe, job):
            if job.turn:
                pe.wait_ge(bank_free[job.bank], job.turn)
        def first_item(tag):
            return sum(len(attention_items(l)) for l in range(tag[0]))
        def moe_experts(eng, split, part, expert, weight):
            m0 = step_of(T_MOE)
            def single(e):
                g = m0 + (12 * e - 4 if e else 0)
                expert(e, lambda n: split.until(g + n + AHEAD, m0), weight(e * S))
            single(0)
            single(1)
            with eng.Fori(0, 3) as i:
                for e in range(2, 6):
                    at = [m0 + 12 * e - 8 + AHEAD]
                    def steps(n):
                        while at[0] < m0 + 12 * e - 4 + n + AHEAD:
                            part(at[0], i, 48)
                            at[0] += 1
                    expert(e, steps, weight(4 * S * i + S * e), i, 48, 4, 2)
            split.next = m0 + 12 * 14 - 8 + AHEAD
            for e in range(14, N_EXPERTS):
                single(e)
            split.until(step_of(N_TILES - 1) + 4, m0)
        block = ctx.enter_context(nc.Block())
        @block.sync
        def _(sp):
            sp.dma_start(c1[:, :], const1).then_inc(consts_in, 16)
            sp.dma_start(col[:, :], columns).then_inc(consts_in, 16)
            for n in range(RING):
                sp.dma_start(ring(n), stream[n]).then_inc(tile_loaded[n], 16)
                if n == 0:
                    sp.dma_start(resid[:, 0:2], x.rearrange("a (t p) d -> p (a t) d", p=P)).then_inc(x_in, 16)
                    sp.dma_start(resid[:, 2:4], ctx_in.rearrange("a (t p) d -> p (a t) d", p=P)).then_inc(x_in, 16)
            with sp.Fori(1, N_TILES // RING) as i:
                for j in range(RING):
                    sp.wait_ge(tiles_started, RING * i + (j - 2))
                    sp.dma_start(ring(j), stream[bass.ds(RING * i + j, 1)].rearrange("a p n -> (a p) n"))\
                        .then_inc(tile_loaded[j], 16)
        @block.tensor
        def _(pe):
            def tile(n):
                pe.wait_ge(tile_loaded[n % RING], 16 * (n // RING + 1))
                return ring(n % RING)
            def products(out, a, b, start, stop):
                return [pe.matmul(out, a[i], b[j], start=start and i + j == 0, stop=stop and i == 1)
                        for i, j in ((0, 0), (0, 1), (1, 0))]
            def take(s, i=0, per=0):
                pe.wait_ge(split_low, per * i + (s + 1))
            def started(s, mm):
                mm[0].then_inc(split_started, 1)
                if tile_of(s)[1] == 0:
                    mm[1].then_inc(tiles_started, 1)
            def weights(s, cols):
                return w_hi[:, s % SPLIT_BUFFERS, cols], w_lo[:, s % SPLIT_BUFFERS, cols]
            def block_products(s, out, T, low, i=0, per=0, tag=None):
                for q in range(2):
                    take(s + q, i, per)
                    for kk in range(4):
                        k = 4 * q + kk
                        if tag:
                            freed(pe, plan[(*tag, k)])
                        mm = products(out, weights(s + q, slice(kk * P, kk * P + P)),
                                      (feat_hi[:, k, 0:T], low[:, k, 0:T]), k == 0, k == KT - 1)
                        if kk == 0:
                            started(s + q, mm)
                return mm[2]
            def feature_blocks(n, names, tag, tokens, ready):
                for b, name in enumerate(names):
                    s = step_of(n) + 2 * b
                    job = plan[tag, name]
                    claim(pe, job)
                    T = tokens(name)
                    if name == "vg":
                        take(s + 1)
                        for t in range(4):
                            for k in range(KT):
                                mm = products(psum[:, job.bank, t * P:t * P + P],
                                              (feat_hi[:, k, t * P:t * P + P], feat_lo[:, k, t * P:t * P + P]),
                                              weights(s + k // 4, slice(k % 4 * P, k % 4 * P + P)),
                                              k == 0, k == KT - 1)
                                if t == 0 and k == 0:
                                    started(s, mm)
                        mm[1].then_inc(split_started, 1)
                        mm = mm[2]
                    else:
                        mm = block_products(s, psum[:, job.bank, 0:T], T, feat_lo, tag=None if b else ready)
                    mm.then_inc(bank_full[job.bank], 1)
            def transposes(tag, tiles, ready, base):
                pe.wait_ge(ready, base)
                for k in range(KT):
                    job = plan[(*tag, k)]
                    claim(pe, job)
                    for t in range(tiles):
                        mm = pe.transpose(psum[:, job.bank, t * P:t * P + P],
                                          xn[:, t, k * P:k * P + P], ident)
                    mm.then_inc(bank_full[job.bank], 1)
            def token_major(n, tag, tiles, kt, lhs):
                per = kt // 4
                for half in range(2):
                    for t in range(tiles):
                        claim(pe, plan[(*tag, half, t)])
                    for g in range(per):
                        w = tile(n + half * per + g)
                        for t in range(tiles):
                            job = plan[(*tag, half, t)]
                            for k in range(4):
                                mm = pe.matmul(psum[:, job.bank, :], lhs(4 * g + k, t),
                                               w[:, k * 512:k * 512 + 512],
                                               start=g == 0 and k == 0, stop=g == per - 1 and k == 3)
                                if t == 0 and k == 0:
                                    mm.then_inc(tiles_started, 1)
                            if g == per - 1:
                                mm.then_inc(bank_full[job.bank], 1)
            def split_token_major(n, tag, tiles, kt, lhs, ready=None):
                s = step_of(n)
                for half in range(2):
                    for t in range(tiles):
                        claim(pe, plan[(*tag, half, t)])
                    for k in range(kt):
                        take(s)
                        if ready and half == 0:
                            pe.wait_ge(relu_free, ready + k)
                        for t in range(tiles):
                            job = plan[(*tag, half, t)]
                            mm = products(psum[:, job.bank, :], lhs(k, t), weights(s, slice(0, 512)),
                                          k == 0, k == kt - 1)
                            if t == 0:
                                started(s, mm)
                            if k == kt - 1:
                                mm[2].then_inc(bank_full[job.bank], 1)
                        s += 1
            def attention(tag, items, S_mm, v_of, probs, probs_t, o_tok):
                n = len(items)
                for i in range(n + 5):
                    if i < n:
                        job = plan[tag, "S", i]
                        claim(pe, job)
                        S_mm(items[i], psum[:, job.bank, 0:items[i][4]]).then_inc(bank_full[job.bank], 1)
                    if 2 <= i < n + 2:
                        job = plan[tag, "T", i - 2]
                        claim(pe, job)
                        if tag == "fox":
                            freed(pe, plan[tag, "S", i - 2])
                        else:
                            pe.wait_ge(probs_ready, first_item(tag) + i - 1)
                        for k in range(items[i - 2][4] // P):
                            mm = pe.transpose(psum[:, job.bank, k * P:k * P + P],
                                              probs[:, (i - 2) % 3, k * P:k * P + P], ident)
                        mm.then_inc(bank_full[job.bank], 1)
                    if 3 <= i < n + 3:
                        branch, q, h, first, keys = items[i - 3]
                        job = plan[tag, "O", (i - 3) // HEADS]
                        if h == 0:
                            claim(pe, job)
                        freed(pe, plan[tag, "T", i - 3])
                        for k in range(keys // P):
                            p = probs_t[:, (i - 3) % 2, k * P:k * P + P]
                            v = v_of(branch, first // P + k, h)
                            if tag == "fox":
                                out, a, b = psum[:, job.bank, h * 64:h * 64 + 64], p, v
                                at = (0, 0)
                            else:
                                r = slice(64 * (h % 2), 64 * (h % 2) + 64)
                                out, a, b = psum[r, job.bank, h // 2 * P:h // 2 * P + P], v, p
                                at = (0, r.start)
                            mm = pe.matmul(out, a, b, start=k == 0, stop=k == keys // P - 1, tile_position=at)
                        if h == HEADS - 1:
                            mm.then_inc(bank_full[job.bank], 1)
                    if tag != "fox" and ada_sums_at(tag[0], i) is not None:
                        chunk, streams = ada_sums_at(tag[0], i), tiles_of(tag[0]) // 2
                        job = plan[tag, "ada", chunk]
                        claim(pe, job)
                        pe.wait_ge(ada_partial, ADA_LATER * tag[0] + chunk + 1)
                        for v in range(streams):
                            for b in range(4):
                                mm = pe.matmul(psum[:, job.bank, 4 * v + b:4 * v + b + 1],
                                               ada_sum[chunk % 2][:, v, b * P:b * P + P], ones[:, 0:1],
                                               start=True, stop=True)
                        mm.then_inc(bank_full[job.bank], 1)
                    if tag == "fox" and i >= HEADS + 4 and (i - HEADS - 4) % HEADS == 0:
                        t = (i - HEADS - 4) // HEADS
                        job = plan[tag, "OT", t]
                        claim(pe, job)
                        pe.wait_ge(b2["onorm"], t + 1)
                        for b in range(4):
                            mm = pe.transpose(psum[:, job.bank, b * P:b * P + P],
                                              o_tok[:, t % 2, b * P:b * P + P], ident)
                        mm.then_inc(bank_full[job.bank], 1)
            def one(job, lhs, rhs, n, wait=None):
                claim(pe, job)
                m = len(lhs)
                for i in range(m):
                    mm = pe.matmul(psum[:, job.bank, 0:n], lhs[i], rhs[i], start=i == 0, stop=i == m - 1)
                mm.then_inc(bank_full[job.bank], 1)
            def gain_rows_mm(l, w, order):
                for v in range(tiles_of(l) // 2):
                    pe.wait_ge(gain_diag, order + v + 1)
                    for half in range(2):
                        one(plan[l, "g", w, v, half], [ones], [diag[w][:, v, half * 512:half * 512 + 512]], 512)
            pe.wait_ge(consts_in, 32)
            gdiag = 0
            for l in range(DEPTH):
                L, n = l * LAYER_TILES, tiles_of(l)
                T = n * P
                if l == 0:
                    pe.wait_ge(silu_ready, 1)
                job = plan[l, "ada"]
                claim(pe, job)
                def ada_chunks(i, later):
                    for chunk in range(2):
                        rows = plan[l, "ada rows", chunk]
                        if later:
                            pe.wait_ge(bank_free[rows.bank], i + (rows.turn + 1))
                        else:
                            claim(pe, rows)
                        for half in range(2):
                            m = L + T_ADA + 2 * chunk + half
                            pe.wait_ge(tile_loaded[m % RING], 16 * i + 16 * (m // RING + 1 + later))
                            for k in range(4):
                                mm = pe.matmul(psum[0:2, rows.bank, :], silu_c[:, 4 * half + k],
                                               ring(m % RING)[:, k * 512:k * 512 + 512],
                                               start=half == 0 and k == 0, stop=half == 1 and k == 3)
                                if k == 0:
                                    mm.then_inc(tiles_started, 1)
                        mm.then_inc(bank_full[rows.bank], 1)
                    for chunk in range(2):
                        rows = plan[l, "ada rows", chunk]
                        pe.wait_ge(bank_free[rows.bank], i + (rows.turn + 1 + later))
                        for b in range(4):
                            pe.matmul(psum[:, job.bank, bass.ds(16 * i + (16 * later + 8 * chunk + 2 * b), 2)],
                                      ada_rows[0:2, chunk, b * P:b * P + P], ident[0:2, 0:2],
                                      start=True, stop=True)
                ada_chunks(0, 0)
                ada_chunks(0, 1)
                pe.transpose(psum[:, job.bank, 384:512], ident, ident).then_inc(bank_full[job.bank], 1)
                transposes((l, "h1"), 4, xn_ready, 4 + (0, 8)[l])
                feature_blocks(L + T_IN, IN_NAMES, l, lambda name: 512 if name[:2] in ("ck", "kr", "kg") else T,
                               (l, "h1"))
                pe.wait_ge(squares_ready, 7 * l + 1)
                claim(pe, plan[l, "ss", "ckv"])
                pe.matmul(psum[:, plan[l, "ss", "ckv"].bank, 0:2], ones, ones[:, 0:2], start=True, stop=True)\
                    .then_inc(split_started, 2)
                one(plan[l, "ss", "ckv"], [ones, ones], [tmp[:, 0], tmp[:, 1]], 512)
                pe.wait_ge(squares_ready, 7 * l + 2)
                one(plan[l, "ss", "cq"], [ones, ones], [tmp[:, 2, 0:T], tmp[:, 3, 0:T]], T)
                for s, name in enumerate(["kg"] + [f"qg{b}" for b in range(4)]):
                    pe.wait_ge(squares_ready, 7 * l + 3 + s)
                    one(plan[l, "ss", name], [bones], [probs_sq(s)[:, 0:512 if s == 0 else T]], 512 if s == 0 else T)
                with pe.Fori(0, GATE_BLOCKS // BANKS) as i:
                    for b in range(BANKS):
                        job = plan[l, "gate", b]
                        pe.wait_ge(bank_free[job.bank], i + job.turn)
                        block_products(step_of(L + T_GATE) + 2 * b, psum[:, job.bank, 0:T], T, feat_lo, i, 16)\
                            .then_inc(bank_full[job.bank], 1)
                base = 7 * l
                pe.wait_ge(normed, base + 7)
                one(plan[l, "rot", "kr"], [c("rot32")], [kr[:, 0:S]], S)
                one(plan[l, "rot", "kg"], [c("rot64")], [kg[:, 0:S]], S)
                for b in range(4):
                    one(plan[l, "rot", f"qg{b}"], [c("rot64")], [qg[:, b, 0:S]], S)
                w = tile(L + T_UP)
                for b in range(4):
                    job = plan[l, "kn", b]
                    claim(pe, job)
                    for k in range(2):
                        mm = pe.matmul(psum[:, job.bank, :], w[:, k * 512 + b * P:k * 512 + b * P + P],
                                       ckv[:, k], start=k == 0, stop=k == 1)
                        if b == 0 and k == 0:
                            mm.then_inc(tiles_started, 1)
                    mm.then_inc(bank_full[job.bank], 1)
                for t in range(4):
                    one(plan[l, "vm", t], [ckv[:, k, t * P:t * P + P] for k in range(2)],
                        [w[:, 1024 + k * 512:1536 + k * 512] for k in range(2)], 512)
                w = tile(L + T_UP + 1)
                for b in range(6):
                    job = plan[l, "qn", b] if b < 4 else plan[l, "qr", b - 4]
                    claim(pe, job)
                    for k in range(2):
                        mm = pe.matmul(psum[:, job.bank, 0:T], w[:, k * 768 + b * P:k * 768 + b * P + P],
                                       cq[:, k, 0:T], start=k == 0, stop=k == 1)
                        if b == 0 and k == 0:
                            mm.then_inc(tiles_started, 1)
                    mm.then_inc(bank_full[job.bank], 1)
                for s in range(n // 2):
                    for g in range(4):
                        job = plan[l, "dft1", s, g]
                        claim(pe, job)
                        for t in range(2):
                            mm = pe.matmul(psum[:, job.bank, t * S:t * S + S],
                                           f_in[:, g, (2 * s + t) * P:(2 * s + t + 1) * P], c("dft_d"),
                                           start=True, stop=True)
                        mm.then_inc(bank_full[job.bank], 1)
                    for g in range(4):
                        freed(pe, plan[l, "dft1", s, g])
                        one(plan[l, "dft2", s, g],
                            [dft_mid[:, g, t * S + h * P:t * S + h * P + P] for h in range(2) for t in range(2)],
                            [c("ndft_s" if h else "dft_s")[:, t * S:t * S + S] for h in range(2) for t in range(2)], S)
                for b in range(2):
                    freed(pe, plan[l, "qr", b])
                    one(plan[l, "rot", f"qr{b}"], [c("rot32")], [qr[:, b, 0:S]], S)
                def S_mm(item, o):
                    branch, q, h, first, keys = item
                    a = slice(first, first + keys)
                    t = slice(q * P, q * P + P)
                    if branch == "m":
                        r = slice(64 * (h % 2), 64 * (h % 2) + 64)
                        pe.matmul(o, qn[r, h // 2, t], kn[r, h // 2, a], start=True, stop=False)
                        r = slice(32 * (h % 4), 32 * (h % 4) + 32)
                        return pe.matmul(o, qr[r, h // 4, t], kr[r, a], start=False, stop=True,
                                         tile_position=(32 * (h % 4), 0))
                    r = slice(64 * (h // 4), 64 * (h // 4) + 64)
                    return pe.matmul(o, qg[r, h % 4, t], kg[r, a], start=True, stop=True)
                def v_of(branch, k, h):
                    if branch == "m":
                        return vm[:, k, h * 64:h * 64 + 64]
                    return vg[:, k, (h // 4) * 64:(h // 4) * 64 + 64]
                pe.wait_ge(roped, 8 * (l + 1))
                for b in range(4):
                    freed(pe, plan[l, "kn", b])
                    freed(pe, plan[l, "vm", b])
                    freed(pe, plan[l, "qn", b])
                attention((l, "att"), attention_items(l), S_mm, v_of, probs, probs_t, o_tok)
                for s in range(n // 2):
                    for g in range(4):
                        freed(pe, plan[l, "dft2", s, g])
                freed(pe, plan[(l, "att"), "O", 2 * n - 1])
                freed(pe, plan[(l, "att"), "O", 2 * n - 2])
                for b in range(KT):
                    w = tile(L + T_BR + b)
                    for r, src in enumerate((f_in, out_m, out_g)):
                        job = plan[l, "branch", b, r]
                        claim(pe, job)
                        for k in range(4):
                            mm = pe.matmul(psum[:, job.bank, 0:T], w[:, (4 * r + k) * P:(4 * r + k + 1) * P],
                                           src[:, k, 0:T], start=k == 0, stop=k == 3)
                            if r == 0 and k == 0:
                                mm.then_inc(tiles_started, 1)
                        mm.then_inc(bank_full[job.bank], 1)
                gain_rows_mm(l, 2, gdiag)
                gdiag += n // 2
                pe.wait_ge(mix_ready, KT * (l + 1))
                token_major(L + T_O, (l, "o", 0), n, KT, lambda k, t: feat[:, k, t * P:t * P + P])
                transposes((l, "h2"), n, xn_ready, (8, 14)[l])
                for k in range(KT):
                    freed(pe, plan[l, "h2", k])
                gain_rows_mm(l, 5, gdiag)
                gdiag += n // 2
                for part in range(2):
                    up = L + T_W1 + 2 * FF_TILES * part
                    with pe.Fori(0, FF_PART // BANKS) as i:
                        for b in range(BANKS):
                            job = plan[l, "ff", part * FF_PART + b]
                            pe.wait_ge(bank_free[job.bank], i + job.turn)
                            block_products(step_of(up) + 2 * b, psum[:, job.bank, 0:T], T, mlp_lo, i, 16)\
                                .then_inc(bank_full[job.bank], 1)
                    split_token_major(up + FF_TILES, (l, "mlp", part), n, FF_PART,
                                      lambda k, t: (ff_hi[:, k, t * P:t * P + P], ff_lo[:, k, t * P:t * P + P]),
                                      NFF * l + FF_PART * part + 3)
            transposes(("h3",), 2, xn_ready, 16)
            feature_blocks(T_IN2, IN2_NAMES, "b2", lambda name: S, ("h3",))
            for t in range(2):
                claim(pe, plan["b2", "v", t])
            for k in range(KT):
                s = step_of(T_V2) + k
                take(s)
                for t in range(2):
                    job = plan["b2", "v", t]
                    mm = products(psum[:, job.bank, :],
                                  (feat_hi[:, k, t * P:t * P + P], feat_lo[:, k, t * P:t * P + P]),
                                  weights(s, slice(0, 512)), k == 0, k == KT - 1)
                    if t == 0:
                        started(s, mm)
                    if k == KT - 1:
                        mm[2].then_inc(bank_full[job.bank], 1)
            pe.wait_ge(const2_in, 16)
            pe.wait_ge(b2["xc"], 1)
            for name, w in (("r", "wa"), ("i", "wx")):
                job = plan["lru", name]
                claim(pe, job)
                for b in range(2):
                    mm = pe.matmul(psum[:, job.bank, b * S:b * S + S], k2(w)[:, b * P:b * P + P], lru[0][:, b],
                                   start=True, stop=True)
                mm.then_inc(bank_full[job.bank], 1)
            pe.wait_ge(b2["lora"], 2)
            for name, r in (("w", slice(0, 32)), ("a", slice(32, 64)), ("g", slice(64, 128))):
                job = plan["rwkv", name]
                claim(pe, job)
                for b in range(2):
                    mm = pe.matmul(psum[:, job.bank, b * S:b * S + S], k2("lora", r)[:, b * P:b * P + P],
                                   pm[r, 6], start=True, stop=True, tile_position=(r.start, 0))
                mm.then_inc(bank_full[job.bank], 1)
            for s in range(8):
                pe.wait_ge(b2["sq_in"], s + 1)
                one(plan["ss", ("q%d" % s) if s < 4 else "k%d" % (s - 4)], [bones], [sq2(s)], S)
            pe.wait_ge(b2["kk_sq"], 1)
            one(plan["rwkv", "kk"], [bones], [rw2("t")], 512)
            def S_fox(item, o):
                _, q, h, first, keys = item
                r = slice(64 * (h % 2), 64 * (h % 2) + 64)
                t = slice(q * P, q * P + P)
                sel = ident[0:HEADS, h:h + 1]
                pe.matmul(o, f2[r, 4 + h // 2, t], f2[r, 8 + h // 2, 0:keys], start=True, stop=False)
                pe.matmul(o, cum[0:HEADS, t], sel.to_broadcast([HEADS, keys]), start=False, stop=False)
                pe.matmul(o[:, keys - P:keys], ident, k2("causal"), start=False, stop=False,
                          skip_group_check=True)
                return pe.matmul(o, sel.to_broadcast([HEADS, P]), ncum[0:HEADS, 0:keys], start=False,
                                 stop=True)
            pe.wait_ge(b2["qk"], 8)
            pe.wait_ge(b2["cum"], 2)
            for t in range(2):
                freed(pe, plan["b2", "v", t])
            attention("fox", FOX_ITEMS, S_fox, lambda branch, k, h: v2[:, k, h * 64:h * 64 + 64],
                      probs2, probs_t2, o_tok2)
            pe.wait_ge(b2["bonus_in"], 1)
            one(plan["rwkv", "bonus"], [bones], [rw2("t")], 512)
            pe.wait_ge(b2["y_sq"], 1)
            one(plan["lru", "ss"], [ones, ones], [lru[2][:, 0], lru[2][:, 1]], S)
            pe.wait_ge(b2["BK"], 1)
            for name, src in (("Btok", Bm), ("Ktok", Km), ("Vtok", pm[:, 4:6])):
                job = plan["rwkv", name]
                claim(pe, job)
                for t in range(2):
                    for b in range(2):
                        mm = pe.transpose(psum[:, job.bank, t * S + b * P:t * S + b * P + P],
                                          src[:, b, t * P:t * P + P], ident)
                mm.then_inc(bank_full[job.bank], 1)
            for name, src in (("BR", Bm), ("KR", Km)):
                for m in range(4):
                    job = plan["rwkv", name, m]
                    claim(pe, job)
                    t, odd = m // 2, m % 2
                    r = slice(64 * odd, 64 * odd + 64)
                    for j in range(2):
                        h = odd + 2 * j
                        mm = pe.matmul(psum[:, job.bank, j * S:j * S + S], src[r, h // 2, t * P:t * P + P],
                                       AR[r, h // 2, :, t * P:t * P + P], start=True, stop=True)
                    mm.then_inc(bank_full[job.bank], 1)
            for m in range(4):
                freed(pe, plan["rwkv", "KR", m])
            for name in ("Btok", "Ktok", "Vtok"):
                freed(pe, plan["rwkv", name])
            job = plan["rwkv", "MV"]
            claim(pe, job)
            for m in range(8):
                mm = pe.matmul(psum[:, job.bank, m * 64:m * 64 + 64], KR[:, m, 0:P],
                               Vtok[:, m // 4, (m % 4) * 64:(m % 4) * 64 + 64], start=True, stop=True)
            mm.then_inc(bank_full[job.bank], 1)
            pe.wait_ge(b2["inv0"], 2)
            for j in range(6):
                pe.wait_ge(b2["lev"], j + 1)
                for half in range(2):
                    job = plan["rwkv", "T1", j, half]
                    claim(pe, job)
                    if j:
                        freed(pe, plan["rwkv", "X", j - 1, half])
                    for m in range(4 * half, 4 * half + 4):
                        mm = pe.matmul(psum[:, job.bank, (m % 4) * P:(m % 4) * P + P], level_l[j % 2][:, m],
                                       inv_x[:, m], start=True, stop=True)
                    mm.then_inc(bank_full[job.bank], 1)
                for what in ("X", "XT"):
                    if what == "X" and j == 5:
                        continue
                    for half in range(2):
                        freed(pe, plan["rwkv", "T1", j, half])
                        job = plan["rwkv", what, j, half]
                        claim(pe, job)
                        if j:
                            freed(pe, plan["rwkv", "XT", j - 1, half])
                        for m in range(4 * half, 4 * half + 4):
                            a, b = (inv_t1, inv_xt) if what == "XT" else (inv_xt, inv_t1)
                            mm = pe.matmul(psum[:, job.bank, (m % 4) * P:(m % 4) * P + P], a[:, m], b[:, m],
                                           start=True, stop=True)
                        mm.then_inc(bank_full[job.bank], 1)
            for half in range(2):
                freed(pe, plan["rwkv", "XT", 5, half])
            for x in range(4):
                claim(pe, plan["rwkv", "O", x])
            for cc in range(4):
                t, r = cc // 2, slice(64 * (cc % 2), 64 * (cc % 2) + 64)
                old = state[cc % 2]
                if cc:
                    pe.wait_ge(b2["ST"], cc)
                    for h in (0, 2, 1, 3):
                        job = plan["rwkv", "U", cc, h % 2]
                        if h < 2:
                            claim(pe, job)
                        rh = slice(64 * (h % 2), 64 * (h % 2) + 64)
                        mm = pe.matmul(psum[r, job.bank, h * 64:h * 64 + 64],
                                       AR[rh, h // 2, 0, cc * 64:cc * 64 + 64], old[rh, h // 2],
                                       start=True, stop=True, tile_position=(rh.start, r.start))
                        if h >= 2:
                            mm.then_inc(bank_full[job.bank], 1)
                pe.wait_ge(b2["U"], cc + 1)
                job = plan["rwkv", "SA", cc]
                claim(pe, job)
                for h in range(4):
                    mm = pe.matmul(psum[r, job.bank, h * 64:h * 64 + 64], inv_xt[r, 4 * t + h, r],
                                   U_sb[r, 0, h * 64:h * 64 + 64], start=True, stop=True,
                                   tile_position=(r.start, r.start))
                mm.then_inc(bank_full[job.bank], 1)
                freed(pe, job)
                if cc < 3:
                    job = plan["rwkv", "ST", cc]
                    claim(pe, job)
                    for h in range(4):
                        rh = slice(64 * (h % 2), 64 * (h % 2) + 64)
                        o = psum[rh, job.bank, (h // 2) * 64:(h // 2) * 64 + 64]
                        hc = slice(h * 64, h * 64 + 64)
                        pe.matmul(o, Btok[r, t, hc], SA_sb[r, 0, hc], start=True, stop=False,
                                  tile_position=(r.start, rh.start))
                        mm = pe.matmul(o, Ktok[r, t, hc], Vtok[r, t, hc], start=False, stop=True,
                                       tile_position=(r.start, rh.start))
                    mm.then_inc(bank_full[job.bank], 1)
                for h in range(4):
                    rh = slice(64 * (h % 2), 64 * (h % 2) + 64)
                    hc, m = slice(h * 64, h * 64 + 64), 4 * t + h
                    at = (h // 2) * S + cc * 64
                    inner, outer = plan["rwkv", "O", cc % 2], plan["rwkv", "O", 2 + h % 2]
                    o = psum[rh, inner.bank, at:at + 64]
                    tr = slice(P + r.start, P + r.stop)
                    pe.matmul(o, Vtok[r, t, hc], KR[r, m, tr], start=True, stop=False,
                              tile_position=(r.start, rh.start))
                    mm = pe.matmul(o, SA_sb[r, 0, hc], BR[r, m, tr], start=False, stop=True,
                                   tile_position=(r.start, rh.start))
                    if cc >= 2 and h == 3:
                        mm.then_inc(bank_full[inner.bank], 1)
                    if cc:
                        mm = pe.matmul(psum[rh, outer.bank, at:at + 64], old[rh, h // 2],
                                       AR[rh, h // 2, 1, cc * 64:cc * 64 + 64],
                                       start=True, stop=True, tile_position=(rh.start, rh.start))
                        if cc == 3 and h >= 2:
                            mm.then_inc(bank_full[outer.bank], 1)
            pe.wait_ge(b2["o_sb"], 1)
            one(plan["rwkv", "mean"], [bones], [rw2("cl")], 512)
            pe.wait_ge(b2["o_sq"], 1)
            one(plan["rwkv", "var"], [bones], [rw2("t")], 512)
            pe.wait_ge(b2["y_done"], 1)
            for t in range(2):
                freed(pe, plan["fox", "OT", t])
            token_major(T_OUT2, ("out2",), 2, KT, lambda k, t: y_t[:, k, t * P:t * P + P])
            transposes(("h4",), 2, xn_ready, 18)
            for k in range(KT):
                freed(pe, plan["h4", k])
            job = plan["route",]
            claim(pe, job)
            for t in range(2):
                for k in range(KT):
                    for part in (feat_hi, feat_lo):
                        mm = pe.matmul(psum[:, job.bank, t * 32:t * 32 + 20],
                                       part[:, k, t * P:t * P + P].bitcast(F32),
                                       k2("w_route")[:, k * 20:k * 20 + 20], start=k == 0 and part is feat_hi,
                                       stop=k == KT - 1 and part is feat_lo)
            mm.then_inc(bank_full[job.bank], 1)
            def gate_up(s, e, turn, i=0, per=0):
                for name in ("gate2", "up2"):
                    job = plan[name, e]
                    turn(job)
                    for b in range(2):
                        mm = block_products(s, psum[:, job.bank, b * S:b * S + S], S, feat_lo, i, per)
                        s += 2
                    mm.then_inc(bank_full[job.bank], 1)
            def down(s, e, ready, last=False, i=0, per=0):
                pe.wait_ge(b2["hid"], ready)
                for b in range(2):
                    for half in range(2):
                        take(s, i, per)
                        for t in range(2):
                            at = slice(b * S + t * P, b * S + t * P + P)
                            mm = [pe.matmul(psum[:, plan["moe", half, t].bank, :], x, w, start=False,
                                            stop=last and b == 1 and lo == 2, skip_group_check=not last)
                                  for lo, (x, w) in enumerate((
                                      (hid_hi[:, e % 2, at], weights(s, slice(0, 512))[0]),
                                      (hid_hi[:, e % 2, at], weights(s, slice(0, 512))[1]),
                                      (hid_lo[:, e % 2, at], weights(s, slice(0, 512))[0])))]
                            if t == 0:
                                started(s, mm)
                        s += 1
                return mm[2]
            m0 = step_of(T_MOE)
            gate_up(m0, 0, lambda job: claim(pe, job))
            job = plan["combT",]
            claim(pe, job)
            pe.wait_ge(b2["comb"], 1)
            for t in range(2):
                mm = pe.transpose(psum[0:N_EXPERTS, job.bank, t * P:t * P + P],
                                  comb16[:, t], ident)
            mm.then_inc(bank_full[job.bank], 1)
            freed(pe, job)
            for e in range(8):
                job = plan["comb", e]
                claim(pe, job)
                for j in range(2):
                    mm = pe.matmul(psum[:, job.bank, j * S:j * S + S],
                                   ident[0:N_EXPERTS, 2 * e + j:2 * e + j + 1].to_broadcast([N_EXPERTS, P]),
                                   combT[0:N_EXPERTS, :], start=True, stop=True)
                mm.then_inc(bank_full[job.bank], 1)
            for half in range(2):
                for t in range(2):
                    job = plan["moe", half, t]
                    claim(pe, job)
                    pe.matmul(psum[:, job.bank, :], ident, resid[:, t, half * 512:half * 512 + 512],
                              start=True, stop=False)
            with pe.Fori(0, 3) as i:
                for j in range(4):
                    s = m0 + 8 + 12 * j
                    gate_up(s, j + 1, lambda job: pe.wait_ge(bank_free[job.bank], 2 * i + job.turn), i, 48)
                    down(s + 8, j, 4 * i + (j + 1), i=i, per=48)
            for e in range(12, 16):
                s = m0 + 8 + 12 * e
                if e < 15:
                    gate_up(s, e + 1, lambda job: claim(pe, job))
                    s += 8
                mm = down(s, e, e + 1, e == N_EXPERTS - 1)
            mm.then_inc(bank_full[plan["moe", 1, 1].bank], 1)
        @block.vector
        def _(dve):
            count = {"post": 0, "pre": 0, "rows": 0, "items": 0, "feat": 0}
            def low_part(s, i=0, per=0):
                m, q = tile_of(s)
                dve.wait_ge(split_high, per * i + (s + 1))
                dve.tensor_tensor(w_lo[:, s % SPLIT_BUFFERS], ring(m % RING)[:, q * 512:q * 512 + 512],
                                  w_hi[:, s % SPLIT_BUFFERS].bitcast(F32), ALU.subtract).then_inc(split_low, 1)
            split = Split(low_part)
            def stats(t, at):
                for half in range(2):
                    dve.bn_stats(stat[:, t * 12 + half * 6:t * 12 + half * 6 + 6],
                                 resid[:, t, half * 512:half * 512 + 512])
                dve.drain()
                return dve.bn_aggr(stat[:, 48 + 2 * t:50 + 2 * t], stat[:, t * 12:t * 12 + 12])
            def layer_norm_rows(tiles):
                base = count["post"]
                for t in range(tiles):
                    stats(t, base).then_inc(post_stats, 1)
                dve.wait_ge(rows_in, 16 * (count["rows"] + 1))
                for t in range(tiles):
                    dve.wait_ge(post_rstd, base + t + 1)
                    dve.scalar_tensor_tensor(resid[:, t], resid[:, t], stat[:, 48 + 2 * t:49 + 2 * t],
                                             lnr[:, 0], ALU.subtract, ALU.mult)
                    dve.drain()
                    ins = dve.scalar_tensor_tensor(resid[:, t], resid[:, t], stat[:, 56 + t:57 + t],
                                                   lnr[:, 1], ALU.mult, ALU.add)
                    if t == tiles - 1:
                        ins.then_inc(rows_used, 1)
                    dve.drain()
                count["post"] += tiles
                count["rows"] += 1
            def norm_tokens(tiles):
                base = count["pre"]
                for t in range(tiles):
                    stats(t, base).then_inc(stats_ready, 1)
                for t in range(tiles):
                    dve.wait_ge(rstd_ready, base + t + 1)
                    dve.tensor_scalar(xn[:, t], resid[:, t], stat[:, 48 + 2 * t:49 + 2 * t],
                                      stat[:, 56 + t:57 + t], ALU.subtract, ALU.mult).then_inc(xn_ready, 1)
                count["pre"] += tiles
            def rms_tokens():
                base = count["pre"]
                for t in range(2):
                    dve.wait_ge(rstd_ready, base + t + 1)
                    dve.tensor_scalar(xn[:, t], resid[:, t], stat[:, 56 + t:57 + t], None,
                                      ALU.mult).then_inc(xn_ready, 1)
                count["pre"] += 2
            def features(tag, of, low, width):
                for k in range(KT + 1):
                    if k < KT:
                        job = plan[(*tag, k)]
                        full(dve, job)
                        dve.drain()
                        of(exact[k % 2], job, k).then_inc(feat_exact, 1)
                    if k:
                        dve.wait_ge(feat_high, count["feat"] + k)
                        dve.tensor_tensor(low[:, k - 1, 0:width], exact[(k - 1) % 2][:, 0:width],
                                          feat_hi[:, k - 1, 0:width].bitcast(F32), ALU.subtract)\
                            .then_inc(bank_free[plan[(*tag, k - 1)].bank], 1)
                count["feat"] += KT
            def modulated(tag, tiles, shift, scale, low):
                def of(x, job, k):
                    for v in range(tiles // 2):
                        ins = dve.tensor_scalar(x[:, v * S:v * S + S], psum[:, job.bank, v * S:v * S + S],
                                                mod[:, scale * KT + k, v:v + 1], mod[:, shift * KT + k, v:v + 1],
                                                ALU.mult, ALU.add)
                    return ins
                features(tag, of, low, tiles * P)
            def rope(job, x, cos, sin, s):
                t = tmp[:, s % 4, 0:S]
                full(dve, job)
                dve.tensor_tensor(t, psum[:, job.bank, 0:S], c(sin), ALU.mult).then_inc(bank_free[job.bank], 1)
                dve.tensor_tensor(x[:, 0:S], x[:, 0:S], c(cos), ALU.mult)
                dve.drain()
                dve.tensor_tensor(x[:, 0:S], x[:, 0:S], t, ALU.add).then_inc(roped, 1)
            def residual(tag, half, tiles, scale=ALPHA):
                for t in range(tiles):
                    job = plan[(*tag, half, t)]
                    hs = slice(half * 512, half * 512 + 512)
                    full(dve, job)
                    dve.tensor_tensor(exact[t % 2], psum[:, job.bank, :], gain_rows[:, t // 2, hs],
                                      ALU.mult).then_inc(bank_free[job.bank], 1)
                    dve.drain()
                    dve.scalar_tensor_tensor(resid[:, t, hs], resid[:, t, hs], scale, exact[t % 2],
                                             ALU.mult, ALU.add)
                dve.drain()
            def one_plus(j):
                dve.tensor_scalar(mod[:, j * KT:(j + 1) * KT], mod[:, j * KT:(j + 1) * KT], 1.0, None, ALU.add)
            def ada_part(l, k):
                chunk, kk = divmod(k, KT)
                m = l * LAYER_TILES + T_ADA_LATER + k // 4
                w = ring(m % RING)[:, k % 4 * 512:k % 4 * 512 + 512]
                if k % 4 == 0:
                    dve.wait_ge(tile_loaded[m % RING], 16 * (m // RING + 1))
                for v in range(tiles_of(l) // 2):
                    a = ada_sum[chunk % 2][:, v]
                    if kk:
                        ins = dve.scalar_tensor_tensor(a, w, silu_c[:, kk, v:v + 1], a, ALU.mult, ALU.add)
                    else:
                        ins = dve.tensor_scalar(a, w, silu_c[:, kk, v:v + 1], None, ALU.mult)
                    if k % 4 == 0 and v == 0:
                        ins.then_inc(tiles_started, 1)
                if kk == KT - 1:
                    ins.then_inc(ada_partial, 1)
            def ada_columns(l, chunk, job):
                at, streams = 2 * KT + 4 * chunk, tiles_of(l) // 2
                full(dve, job)
                dve.tensor_tensor(mod[:, at:at + 4, 0:streams],
                                  psum[:, job.bank, 0:4 * streams].rearrange("p (v j) -> p j v", v=streams),
                                  cols(f"b_ada{l}", at, 4).unsqueeze(2).to_broadcast([P, 4, streams]),
                                  ALU.add).then_inc(bank_free[job.bank], 1)
            def gain_diagonals(l, w):
                for v in range(tiles_of(l) // 2):
                    dve.tensor_tensor(diag[w][:, v].rearrange("p (k f) -> p k f", f=P),
                                      ident.unsqueeze(1).to_broadcast([P, KT, P]),
                                      mod[:, w * KT:(w + 1) * KT, v:v + 1].to_broadcast([P, KT, P]),
                                      ALU.mult).then_inc(gain_diag, 1)
            def attention(tag, items, scale, probs_t, o_tok):
                n, base = len(items), count["items"]
                for i in range(n + 5):
                    if i < n:
                        job, m = plan[tag, "S", i], 64 + i
                        full(dve, job)
                        dve.reduce_max(stat[:, 208 + i % 2:209 + i % 2], psum[:, job.bank, 0:items[i][4]], AX.X)
                        dve.drain()
                        dve.tensor_scalar(stat[:, m:m + 1], stat[:, 208 + i % 2:209 + i % 2],
                                          -scale(items[i]), None, ALU.mult).then_inc(neg_max, 1)
                    if tag != "fox" and ada_sums_at(tag[0], i - 1) is not None:
                        chunk = ada_sums_at(tag[0], i - 1)
                        ada_columns(tag[0], chunk, plan[tag, "ada", chunk])
                    if 2 <= i < n + 2 and copied_by_dve(tag, i - 2):
                        job = plan[tag, "T", i - 2]
                        full(dve, job)
                        keys = items[i - 2][4]
                        dve.tensor_copy(probs_t[:, i % 2, 0:keys], psum[:, job.bank, 0:keys])\
                            .then_inc(bank_free[job.bank], 1)
                    if tag != "fox" and 1 <= i <= n:
                        freed(dve, plan[tag, "S", i - 1])
                        dve.reciprocal(stat[:, 192 + (i - 1) % 8:193 + (i - 1) % 8],
                                       stat[:, 127 + i:128 + i]).then_inc(sum_inverse, 1)
                    if tag != "fox" and i < n:
                        a, z = ada_parts(tag[0])[i]
                        for k in range(a, z):
                            if k > a:
                                dve.drain()
                            ada_part(tag[0], k)
                    if tag == "fox" and i >= HEADS + 3 and (i - HEADS - 3) % HEADS == 0:
                        t = (i - HEADS - 3) // HEADS
                        dve.wait_ge(b2["fox_rstd"], t + 1)
                        dve.tensor_scalar(o_tok[:, t % 2], o_tok[:, t % 2], stat[:, 212 + t:213 + t], None,
                                          ALU.mult).then_inc(b2["onorm"], 1)
                    if tag == "fox" and i >= HEADS + 2 and (i - HEADS - 2) % HEADS == 0:
                        t = (i - HEADS - 2) // HEADS
                        job, r = plan[tag, "O", t], 192 + 8 * (t % 2)
                        freed(dve, plan[tag, "S", HEADS * t + HEADS - 1])
                        dve.reciprocal(stat[:, r:r + HEADS], stat[:, 128 + HEADS * t:128 + HEADS * t + HEADS])
                        full(dve, job)
                        dve.drain()
                        dve.tensor_tensor(o_tok[:, t % 2].rearrange("p (h v) -> p h v", v=64),
                                          psum[:, job.bank, :].rearrange("p (h v) -> p h v", v=64),
                                          stat[:, r:r + HEADS].unsqueeze(2).to_broadcast([P, HEADS, 64]),
                                          ALU.mult).then_inc(bank_free[job.bank], 1)
                count["items"] += n
            dve.wait_ge(consts_in, 32)
            dve.wait_ge(silu_exp, 1)
            cc16 = col[:, COL["c"][0]:COL["c"][0] + 16]
            dve.tensor_scalar(stat[:, 16:32], stat[:, 0:16], 1.0, None, ALU.add)
            dve.drain()
            dve.reciprocal(stat[:, 32:48], stat[:, 16:32])
            dve.drain()
            dve.tensor_tensor(silu_c.rearrange("p k v -> p v k"), cc16.rearrange("p (v k) -> p v k", v=2),
                              stat[:, 32:48].rearrange("p (v k) -> p v k", v=2), ALU.mult).then_inc(silu_ready, 1)
            dve.nop().then_inc(relu_free, 2)
            dve.wait_ge(x_in, 32)
            for l in range(DEPTH):
                L, n = l * LAYER_TILES, tiles_of(l)
                T = n * P
                norm_tokens(4)
                s_in, s_gate, s_up = (step_of(L + x) for x in (T_IN, T_GATE, T_W1))
                split.until(s_in + AHEAD, s_in)
                job = plan[l, "ada"]
                full(dve, job)
                dve.tensor_tensor(mod[:, 0:2 * KT], psum[:, job.bank, 0:4 * KT].rearrange("p (j v) -> p j v", v=2),
                                  cols(f"b_ada{l}", 0, 2 * KT).unsqueeze(2).to_broadcast([P, 2 * KT, 2]),
                                  ALU.add).then_inc(bank_free[job.bank], 1)
                dve.drain()
                one_plus(1)
                dve.drain()
                modulated((l, "h1"), 4, 0, 1, feat_lo)
                for name, to in (("ckv0", ckv[:, 0]), ("ckv1", ckv[:, 1]), ("kr", kr), ("kg", kg),
                                 ("cq0", cq[:, 0]), ("cq1", cq[:, 1]), ("qg0", qg[:, 0]),
                                 ("qg1", qg[:, 1]), ("qg2", qg[:, 2]), ("qg3", qg[:, 3])):
                    job, w = plan[l, name], T if "q" in name else 512
                    split.until(s_in + 2 * IN_NAMES.index(name) + 2 + AHEAD, s_in)
                    full(dve, job)
                    dve.tensor_copy(to[:, 0:w], psum[:, job.bank, 0:w]).then_inc(bank_free[job.bank], 1)
                dve.drain()
                r = 7 * l
                for s, (rows, group) in enumerate([
                        (tmp[:, 0], [(ckv[:, i], f"mla_kv_g{l}", i, 512) for i in range(2)]),
                        (tmp[:, 2], [(cq[:, i], f"mla_q_g{l}", i, T) for i in range(2)]),
                        (probs_sq(0), [(kg, f"gqa_k_g{l}", 0, 512)])]
                        + [(probs_sq(1 + b), [(qg[:, b], f"gqa_q_g{l}", 0, T)]) for b in range(4)]):
                    split.until(s_gate + 1 + 2 * s, s_in)
                    dve.wait_ge(rstd_rows_ready, r + s + 1)
                    for a, gain, i, w in group:
                        ins = dve.scalar_tensor_tensor(a[:, 0:w], a[:, 0:w], cols(gain, i), rows[:, 0:w],
                                                       ALU.mult, ALU.mult)
                    ins.then_inc(normed, 1)
                split.until(s_gate + 16, s_in)
                with dve.Fori(0, GATE_BLOCKS // BANKS - 1) as i:
                    for j in range(16):
                        low_part(s_gate + 16 + j, i, 16)
                split.next = s_gate + 2 * GATE_BLOCKS
                dve.drain()
                rope(plan[l, "rot", "kr"], kr, "cos32", "sin32", 0)
                rope(plan[l, "rot", "kg"], kg, "cos64", "sin64", 1)
                for b in range(4):
                    rope(plan[l, "rot", f"qg{b}"], qg[:, b], "cos64", "sin64", 2 + b)
                for t in range(4):
                    job = plan[l, "vm", t]
                    full(dve, job)
                    dve.tensor_copy(vm[:, t], psum[:, job.bank, :]).then_inc(bank_free[job.bank], 1)
                for s in range(n // 2):
                    for g in range(4):
                        job = plan[l, "dft2", s, g]
                        full(dve, job)
                        dve.tensor_copy(f_in[:, g, s * S:s * S + S], psum[:, job.bank, 0:S])\
                            .then_inc(bank_free[job.bank], 1)
                dve.drain()
                for b in range(2):
                    freed(dve, plan[l, "qr", b])
                    rope(plan[l, "rot", f"qr{b}"], qr[:, b], "cos32", "sin32", b)
                attention((l, "att"), attention_items(l), lambda it: SCALE_M if it[0] == "m" else SCALE_G,
                          probs_t, o_tok)
                dve.drain()
                one_plus(4)
                for b in range(KT):
                    for r in range(3):
                        job, g = plan[l, "branch", b, r], gates[:, r * KT + b, 0:T]
                        full(dve, job)
                        freed(dve, plan[l, "gate", r * KT + b])
                        dve.tensor_tensor(g, psum[:, job.bank, 0:T], g, ALU.mult)\
                            .then_inc(bank_free[job.bank], 1)
                gain_diagonals(l, 2)
                for v in range(n // 2):
                    for half in range(2):
                        freed(dve, plan[l, "g", 2, v, half])
                for half in range(2):
                    residual((l, "o", 0), half, n)
                layer_norm_rows(n)
                norm_tokens(n)
                split.until(s_up + AHEAD, s_up)
                modulated((l, "h2"), n, 3, 4, mlp_lo)
                gain_diagonals(l, 5)
                for part in range(2):
                    s = s_up + 4 * 2 * FF_TILES * part
                    with dve.Fori(0, FF_PART // BANKS) as i:
                        for b in range(BANKS):
                            low_part(s + 2 * b + AHEAD, i, 16)
                            low_part(s + 2 * b + 1 + AHEAD, i, 16)
                            h, r = exact[b % 2][:, 0:T], relu[b % 2][:, 0:T]
                            done = NFF * l + FF_PART * part + b + 1
                            job = plan[l, "ff", part * FF_PART + b]
                            dve.wait_ge(bank_free[job.bank], i + (job.turn + 1))
                            dve.tensor_tensor(h, r, r, ALU.mult)
                            dve.drain()
                            dve.wait_ge(hidden_high, 8 * i + done)
                            dve.tensor_tensor(big_r[:, bass.ds(4096 * i + 512 * (FF_PART + b), T)], h,
                                              big_r[:, bass.ds(4096 * i + 512 * b, T)].bitcast(F32),
                                              ALU.subtract).then_inc(relu_free, 1)
                    split.next = s + 2 * FF_PART + AHEAD
                    if part == 0:
                        for v in range(n // 2):
                            for half in range(2):
                                freed(dve, plan[l, "g", 5, v, half])
                    for half in range(2):
                        split.until(s + 2 * FF_PART + FF_PART * (half + 1) + AHEAD, s)
                        residual((l, "mlp", part), half, n, 1.0 if part else ALPHA)
                layer_norm_rows(n)
                if l == DEPTH - 1:
                    dve.nop().then_inc(resid_ready, 1)
            rms_tokens()
            def gained(tag, name):
                features((tag,), lambda x, job, k: dve.tensor_scalar(
                    x[:, 0:S], psum[:, job.bank, 0:S], cols(name, k), None, ALU.mult), feat_lo, S)
            s_in = step_of(T_IN2)
            gained("h3", "norm1_g")
            for b in range(0, 20, 2):
                job = plan["b2", IN2_NAMES[b]]
                split.until(s_in + 2 * b + 4 + AHEAD, s_in)
                full(dve, job)
                dve.tensor_copy(f2[:, b], psum[:, job.bank, 0:S]).then_inc(bank_free[job.bank], 1)
            split.until(s_in + 48, s_in)
            for t in range(2):
                job = plan["b2", "v", t]
                full(dve, job)
                dve.tensor_copy(v2[:, t], psum[:, job.bank, :]).then_inc(bank_free[job.bank], 1)
            for b in range(1, 20, 2):
                freed(dve, plan["b2", IN2_NAMES[b]])
            dve.wait_ge(const2_in, 16)
            dve.drain()
            for b in range(2):
                dve.tensor_scalar(lru[0][:, b], f2[:, b], cols("conv_w", 4 * b + 3), cols("conv_b", b),
                                  ALU.mult, ALU.add)
            for j in (2, 1, 0):
                dve.drain()
                d = 3 - j
                for b in range(2):
                    ins = dve.scalar_tensor_tensor(lru[0][:, b, d:], f2[:, b, 0:S - d],
                                                   cols("conv_w", 4 * b + j), lru[0][:, b, d:],
                                                   ALU.mult, ALU.add)
            ins.then_inc(b2["xc"], 1)
            pc = f2[:, 12:19]
            dve.tensor_tensor(pm[:, :, 1:], pc[:, :, 0:S - 1], pc[:, :, 1:], ALU.subtract)
            dve.tensor_scalar(pm[:, :, 0:1], pc[:, :, 0:1], -1.0, None, ALU.mult)
            dve.drain()
            for b in range(7):
                ins = dve.scalar_tensor_tensor(pm[:, b], pm[:, b], cols("mu", b), pc[:, b], ALU.mult, ALU.add)
            ins.then_inc(b2["mixed"], 1)
            ga, gx = f2[:, 2:4], rw["Wi"]
            dve.tensor_tensor(gx, ga, ga, ALU.mult)
            dve.drain()
            dve.tensor_scalar(gx, gx, 0.044715, 1.0, ALU.mult, ALU.add)
            dve.drain()
            dve.tensor_tensor(gx, gx, ga, ALU.mult).then_inc(b2["gelu_arg"], 1)
            H = slice(0, HEADS)
            dve.tensor_scalar(gq8, cols("fox_q_g"), SCALE_G, None, ALU.mult)
            dve.tensor_scalar(cum[H], f2[H, 19], cols("fox_fb")[H], 0.0, ALU.add, ALU.min).then_inc(b2["z"], 1)
            dve.memset(rw["W"][H, 0], 1.0)
            dve.wait_ge(b2["log_f"], 1)
            dve.drain()
            dve.tensor_tensor(ncum[H], cum[H], f2[H, 19], ALU.subtract)
            dve.drain()
            dve.tensor_tensor_scan(cum[H], rw["W"][H, 0], ncum[H], 0.0, ALU.mult, ALU.add).then_inc(b2["cum"], 1)
            dve.drain()
            dve.tensor_scalar(ncum[H], cum[H], -1.0, None, ALU.mult).then_inc(b2["cum"], 1)
            for b in range(2):
                dve.tensor_scalar(rw["kk"][:, b], pm[:, 2 + b], cols("k_k", b), None, ALU.mult)
            dve.drain()
            dve.tensor_tensor(rw["t"], rw["kk"], rw["kk"], ALU.mult).then_inc(b2["kk_sq"], 1)
            dve.wait_ge(b2["spl"], 1)
            dve.tensor_scalar(m8, stat[:, 220:222], -8.0, None, ALU.mult)
            dve.drain()
            freed(dve, plan["lru", "r"])
            for b in range(2):
                ins = dve.tensor_scalar(lru[1][:, b], lru[1][:, b], m8[:, b:b + 1], None, ALU.mult)
            ins.then_inc(b2["log_a"], 1)
            freed(dve, plan["lru", "i"])
            dve.tensor_tensor(lru[2], lru[2], lru[0], ALU.mult).then_inc(b2["lru_b"], 1)
            freed(dve, plan["rwkv", "w"])
            dve.tensor_scalar(rw["ld"], rw["ld"], -float(np.exp(-0.5)), None, ALU.mult)
            dve.drain()
            for b in range(2):
                dve.tensor_tensor_scan(rw["cl"][:, b], k2("reset"), rw["ld"][:, b], 0.0, ALU.mult, ALU.add)
            dve.drain()
            dve.tensor_tensor(rw["ld"], rw["cl"], rw["ld"], ALU.subtract).then_inc(b2["cl"], 1)
            freed(dve, plan["rwkv", "a"])
            A, R = AR[:, :, 0], AR[:, :, 1]
            for b in range(2):
                dve.tensor_scalar(A[:, b], rw["a"][:, b], -1.0, cols("k_a", b), ALU.add, ALU.mult)
            dve.drain()
            dve.scalar_tensor_tensor(Km, A, 1.0, pm[:, 2:4], ALU.add, ALU.mult)
            dve.wait_ge(b2["gelu"], 1)
            dve.scalar_tensor_tensor(ga, gx, 1.0, ga, ALU.add, ALU.mult)
            dve.wait_ge(b2["tanh_a"], 1)
            u = f2[:, 0:2]
            dve.tensor_scalar(u, u, 2.0 ** -62, None, ALU.max).then_inc(b2["sqrt_b"], 1)
            for s in range(8):
                a = f2[:, 4 + s]
                dve.wait_ge(b2["rsq"], s + 1)
                dve.scalar_tensor_tensor(a, a, gq8 if s < 4 else cols("fox_k_g"), sq2(s), ALU.mult,
                                         ALU.mult).then_inc(b2["qk"], 1)
            job = plan["rwkv", "kk"]
            full(dve, job)
            dve.tensor_scalar(rw2("t"), psum[:, job.bank, :], 1e-24, None, ALU.max)\
                .then_inc(bank_free[job.bank], 1)
            dve.wait_ge(b2["lnd"], 1)
            dve.tensor_tensor(lru[0], lru[0], u, ALU.subtract).then_inc(b2["sqrt_b"], 1)
            dve.wait_ge(b2["exp_a"], 1)
            dve.tensor_tensor(lru[2], lru[2], lru[0], ALU.mult)
            dve.drain()
            for b in range(2):
                dve.tensor_tensor_scan(lru[0][:, b], u[:, b], lru[2][:, b], 0.0, ALU.mult, ALU.add)
            dve.drain()
            dve.scalar_tensor_tensor(lru[1], ga, 0.5, lru[0], ALU.mult, ALU.mult)
            dve.drain()
            dve.tensor_tensor(lru[2], lru[1], lru[1], ALU.mult).then_inc(b2["y_sq"], 1)
            dve.wait_ge(b2["kk_rstd"], 1)
            dve.tensor_tensor(rw["kk"], rw["kk"], rw["t"], ALU.mult)
            for b in range(2):
                dve.scalar_tensor_tensor(R[:, b], pm[:, b], cols("r_k", b), Km[:, b], ALU.mult, ALU.mult)
            dve.drain()
            dve.tensor_copy(rw["t"], R).then_inc(b2["bonus_in"], 1)
            dve.wait_ge(b2["expW"], 3)
            dve.tensor_tensor(Bm, rw["kk"], rw["a"], ALU.mult)
            dve.tensor_tensor(A, rw["kk"], rw["ld"], ALU.mult)
            dve.tensor_tensor(Km, Km, rw["Wi"], ALU.mult)
            dve.drain()
            dve.tensor_tensor(Bm, Bm, rw["Wi"], ALU.mult)
            dve.tensor_tensor(R, pm[:, 0:2], rw["W"], ALU.mult).then_inc(b2["BK"], 1)
            for m in (inv_x, inv_xt):
                dve.tensor_copy(m, ident.unsqueeze(1).to_broadcast([P, 8, P])).then_inc(b2["inv0"], 1)
            attention("fox", FOX_ITEMS, lambda it: 1.0, probs_t2, o_tok2)
            job = plan["rwkv", "bonus"]
            full(dve, job)
            dve.tensor_tensor(flat(pm[:, 2:4]), psum[:, job.bank, :], flat(pm[:, 4:6]), ALU.mult)\
                .then_inc(bank_free[job.bank], 1)
            dve.wait_ge(b2["y_rstd"], 1)
            for b in range(2):
                dve.scalar_tensor_tensor(y_t[:, b], lru[1][:, b], cols("lru_norm_g", b), lru[0][:, 0],
                                         ALU.mult, ALU.mult)
            for name, to in (("Btok", Btok), ("Ktok", Ktok), ("Vtok", Vtok)):
                job = plan["rwkv", name]
                full(dve, job)
                dve.tensor_copy(flat(to), psum[:, job.bank, :]).then_inc(bank_free[job.bank], 1)
            for name, to in (("BR", BR), ("KR", KR)):
                for m in range(4):
                    job = plan["rwkv", name, m]
                    full(dve, job)
                    at = 4 * (m // 2) + m % 2
                    dve.tensor_tensor(to[:, at:at + 3:2], psum[:, job.bank, :].rearrange("p (a b) -> p a b", b=S),
                                      k2("strict_incl").unsqueeze(1).to_broadcast([P, 2, S]),
                                      ALU.mult).then_inc(bank_free[job.bank], 1)
            job = plan["rwkv", "MV"]
            full(dve, job)
            dve.tensor_copy(flat(MV), psum[:, job.bank, :]).then_inc(bank_free[job.bank], 1)
            for j in range(6):
                for what, to in (("X", inv_x), ("XT", inv_xt)):
                    if what == "X" and j == 5:
                        continue
                    for half in range(2):
                        job, v = plan["rwkv", what, j, half], flat(to[:, 4 * half:4 * half + 4])
                        full(dve, job)
                        dve.drain()
                        dve.tensor_tensor(v, v, psum[:, job.bank, :], ALU.subtract)\
                            .then_inc(bank_free[job.bank], 1)
            for cc in range(4):
                t, r = cc // 2, slice(64 * (cc % 2), 64 * (cc % 2) + 64)
                mv = flat(MV[r, 4 * t:4 * t + 4])
                if cc:
                    for odd in range(2):
                        job = plan["rwkv", "U", cc, odd]
                        full(dve, job)
                        of_heads = lambda v: v.rearrange("p (b o v) -> p b o v", o=2, v=64)[:, :, odd]
                        dve.tensor_tensor(of_heads(U_sb[r, 0]), of_heads(psum[r, job.bank, 0:S]),
                                          of_heads(mv), ALU.add).then_inc(bank_free[job.bank], 1)
                    dve.drain()
                    dve.nop().then_inc(b2["U"], 1)
                else:
                    dve.tensor_copy(U_sb[r, 0], mv).then_inc(b2["U"], 1)
                job = plan["rwkv", "SA", cc]
                full(dve, job)
                dve.tensor_scalar(SA_sb[r, 0], psum[r, job.bank, 0:S], -1.0, None, ALU.mult)\
                    .then_inc(bank_free[job.bank], 1)
                if cc < 3:
                    job, new, old = plan["rwkv", "ST", cc], state[(cc + 1) % 2], state[cc % 2]
                    ps = psum[:, job.bank, 0:P].rearrange("p (b v) -> p b v", v=64)
                    full(dve, job)
                    end = rw["W"][:, :, cc * 64 + 63:cc * 64 + 64].to_broadcast([P, 2, 64])
                    if cc:
                        dve.tensor_tensor(new, ps, old, ALU.add).then_inc(bank_free[job.bank], 1)
                    else:
                        dve.tensor_copy(new, ps).then_inc(bank_free[job.bank], 1)
                    dve.drain()
                    dve.tensor_tensor(new, new, end, ALU.mult).then_inc(b2["ST"], 1)
            o, t = rw2("cl"), rw2("t")
            of_chunks = lambda v, odd: v.rearrange("p (a o t) -> p a o t", o=2, t=64)[:, :, odd]
            for odd in range(2):
                job = plan["rwkv", "O", odd]
                full(dve, job)
                dve.tensor_copy(of_chunks(o, odd), of_chunks(psum[:, job.bank, :], odd))\
                    .then_inc(bank_free[job.bank], 1)
            dve.drain()
            for odd in range(2):
                job, r = plan["rwkv", "O", 2 + odd], slice(64 * odd, 64 * odd + 64)
                full(dve, job)
                later = rw["cl"][r, :, CHUNK:]
                dve.tensor_tensor(later, later, psum[r, job.bank, :].rearrange("p (b t) -> p b t", t=S)[:, :, CHUNK:],
                                  ALU.add).then_inc(bank_free[job.bank], 1)
            dve.drain()
            dve.nop().then_inc(b2["o_sb"], 1)
            job = plan["rwkv", "mean"]
            full(dve, job)
            dve.scalar_tensor_tensor(o, psum[:, job.bank, :], -1.0 / 64, o, ALU.mult, ALU.add)\
                .then_inc(bank_free[job.bank], 1)
            dve.drain()
            dve.tensor_tensor(t, o, o, ALU.mult).then_inc(b2["o_sq"], 1)
            dve.wait_ge(b2["o_rstd"], 1)
            dve.tensor_tensor(o, o, rw2("ld"), ALU.mult)
            dve.drain()
            for b in range(2):
                dve.tensor_scalar(rw["cl"][:, b], rw["cl"][:, b], cols("ln_g", b), cols("ln_b", b),
                                  ALU.mult, ALU.add)
            dve.drain()
            dve.tensor_tensor(rw["cl"], rw["cl"], pm[:, 2:4], ALU.add)
            dve.drain()
            dve.tensor_tensor(y_t[:, 6:8], rw["cl"], rw["g"], ALU.mult).then_inc(b2["y_done"], 1)
            for half in range(2):
                for t in range(2):
                    job, hs = plan["out2", half, t], slice(half * 512, half * 512 + 512)
                    full(dve, job)
                    dve.tensor_tensor(resid[:, t, hs], resid[:, t, hs], psum[:, job.bank, :], ALU.add)\
                        .then_inc(bank_free[job.bank], 1)
            dve.drain()
            dve.nop().then_inc(resid_ready, 1)
            rms_tokens()
            gained("h4", "norm2_g")
            m0 = step_of(T_MOE)
            split.until(m0 + 2, m0)
            job = plan["route",]
            full(dve, job)
            lg = rcol(0, 2, 20)
            dve.tensor_tensor(lg, psum[:, job.bank, 0:64].rearrange("p (t e) -> p t e", e=32)[:, :, 0:20],
                              k2("b_route").unsqueeze(1).to_broadcast([P, 2, 20]), ALU.add)\
                .then_inc(bank_free[job.bank], 1)
            dve.drain()
            rev = k2("rev").unsqueeze(1).to_broadcast([P, 2, 4])
            at = [48]
            def new(*dims):
                v = rcol(at[0], *dims)
                at[0] += int(np.prod(dims))
                return v
            def bc(v, n=4):
                return v.unsqueeze(2).to_broadcast([P, 2, n])
            def first_max(v, top):
                eq, best, hot = new(2, 4), new(2), new(2, 4)
                dve.reduce_max(top, v, AX.X)
                dve.drain()
                dve.tensor_tensor(eq, v, bc(top), ALU.is_equal)
                dve.drain()
                dve.tensor_tensor(eq, eq, rev, ALU.mult)
                dve.drain()
                dve.reduce_max(best, eq, AX.X)
                dve.drain()
                dve.tensor_tensor(hot, rev, bc(best), ALU.is_equal)
                dve.drain()
                return hot
            split.until(m0 + 4, m0)
            g_top, g_sh, g_exp, g_sum, g_p = new(2), new(2, 4), new(2, 4), new(2), new(2)
            e_top, e_top2, e_diff, e_exp, e_den = new(2), new(2), new(2), new(2), new(2)
            group = first_max(lg[:, :, 0:4], g_top)
            dve.tensor_tensor(g_sh, lg[:, :, 0:4], bc(g_top), ALU.subtract).then_inc(b2["route_shift"], 1)
            split.until(m0 + 5, m0)
            prod, el = new(2, 16), new(2, 4)
            sel16 = [group[:, t].unsqueeze(2).to_broadcast([P, 4, 4]) for t in range(2)]
            for t in range(2):
                dve.tensor_tensor(prod[:, t].rearrange("p (g e) -> p g e", e=4),
                                  lg[:, t, 4:20].rearrange("p (g e) -> p g e", e=4), sel16[t], ALU.mult)
            dve.drain()
            dve.tensor_reduce(el, prod.rearrange("p t (g e) -> p t e g", e=4), AX.X, ALU.add)
            dve.drain()
            split.until(m0 + 6, m0)
            hot1 = first_max(el, e_top)
            rest = new(2, 4)
            dve.scalar_tensor_tensor(rest, hot1, -3.0e38, el, ALU.mult, ALU.add)
            dve.drain()
            hot2 = first_max(rest, e_top2)
            dve.tensor_tensor(e_diff, e_top2, e_top, ALU.subtract).then_inc(b2["route2_shift"], 1)
            split.until(m0 + 8, m0)
            dve.wait_ge(b2["route_exp"], 1)
            dve.tensor_reduce(g_sum, g_exp, AX.X, ALU.add)
            dve.wait_ge(b2["route2_exp"], 1)
            dve.tensor_scalar(e_den, e_exp, 1.0, None, ALU.add)
            dve.drain()
            dve.tensor_tensor(e_den, e_den, g_sum, ALU.mult)
            dve.drain()
            dve.reciprocal(g_p, e_den)
            dve.drain()
            dve.tensor_tensor(e_exp, e_exp, g_p, ALU.mult)
            dve.tensor_tensor(hot1, hot1, bc(g_p), ALU.mult)
            dve.drain()
            dve.tensor_tensor(hot2, hot2, bc(e_exp), ALU.mult)
            dve.drain()
            dve.tensor_tensor(hot1, hot1, hot2, ALU.add)
            dve.drain()
            for t in range(2):
                ins = dve.tensor_tensor(comb16[:, t].rearrange("p (g e) -> p g e", e=4), sel16[t],
                                        hot1[:, t].unsqueeze(1).to_broadcast([P, 4, 4]), ALU.mult)
            ins.then_inc(b2["comb"], 1)
            assert at[0] <= 448
            job = plan["combT",]
            full(dve, job)
            dve.tensor_copy(combT[0:N_EXPERTS, :], psum[0:N_EXPERTS, job.bank, 0:S])\
                .then_inc(bank_free[job.bank], 1)
            for e in range(8):
                freed(dve, plan["comb", e])
            def expert(e, steps, weight, i=0, per=0, experts=0, jobs=0):
                g, up, p = plan["gate2", e], plan["up2", e], e % 2
                steps(4)
                dve.wait_ge(b2["sig"], experts * i + (e + 1))
                dve.tensor_tensor(h_t1[:, p], sig2[:, p], psum[:, g.bank, :], ALU.mult)\
                    .then_inc(bank_free[g.bank], 1)
                steps(8)
                dve.drain()
                dve.wait_ge(bank_full[up.bank], jobs * i + (up.turn + 1))
                dve.tensor_tensor(h_t1[:, p], h_t1[:, p], psum[:, up.bank, :], ALU.mult)\
                    .then_inc(bank_free[up.bank], 1)
                dve.drain()
                dve.tensor_tensor(hid[:, p].rearrange("p (b t) -> p b t", t=S),
                                  h_t1[:, p].rearrange("p (b t) -> p b t", t=S),
                                  weight.unsqueeze(1).to_broadcast([P, 2, S]), ALU.mult)\
                    .then_inc(b2["hid_exact"], 1)
                dve.drain()
                dve.wait_ge(b2["hid_high"], experts * i + (e + 1))
                dve.tensor_tensor(hid_lo[:, p], hid[:, p], hid_hi[:, p].bitcast(F32), ALU.subtract)\
                    .then_inc(b2["hid"], 1)
            moe_experts(dve, split, low_part, expert, lambda at: big[:, bass.ds(at, S)])
            full(dve, plan["moe", 1, 1])
            for t in range(2):
                dve.tensor_copy(out_sb[:, t, 0:512], psum[:, plan["moe", 0, t].bank, :])\
                    .then_inc(b2["out"], 1)
        @block.scalar
        def _(act):
            count = {"post": 0, "pre": 0, "items": 0, "feat": 0}
            def high_part(s, i=0, per=0):
                m, q = tile_of(s)
                act.wait_ge(tile_loaded[m % RING], (per // 16) * 16 * i + 16 * (m // RING + 1))
                if s >= SPLIT_BUFFERS:
                    act.wait_ge(split_started, per * i + (s - SPLIT_BUFFERS + 2))
                act.activation(w_hi[:, s % SPLIT_BUFFERS], ring(m % RING)[:, q * 512:q * 512 + 512], ACT.Copy)\
                    .then_inc(split_high, 1)
            split = Split(high_part)
            act.preload_act_table_set(EXP_LN)
            act.wait_ge(consts_in, 32)
            act.activation(stat[:, 0:16], col[:, COL["c"][0]:COL["c"][0] + 16], ACT.Exp, bias=cols("zero"),
                           scale=-1.0).then_inc(silu_exp, 1)
            def rstd(to, of, eps, scale=1.0):
                act.activation(to, of, ACT.Ln, bias=eps, scale=scale)
                act.drain()
                return act.activation(to, to, ACT.Exp, bias=cols("zero"), scale=-0.5)
            def token_rstd(tiles, ready, done, which):
                for t in range(tiles):
                    act.wait_ge(ready, count[which] + t + 1)
                    rstd(stat[:, 56 + t:57 + t], stat[:, 49 + 2 * t:50 + 2 * t], cols("eps")).then_inc(done, 1)
                count[which] += tiles
            def high_features(width):
                for k in range(KT):
                    act.wait_ge(feat_exact, count["feat"] + k + 1)
                    act.activation(feat_hi[:, k, 0:width], exact[k % 2][:, 0:width], ACT.Copy)\
                        .then_inc(feat_high, 1)
                count["feat"] += KT
            def evacuate(job, to, n):
                full(act, job)
                act.activation(to, psum[:, job.bank, 0:n], ACT.Copy).then_inc(bank_free[job.bank], 1)
            def attention(tag, items, scale, probs, probs_t, o_tok, to):
                n, base = len(items), count["items"]
                for i in range(n + 5):
                    if i < n:
                        job, keys = plan[tag, "S", i], items[i][4]
                        act.wait_ge(neg_max, base + i + 1)
                        act.activation(probs[:, i % 3, 0:keys], psum[:, job.bank, 0:keys], ACT.Exp,
                                       bias=stat[:, 64 + i:65 + i], scale=scale(items[i]),
                                       accum_out=stat[:, 128 + i:129 + i]).then_inc(bank_free[job.bank], 1)
                    if tag != "fox" and 1 <= i <= n:
                        keys, p = items[i - 1][4], (i - 1) % 3
                        act.wait_ge(sum_inverse, first_item(tag) + i)
                        act.activation(probs[:, p, 0:keys], probs[:, p, 0:keys], ACT.Copy,
                                       scale=stat[:, 192 + (i - 1) % 8:193 + (i - 1) % 8]).then_inc(probs_ready, 1)
                    if 2 <= i < n + 2 and not copied_by_dve(tag, i - 2):
                        job = plan[tag, "T", i - 2]
                        evacuate(job, probs_t[:, i % 2, 0:items[i - 2][4]], items[i - 2][4])
                    if tag == "fox" and i >= HEADS + 2 and (i - HEADS - 2) % HEADS == 0:
                        t = (i - HEADS - 2) // HEADS
                        freed(act, plan[tag, "O", t])
                        act.activation(f2[:, 0:2], o_tok[:, t % 2].rearrange("p (a b) -> p a b", b=S), ACT.Square,
                                       accum_out=stat[:, 212 + t:213 + t])
                        act.drain()
                        rstd(stat[:, 212 + t:213 + t], stat[:, 212 + t:213 + t], cols("eps"), 1.0 / 512)\
                            .then_inc(b2["fox_rstd"], 1)
                    late = 4 if tag == "fox" else 2
                    if i >= HEADS + late and (i - HEADS - late) % HEADS == 0:
                        t = (i - HEADS - late) // HEADS
                        job = plan[tag, "OT" if tag == "fox" else "O", t]
                        full(act, job)
                        to(t, items[HEADS * t], job)
                count["items"] += n
            next_rows = 0
            for l in range(DEPTH):
                L, n = l * LAYER_TILES, tiles_of(l)
                s_in, s_gate, s_up = (step_of(L + x) for x in (T_IN, T_GATE, T_W1))
                T = n * P
                def ada(i=0, first=0):
                    for chunk in range(2):
                        rows = plan[l, "ada rows", chunk]
                        act.wait_ge(bank_full[rows.bank], i + (rows.turn + 1 + first))
                        act.activation(ada_rows[0:2, chunk], psum[0:2, rows.bank, :], ACT.Copy)\
                            .then_inc(bank_free[rows.bank], 1)
                ada()
                token_rstd(4, stats_ready, rstd_ready, "pre")
                ada(0, 1)
                split.until(s_in + AHEAD, s_in)
                high_features(4 * P)
                def ahead(name):
                    split.until(s_in + 2 * IN_NAMES.index(name) + 2 + AHEAD, s_in)
                def squares(name, to, of, signal=True):
                    ahead(name)
                    freed(act, plan[l, name])
                    ins = act.activation(to, of, ACT.Square)
                    if signal:
                        ins.then_inc(squares_ready, 1)
                squares("ckv0", tmp[:, 0], ckv[:, 0], False)
                squares("ckv1", tmp[:, 1], ckv[:, 1])
                ahead("vg")
                evacuate(plan[l, "vg"], vg.rearrange("p a b -> p (a b)"), 512)
                for g in range(4):
                    ahead(f"f{g}")
                    evacuate(plan[l, f"f{g}"], f_in[:, g, 0:T], T)
                squares("cq0", tmp[:, 2, 0:T], cq[:, 0, 0:T], False)
                squares("cq1", tmp[:, 3, 0:T], cq[:, 1, 0:T])
                squares("kg", probs_sq(0), kg)
                for b in range(4):
                    squares(f"qg{b}", probs_sq(1 + b)[:, 0:T], qg[:, b, 0:T])
                for name, rows, w, k in ([("ckv", tmp[:, 0], 512, 256), ("cq", tmp[:, 2], T, 256),
                                          ("kg", probs_sq(0), 512, 64)]
                                         + [(f"qg{b}", probs_sq(1 + b), T, 64) for b in range(4)]):
                    job = plan[l, "ss", name]
                    split.until(s_gate + 1, s_in)
                    full(act, job)
                    act.activation(rows[:, 0:w], psum[:, job.bank, 0:w], ACT.Ln, bias=cols("eps"),
                                   scale=1.0 / k).then_inc(bank_free[job.bank], 1)
                    act.drain()
                    act.activation(rows[:, 0:w], rows[:, 0:w], ACT.Exp, bias=cols("zero"), scale=-0.5)\
                        .then_inc(rstd_rows_ready, 1)
                at = COL[f"b_gate{l}"][0]
                act.preload_act_table_set(SIGMOID)
                split.until(s_gate + AHEAD, s_in)
                def gate(b, i=0):
                    job = plan[l, "gate", b]
                    act.wait_ge(bank_full[job.bank], i + (job.turn + 1))
                    act.activation(big[:, bass.ds(4096 * i + 512 * b, T)], psum[:, job.bank, 0:T], ACT.Sigmoid,
                                   bias=col[:, bass.ds(8 * i + (at + b), 1)]).then_inc(bank_free[job.bank], 1)
                with act.Fori(0, GATE_BLOCKS // BANKS - 1) as i:
                    for b in range(BANKS):
                        high_part(s_gate + 2 * b + AHEAD, i, 16)
                        high_part(s_gate + 2 * b + 1 + AHEAD, i, 16)
                        gate(b, i)
                split.next = s_gate + 2 * (GATE_BLOCKS - BANKS) + AHEAD
                for b in range(GATE_BLOCKS - BANKS, GATE_BLOCKS):
                    split.until(s_gate + 2 * b + 2 + AHEAD, s_in)
                    gate(b)
                if l:
                    act.wait_ge(rows_used, next_rows)
                act.dma_start(rows_t[:, :], ln_rows[next_rows].partition_broadcast(P)).then_inc(rows_in, 16)
                next_rows += 1
                act.preload_act_table_set(EXP_LN)
                for b in range(4):
                    evacuate(plan[l, "kn", b], kn[:, b], 512)
                for b in range(4):
                    evacuate(plan[l, "qn", b], qn[:, b, 0:T], T)
                for b in range(2):
                    evacuate(plan[l, "qr", b], qr[:, b, 0:T], T)
                for s in range(n // 2):
                    for g in range(4):
                        evacuate(plan[l, "dft1", s, g], dft_mid[:, g], 512)
                def to_features(t, item, job):
                    to = out_m if item[0] == "m" else out_g
                    q = item[1]
                    act.activation(to[:, 0:4, q * P:q * P + P],
                                   psum[:, job.bank, :].rearrange("p (b t) -> p b t", t=P), ACT.Copy)\
                        .then_inc(bank_free[job.bank], 1)
                attention((l, "att"), attention_items(l), lambda it: SCALE_M if it[0] == "m" else SCALE_G,
                          probs, probs_t, o_tok, to_features)
                for v in range(n // 2):
                    for half in range(2):
                        evacuate(plan[l, "g", 2, v, half], gain_rows[:, v, half * 512:half * 512 + 512], 512)
                if l == DEPTH - 1:
                    act.dma_start(c2, const2).then_inc(const2_in, 16)
                split.until(s_up + AHEAD, s_up)
                token_rstd(n, post_stats, post_rstd, "post")
                token_rstd(n, stats_ready, rstd_ready, "pre")
                high_features(T)
                act.wait_ge(rows_used, next_rows)
                act.dma_start(rows_t[:, :], ln_rows[next_rows].partition_broadcast(P)).then_inc(rows_in, 16)
                next_rows += 1
                for v in range(n // 2):
                    for half in range(2):
                        evacuate(plan[l, "g", 5, v, half], gain_rows[:, v, half * 512:half * 512 + 512], 512)
                for part in range(2):
                    s = s_up + 4 * 2 * FF_TILES * part
                    with act.Fori(0, FF_PART // BANKS) as i:
                        for b in range(BANKS):
                            job = plan[l, "ff", part * FF_PART + b]
                            high_part(s + 2 * b + AHEAD, i, 16)
                            high_part(s + 2 * b + 1 + AHEAD, i, 16)
                            done = NFF * l + FF_PART * part + b + 1
                            act.wait_ge(bank_full[job.bank], i + (job.turn + 1))
                            act.wait_ge(relu_free, 8 * i + done)
                            act.activation(relu[b % 2][:, 0:T], psum[:, job.bank, 0:T], ACT.Relu)\
                                .then_inc(bank_free[job.bank], 1)
                            act.wait_ge(bank_free[job.bank], i + (job.turn + 1))
                            act.activation(big_r[:, bass.ds(4096 * i + 512 * b, T)], relu[b % 2][:, 0:T],
                                           ACT.Square).then_inc(hidden_high, 1)
                    split.next = s + 2 * FF_PART + AHEAD
                    split.until(s + 4 * FF_PART + AHEAD, s)
                token_rstd(n, post_stats, post_rstd, "post")
            def rms(wait, scratch):
                act.wait_ge(resid_ready, wait)
                for t in range(2):
                    act.drain()
                    act.activation(scratch, resid[:, t], ACT.Square, accum_out=stat[:, 60 + t:61 + t])
                    act.drain()
                    rstd(stat[:, 56 + t:57 + t], stat[:, 60 + t:61 + t], cols("eps"), 1.0 / D)\
                        .then_inc(rstd_ready, 1)
            scratch = view(work, 21 * 512, D)
            s_in = step_of(T_IN2)
            rms(1, view(work, 5 * 512, D))
            high_features(S)
            for b in range(1, 20, 2):
                split.until(s_in + 2 * b + 2 + AHEAD, s_in)
                evacuate(plan["b2", IN2_NAMES[b]], f2[:, b], S)
            split.until(s_in + 48, s_in)
            for b in range(0, 20, 2):
                freed(act, plan["b2", IN2_NAMES[b]])
            for t in range(2):
                freed(act, plan["b2", "v", t])
            act.drain()
            for s in range(8):
                act.activation(sq2(s), f2[:, 4 + s], ACT.Square).then_inc(b2["sq_in"], 1)
            H = slice(0, HEADS)
            act.activation(stat[:, 220:222], cols("lru_lambda", 0, 2), ACT.Exp, bias=cols("zero"), scale=-1.0)
            act.activation(probs2[H, 0], f2[H, 19], ACT.Abs, bias=cols("fox_fb")[H])
            act.drain()
            act.activation(stat[:, 220:222], stat[:, 220:222], ACT.Ln, bias=cols("one")).then_inc(b2["spl"], 1)
            act.activation(probs2[H, 1], probs2[H, 0], ACT.Exp, bias=cols("zero")[H], scale=-1.0)
            act.wait_ge(b2["gelu_arg"], 1)
            act.wait_ge(b2["z"], 1)
            act.drain()
            act.activation(f2[H, 19], probs2[H, 1], ACT.Ln, bias=cols("one")[H]).then_inc(b2["log_f"], 1)
            act.wait_ge(b2["mixed"], 1)
            act.preload_act_table_set(SIGMOID)
            act.activation(pm[0:32, 6], pm[0:32, 6], ACT.Tanh).then_inc(b2["lora"], 1)
            act.activation(pm[64:128, 6], pm[64:128, 6], ACT.Sigmoid).then_inc(b2["lora"], 1)
            def blocks(job, to, func, bias):
                full(act, job)
                for b in range(2):
                    ins = act.activation(to[:, b], psum[:, job.bank, b * S:b * S + S], func, bias=cols(bias, b))
                ins.then_inc(bank_free[job.bank], 1)
            blocks(plan["lru", "r"], lru[1], ACT.Sigmoid, "lru_ba")
            blocks(plan["lru", "i"], lru[2], ACT.Sigmoid, "lru_bx")
            blocks(plan["rwkv", "w"], rw["ld"], ACT.Sigmoid, "w0")
            blocks(plan["rwkv", "a"], rw["a"], ACT.Sigmoid, "a0")
            evacuate(plan["rwkv", "g"], rw2("g"), 512)
            act.activation(rw["Wi"], rw["Wi"], ACT.Tanh, scale=float(np.sqrt(2 / np.pi))).then_inc(b2["gelu"], 1)
            act.wait_ge(b2["log_a"], 1)
            u = f2[:, 0:2]
            act.activation(u, lru[1], ACT.Tanh, scale=-1.0).then_inc(b2["tanh_a"], 1)
            act.preload_act_table_set(EXP_LN)
            for s in range(8):
                job = plan["ss", ("q%d" % s) if s < 4 else "k%d" % (s - 4)]
                full(act, job)
                act.activation(sq2(s), psum[:, job.bank, 0:S], ACT.Ln, bias=cols("eps"), scale=1.0 / 64)\
                    .then_inc(bank_free[job.bank], 1)
                act.drain()
                act.activation(sq2(s), sq2(s), ACT.Exp, bias=cols("zero"), scale=-0.5).then_inc(b2["rsq"], 1)
            act.wait_ge(b2["sqrt_b"], 1)
            act.wait_ge(b2["lru_b"], 1)
            act.activation(lru[0], u, ACT.Ln, bias=cols("zero"), scale=2.0)
            act.activation(u, u, ACT.Ln, bias=cols("one")).then_inc(b2["lnd"], 1)
            act.wait_ge(b2["sqrt_b"], 2)
            act.drain()
            act.activation(lru[0], lru[0], ACT.Exp, bias=cols("zero"), scale=0.5)
            act.activation(u, lru[1], ACT.Exp, bias=cols("zero")).then_inc(b2["exp_a"], 1)
            freed(act, plan["rwkv", "kk"])
            act.activation(rw["t"], rw["t"], ACT.Ln, bias=cols("zero"))
            act.drain()
            act.activation(rw["t"], rw["t"], ACT.Exp, bias=cols("zero"), scale=-0.5).then_inc(b2["kk_rstd"], 1)
            act.wait_ge(b2["cl"], 1)
            act.activation(rw["W"], rw["cl"], ACT.Exp, bias=cols("zero")).then_inc(b2["expW"], 1)
            act.activation(rw["Wi"], rw["cl"], ACT.Exp, bias=cols("zero"), scale=-1.0).then_inc(b2["expW"], 1)
            act.activation(rw["ld"], rw["ld"], ACT.Exp, bias=cols("zero")).then_inc(b2["expW"], 1)
            def fox_features(t, item, job):
                for b in range(4):
                    ins = act.activation(y_t[:, 2 + b, t * P:t * P + P], psum[:, job.bank, b * P:b * P + P],
                                         ACT.Copy, scale=cols("fox_norm_g", b))
                ins.then_inc(bank_free[job.bank], 1)
            attention("fox", FOX_ITEMS, lambda it: 1.0, probs2, probs_t2, o_tok2, fox_features)
            job = plan["lru", "ss"]
            full(act, job)
            act.activation(lru[0][:, 0], psum[:, job.bank, 0:S], ACT.Ln, bias=cols("eps"), scale=1.0 / S)\
                .then_inc(bank_free[job.bank], 1)
            act.drain()
            act.activation(lru[0][:, 0], lru[0][:, 0], ACT.Exp, bias=cols("zero"), scale=-0.5)\
                .then_inc(b2["y_rstd"], 1)
            for j in range(6):
                for half in range(2):
                    evacuate(plan["rwkv", "T1", j, half], flat(inv_t1[:, 4 * half:4 * half + 4]), 512)
            job = plan["rwkv", "var"]
            full(act, job)
            act.activation(rw2("ld"), psum[:, job.bank, :], ACT.Ln, bias=cols("gn_eps"), scale=1.0 / 64)\
                .then_inc(bank_free[job.bank], 1)
            act.drain()
            act.activation(rw2("ld"), rw2("ld"), ACT.Exp, bias=cols("zero"), scale=-0.5).then_inc(b2["o_rstd"], 1)
            rms(2, scratch)
            high_features(S)
            r = lambda at, *dims: rcol(at, *dims)
            m0 = step_of(T_MOE)
            split.until(m0 + 5, m0)
            act.wait_ge(b2["route_shift"], 1)
            act.activation(r(58, 8), r(50, 8), ACT.Exp, bias=cols("zero")).then_inc(b2["route_exp"], 1)
            split.until(m0 + 8, m0)
            act.wait_ge(b2["route2_shift"], 1)
            act.activation(r(76, 2), r(74, 2), ACT.Exp, bias=cols("zero")).then_inc(b2["route2_exp"], 1)
            for e in range(8):
                evacuate(plan["comb", e], flat(comb_b[:, 2 * e:2 * e + 2]), 512)
            act.preload_act_table_set(SIGMOID)
            def expert(e, steps, weight, i=0, per=0, experts=0, jobs=0):
                job, p = plan["gate2", e], e % 2
                steps(4)
                act.wait_ge(bank_full[job.bank], jobs * i + (job.turn + 1))
                act.activation(sig2[:, p], psum[:, job.bank, :], ACT.Sigmoid).then_inc(b2["sig"], 1)
                steps(8)
                act.wait_ge(b2["hid_exact"], experts * i + (e + 1))
                act.activation(hid_hi[:, p], hid[:, p], ACT.Copy).then_inc(b2["hid_high"], 1)
            moe_experts(act, split, high_part, expert, lambda at: None)
            full(act, plan["moe", 1, 1])
            for t in range(2):
                act.activation(out_sb[:, t, 512:1024], psum[:, plan["moe", 1, t].bank, :], ACT.Copy)\
                    .then_inc(b2["out"], 1)
            act.wait_ge(b2["out"], 4)
            act.dma_start(out.rearrange("a (t p) d -> p (a t) d", p=P), out_sb).then_inc(out_stored, 16)
            act.wait_ge(out_stored, 16)
        @block.gpsimd
        def _(pool):
            for l in range(DEPTH):
                T = tiles_of(l) * P
                for b in range(KT):
                    for r in range(3):
                        freed(pool, plan[l, "branch", b, r])
                    g = [gates[:, r * KT + b, 0:T] for r in range(3)]
                    pool.tensor_tensor(g[0], g[0], g[1], ALU.add).then_inc(gated, 1)
                    pool.wait_ge(gated, KT * l + b + 1)
                    pool.tensor_tensor(feat[:, b, 0:T], g[0], g[2], ALU.add).then_inc(mix_ready, 1)
            pool.wait_ge(const2_in, 16)
            for m in range(4):
                freed(pool, plan["rwkv", "BR", m])
            for j in range(6):
                if j >= 2:
                    full(pool, plan["rwkv", "T1", j - 2, 1])
                pool.tensor_tensor(level_l[j % 2], BR[:, :, 0:P],
                                   k2("levels")[:, j * P:j * P + P].unsqueeze(1).to_broadcast([P, 8, P]),
                                   ALU.mult).then_inc(b2["lev"], 1)


def blocks_of(w, names_cols):
    out = np.zeros((len(names_cols), P, w.shape[0] // P, P), w.dtype)
    for i, idx in enumerate(names_cols):
        if len(idx):
            out[i, :, :, :len(idx)] = w[:, idx].reshape(-1, P, len(idx)).transpose(1, 0, 2)
    return out


def pairs(blocks):
    n = blocks.shape[0]
    if n % 2:
        blocks = np.concatenate([blocks, np.zeros_like(blocks[:1])])
    return blocks.reshape(-1, 2, P, D).transpose(0, 2, 1, 3).reshape(-1, P, TILE)


def halves(w):
    k = w.shape[0] // P
    return w.reshape(k // 4, 4, P, 2, 512).transpose(3, 0, 2, 1, 4).reshape(-1, P, TILE)


def padded(a):
    a = a.reshape(P, -1)
    return np.concatenate([a, np.zeros((P, TILE - a.shape[1]), a.dtype)], 1)[None]


def rows_first(w):
    return w.reshape(-1, P, w.shape[1]).transpose(1, 0, 2).reshape(P, -1)


def pack_stream(i):
    r = np.arange
    tiles = []
    for l in range(DEPTH):
        w = i["w_in"][l]
        ada = i["w_ada"][l].reshape(2, 4, P, ADA_CHUNKS, 512).transpose(3, 0, 2, 1, 4).reshape(-1, P, TILE)
        tiles.append(ada[:ADA_TILES])
        q0 = 544 + 512 + 256
        qg = [np.concatenate([q0 + r(b * 64, b * 64 + 64), q0 + r((b + 4) * 64, (b + 4) * 64 + 64)])
              for b in range(4)]
        tiles.append(pairs(blocks_of(w, [r(0, 128), r(128, 256), np.tile(r(256, 288), 4), r(288, 416),
                                         r(416, 544)] + [544 + r(b * P, b * P + P) for b in range(4)]
                                     + [1056 + r(b * P, b * P + P) for b in range(2)] + qg)))
        tiles.append(pairs(blocks_of(w, [1824 + r(b * P, b * P + P) for b in range(GATE_BLOCKS)])))
        tiles.append(np.concatenate([rows_first(i["w_uk"][l]), rows_first(i["w_uv"][l])], 1)[None])
        heads = i["w_uq"][l].reshape(256, HEADS, 96)
        uq = np.concatenate([heads[:, :, :64].reshape(256, 512), heads[:, :, 64:].reshape(256, 256)], 1)
        tiles.append(padded(rows_first(uq)))
        tiles.append(ada[ADA_TILES:])
        for b in range(KT):
            tiles.append(padded(np.concatenate([rows_first(i[n][l][:, b * P:b * P + P])
                                                for n in ("w_fo", "w_mo", "w_go")], 1)))
        tiles.append(halves(i["w_o"][l]))
        up = pairs(blocks_of(i["w1"][l], [r(b * P, b * P + P) for b in range(NFF)]))
        for part in range(2):
            tiles.append(up[part * FF_TILES:(part + 1) * FF_TILES])
            tiles.append(halves(i["w2"][l][part * FF_PART * P:(part + 1) * FF_PART * P]))
    w = i["w_in_2"][0]
    starts = [0, 128, 256, 384] + [512 + b * P for b in range(8)] + [2056 + b * P for b in range(7)]
    tiles.append(pairs(blocks_of(w, [r(s, s + P) for s in starts] + [r(2048, 2056)])))
    v = w[:, 1536:2048]
    tiles.append(v.reshape(2, 4, P, 512).transpose(0, 2, 1, 3).reshape(2, P, TILE))
    tiles.append(halves(i["w_out_2"][0]))
    gate, up = (i[name][0].reshape(N_EXPERTS, KT, P, 2, P).transpose(0, 2, 3, 1, 4).reshape(N_EXPERTS, P, TILE)
                for name in ("exp_w_gate_2", "exp_w_up_2"))
    down = i["exp_w_down_2"][0].reshape(N_EXPERTS, 2, P, D).transpose(0, 2, 1, 3).reshape(N_EXPERTS, P, TILE)
    tiles += [gate[0:1], up[0:1]]
    for e in range(N_EXPERTS):
        if e + 1 < N_EXPERTS:
            tiles += [gate[e + 1:e + 2], up[e + 1:e + 2]]
        tiles.append(down[e:e + 1])
    out = np.concatenate(tiles)
    assert out.shape == (N_TILES, P, TILE), out.shape
    return out


def pack_columns(i):
    out = np.zeros((P, N_COL), np.float32)
    def put(name, a):
        at, n = COL[name]
        a = np.asarray(a)
        out[:a.size // n if a.size < P * n else P, at:at + n] = a.reshape(n, -1).T
    put("c", i["c"][0])
    put("c_ctx", i["c_ctx"])
    for l in range(DEPTH):
        put(f"b_ada{l}", i["b_ada"][l])
        put(f"b_gate{l}", i["b_gate"][l])
        put(f"mla_q_g{l}", i["mla_q_g"][l])
        put(f"mla_kv_g{l}", i["mla_kv_g"][l])
        put(f"gqa_q_g{l}", np.tile(i["gqa_q_g"][l], 2))
        put(f"gqa_k_g{l}", np.tile(i["gqa_k_g"][l], 2))
    put("norm1_g", i["norm1_g_2"][0])
    put("conv_w", i["conv_w_2"][0].reshape(4, 2, P).transpose(1, 0, 2).reshape(-1))
    for name, of in (("conv_b", "conv_b_2"), ("lru_ba", "lru_ba_2"), ("lru_bx", "lru_bx_2"),
                     ("lru_lambda", "lru_lambda_2"), ("lru_norm_g", "lru_norm_g_2"),
                     ("fox_norm_g", "fox_norm_g_2"), ("fox_fb", "fox_fb_2"), ("mu", "rwkv_mu_2"),
                     ("w0", "rwkv_w0_2"), ("a0", "rwkv_a0_2"), ("k_k", "rwkv_kk_2"), ("k_a", "rwkv_ka_2"),
                     ("r_k", "rwkv_rk_2"), ("ln_g", "rwkv_ln_g_2"), ("ln_b", "rwkv_ln_b_2"),
                     ("norm2_g", "norm2_g_2")):
        put(name, i[of][0])
    put("fox_q_g", np.tile(i["fox_qnorm_g_2"][0], 2))
    put("fox_k_g", np.tile(i["fox_knorm_g_2"][0], 2))
    put("eps", np.full(P, EPS, np.float32))
    put("gn_eps", np.full(P, GN_EPS, np.float32))
    put("one", np.ones(P, np.float32))
    return out


def rope_tables(d):
    n = d // 4
    freqs = 10000.0 ** (-np.arange(n, dtype=np.float32) / n)
    t = np.arange(S)
    rows, cols = (t // 64).astype(np.float32), (t % 64).astype(np.float32)
    ang = np.concatenate([rows[:, None] * freqs, cols[:, None] * freqs], 1).astype(np.float32).T
    ang = np.tile(ang, (P // (d // 2), 1))
    return np.cos(ang), np.sin(ang)


def rotation(d):
    m = np.zeros((P, P), np.float32)
    for p in range(P):
        if p % d < d // 2:
            m[p + d // 2, p] = -1.0
        else:
            m[p - d // 2, p] = 1.0
    return m


def constants_1():
    i = np.arange(P)
    bones = (i[:, None] // 64 == i[None] // 64)
    t = np.arange(S)
    norm = (S * P) ** -0.5
    d = 2 * np.pi * np.outer(i, i) / P
    s = 2 * np.pi * np.outer(t, t) / S
    by_tile = lambda a: a.reshape(2, P, S).transpose(1, 0, 2).reshape(P, 512)
    c32, s32 = rope_tables(32)
    c64, s64 = rope_tables(64)
    parts = [np.eye(P), np.ones((P, P)), bones, np.concatenate([np.cos(d), np.sin(d)], 1) * norm,
             by_tile(np.cos(s)), -by_tile(np.sin(s)), rotation(32), rotation(64), c32, s32, c64, s64]
    out = np.concatenate([np.asarray(p, np.float32) for p in parts], 1)
    assert out.shape == (P, N_C1)
    return out


def constants_2(i):
    p = np.arange(P)
    s, t = p[:, None], p[None]
    causal = np.where(t <= s, 0.0, NEG)
    same = s // CHUNK == t // CHUNK
    levels = [(s >> (j + 1) == t >> (j + 1)) & ((s >> j) % 2 == 0) & ((t >> j) % 2 == 1) for j in range(6)]
    reset = np.tile((np.arange(S) % CHUNK != 0).astype(np.float32), (P, 1))
    def diagonal(w):
        out = np.zeros((P, 2, P), np.float32)
        for h in range(4):
            a = slice(64 * (h % 2), 64 * (h % 2) + 64)
            out[a, h // 2, a] = w[0, h]
        return out.reshape(P, 256)
    lora = np.concatenate([i["rwkv_w2_2"][0], i["rwkv_a2_2"][0], i["rwkv_g2_2"][0]], 0)
    route = np.concatenate([i["router_gw_2"][0], i["router_ew_2"][0]], 1)
    bias = np.tile(np.concatenate([i["router_gb_2"][0], i["router_eb_2"][0]]), (P, 1))
    parts = [causal, np.concatenate([same & (s < t), same & (s <= t)], 1), *levels, reset, lora,
             diagonal(i["lru_wa_2"]), diagonal(i["lru_wx_2"]), rows_first(route), bias,
             np.tile([4.0, 3.0, 2.0, 1.0], (P, 1)), np.zeros((P, 8))]
    out = np.concatenate([np.asarray(a, np.float32) for a in parts], 1)
    assert out.shape == (P, N_C2)
    return out


def kernel(**inputs):
    import concourse.bacc as bacc
    from concourse.bass_utils import run_bass_kernel_spmd as run
    i = {k: np.asarray(v) for k, v in inputs.items()}
    arrays = {
        "stream": pack_stream(i), "columns": pack_columns(i), "const1": constants_1(),
        "const2": constants_2(i), "x": np.ascontiguousarray(i["x"]), "ctx": np.ascontiguousarray(i["ctx"]),
        "ln_rows": np.stack([np.concatenate([i[f"ln{n}_g"][l], i[f"ln{n}_b"][l]])
                             for l in range(DEPTH) for n in (1, 2)]),
    }
    nc = bacc.Bacc("TRN2", target_bir_lowering=False, num_devices=1)
    aps = [nc.dram_tensor(name, a.shape, F32, kind="ExternalInput").ap() for name, a in arrays.items()]
    out = nc.dram_tensor("out", (1, S, D), F32, kind="ExternalOutput").ap()
    build(nc, *aps, out)
    r = run(nc, [arrays], core_ids=[0])
    return r.results[0]["out"]
```
